# Optimizing a Trainium2 kernel written in Bass

```python
import math
import jax, jax.numpy as jnp
from jax import lax
import numpy as np

D_MODEL = 1024
BATCH = 1
SEQ = 1024
DEPTH = 2
DEC_BATCH = 8
DEC_SEQ = 4
PAST_LEN = 1024
PAGE_SIZE = 128

N_A = max(1, DEPTH // 2)
N_B = DEPTH - N_A
A_KDIM = 128
A_HEADS = D_MODEL // A_KDIM
A_VDIM = D_MODEL // A_HEADS
A_HK = A_HEADS * A_KDIM
A_HV = A_HEADS * A_VDIM
HGRN_CHUNK = 64
SB_HEAD_DIM = 64
SB_HEADS = D_MODEL // SB_HEAD_DIM
SB_HD = SB_HEADS * SB_HEAD_DIM
SB_BLOCK = 128
SB_BIAS_INIT = -6.0
D_FF = ((8 * D_MODEL // 3 + 255) // 256) * 256
PLE_DIM = 256
EPS = 1e-6

kernel_name = "yoco_hgrn2_stickbreaking_step"

def rmsnorm(x, g):
    xf = x.astype(jnp.float32)
    y = xf * lax.rsqrt(jnp.mean(xf * xf, axis=-1, keepdims=True) + EPS)
    return y.astype(x.dtype) * g

def swiglu(xn, w_in, w_out):
    gu = xn @ w_in
    gate, up = gu[..., :D_FF], gu[..., D_FF:]
    return (jax.nn.silu(gate) * up) @ w_out

def ple_add(h, p, g, w_pe, w_pg):
    gate = jax.nn.sigmoid(rmsnorm(h, g) @ w_pg)
    return (p @ w_pe) * gate

def hgrn2_chunk_step(S, xs):
    q, k, lf, v = xs
    C = q.shape[1]
    G = jnp.cumsum(lf, axis=1)
    causal = jnp.tril(jnp.ones((C, C), dtype=bool))[None, :, :, None, None]
    diff = G[:, :, None] - G[:, None, :]
    dec = jnp.exp(jnp.where(causal, diff, -jnp.inf))
    att = jnp.einsum('bthk,bshk,btshk->bhts', q, k, dec)
    intra = jnp.einsum('bhts,bshv->bthv', att, v)
    inter = jnp.einsum('bthk,bhkv->bthv', q * jnp.exp(G), S)
    g_last = G[:, -1]
    k_dec = k * jnp.exp(g_last[:, None] - G)
    S_new = jnp.exp(g_last)[..., None] * S + jnp.einsum('bshk,bshv->bhkv', k_dec, v)
    return S_new, intra + inter

def hgrn2_mix(xn, S0, w_in, lb, g_onorm, w_o):
    B, L, _ = xn.shape
    proj = xn @ w_in
    q = proj[..., :A_HK]
    f = proj[..., A_HK:2 * A_HK]
    i = proj[..., 2 * A_HK:2 * A_HK + A_HV]
    og = proj[..., 2 * A_HK + A_HV:]
    q = jax.nn.silu(q.astype(jnp.float32)).reshape(B, L, A_HEADS, A_KDIM)
    fg = lb + (1.0 - lb) * jax.nn.sigmoid(f.astype(jnp.float32))
    lf = jnp.log(fg).reshape(B, L, A_HEADS, A_KDIM)
    kk = (1.0 - fg).reshape(B, L, A_HEADS, A_KDIM)
    v = i.astype(jnp.float32).reshape(B, L, A_HEADS, A_VDIM)
    C = HGRN_CHUNK if L % HGRN_CHUNK == 0 else L
    n = L // C

    def to_chunks(a):
        return a.reshape(B, n, C, A_HEADS, a.shape[-1]).transpose(1, 0, 2, 3, 4)

    S_fin, o = lax.scan(hgrn2_chunk_step, S0.astype(jnp.float32),
                        (to_chunks(q), to_chunks(kk), to_chunks(lf), to_chunks(v)))
    o = o.transpose(1, 0, 2, 3, 4).reshape(B, L, A_HEADS, A_VDIM)
    o = o * lax.rsqrt(jnp.mean(o * o, axis=-1, keepdims=True) + EPS)
    o = o * g_onorm.reshape(A_HEADS, A_VDIM).astype(jnp.float32)
    o = o.reshape(B, L, A_HV) * jax.nn.silu(og.astype(jnp.float32))
    return o.astype(xn.dtype) @ w_o, S_fin

def sb_block(q, k, v, bias, q_pos, k_pos):
    z = jnp.einsum('bqhd,bkhd->bhqk', q.astype(jnp.float32), k.astype(jnp.float32)) / math.sqrt(SB_HEAD_DIM)
    z = z + bias.astype(jnp.float32)[None, :, None, None]
    mask = (k_pos[None, :] < q_pos[:, None])[None, None]
    log_1mb = jnp.where(mask, jax.nn.log_sigmoid(-z), 0.0)
    tail = lax.cumsum(log_1mb, axis=3, reverse=True) - log_1mb
    log_a = jnp.where(mask, jax.nn.log_sigmoid(z) + tail, -jnp.inf)
    a = jnp.exp(log_a)
    o = jnp.einsum('bhqk,bkhd->bqhd', a, v.astype(jnp.float32))
    return o.astype(q.dtype)

def sb_attention(q, k, v, bias, q_pos, k_pos):
    B, Tq = q.shape[0], q.shape[1]
    if Tq % SB_BLOCK == 0 and Tq > SB_BLOCK:
        nb = Tq // SB_BLOCK
        qb = q.reshape(B, nb, SB_BLOCK, SB_HEADS, SB_HEAD_DIM).transpose(1, 0, 2, 3, 4)
        pb = q_pos.reshape(nb, SB_BLOCK)
        ob = lax.map(lambda a: sb_block(a[0], k, v, bias, a[1], k_pos), (qb, pb))
        return ob.transpose(1, 0, 2, 3, 4).reshape(B, Tq, SB_HEADS, SB_HEAD_DIM)
    return sb_block(q, k, v, bias, q_pos, k_pos)

def trunk(x, p, state_a, past_k, past_v, lbs, w_a_in, g_a_onorm, w_a_o, g_kv, w_kv, w_b_q, w_b_o, sb_bias,
          g_mix, g_ffn, w_ffn_in, w_ffn_out, g_ple, w_ple_in, w_ple_gate, g_final):
    B, L, _ = x.shape
    past_len = 0 if past_k is None else past_k.shape[1]
    q_pos = past_len + jnp.arange(L, dtype=jnp.int32)
    k_pos = jnp.arange(past_len + L, dtype=jnp.int32)
    h = x
    new_states = []
    k_new = v_new = k_all = v_all = None
    for layer in range(DEPTH):
        hn = rmsnorm(h, g_mix[layer])
        if layer < N_A:
            mix, s = hgrn2_mix(hn, state_a[layer], w_a_in[layer], lbs[layer], g_a_onorm[layer], w_a_o[layer])
            new_states.append(s)
        else:
            j = layer - N_A
            q = (hn @ w_b_q[j]).reshape(B, L, SB_HEADS, SB_HEAD_DIM)
            mix = sb_attention(q, k_all, v_all, sb_bias[j], q_pos, k_pos).reshape(B, L, SB_HD) @ w_b_o[j]
        h = h + mix
        h = h + swiglu(rmsnorm(h, g_ffn[layer]), w_ffn_in[layer], w_ffn_out[layer])
        h = h + ple_add(h, p[layer], g_ple[layer], w_ple_in[layer], w_ple_gate[layer])
        if layer == N_A - 1:
            kv = rmsnorm(h, g_kv) @ w_kv
            k_new = kv[..., :SB_HD].reshape(B, L, SB_HEADS, SB_HEAD_DIM)
            v_new = kv[..., SB_HD:].reshape(B, L, SB_HEADS, SB_HEAD_DIM)
            if past_k is None:
                k_all, v_all = k_new, v_new
            else:
                k_all = jnp.concatenate([past_k.astype(k_new.dtype), k_new], axis=1)
                v_all = jnp.concatenate([past_v.astype(v_new.dtype), v_new], axis=1)
    y = rmsnorm(h, g_final)
    return y, jnp.stack(new_states, axis=0), k_new, v_new

def setup_inputs(seed: int = 0) -> dict:
    key = jax.random.key(seed)
    ks = jax.random.split(key, 32)
    n_pages = PAST_LEN // PAGE_SIZE
    n_used = DEC_BATCH * n_pages
    n_pool = n_used + n_used // 4
    f32 = jnp.float32

    def nrm(k, shape, scale=1.0):
        return jax.random.normal(k, shape, f32) * scale

    def gain(k, shape):
        return 1.0 + 0.02 * jax.random.normal(k, shape, f32)

    perm = jax.random.permutation(ks[0], n_pool).astype(jnp.int32)
    page_table = perm[:n_used].reshape(DEC_BATCH, n_pages)
    return {
        "x_prompt": nrm(ks[1], (BATCH, SEQ, D_MODEL)),
        "x_sample": nrm(ks[2], (DEC_BATCH, DEC_SEQ, D_MODEL)),
        "p_prompt": nrm(ks[3], (DEPTH, BATCH, SEQ, PLE_DIM)),
        "p_sample": nrm(ks[4], (DEPTH, DEC_BATCH, DEC_SEQ, PLE_DIM)),
        "state_hgrn": nrm(ks[5], (N_A, DEC_BATCH, A_HEADS, A_KDIM, A_VDIM), 0.3),
        "cache_k": nrm(ks[6], (n_pool, PAGE_SIZE, SB_HEADS, SB_HEAD_DIM)),
        "cache_v": nrm(ks[7], (n_pool, PAGE_SIZE, SB_HEADS, SB_HEAD_DIM)),
        "page_table": page_table,
        "a_lb": nrm(ks[8], (N_A + 1, A_HK), 0.1),
        "w_a_in": nrm(ks[9], (N_A, D_MODEL, 2 * A_HK + 2 * A_HV), D_MODEL ** -0.5),
        "g_a_onorm": gain(ks[10], (N_A, A_HV)),
        "w_a_o": nrm(ks[11], (N_A, A_HV, D_MODEL), A_HV ** -0.5),
        "g_kv": gain(ks[12], (D_MODEL,)),
        "w_kv": nrm(ks[13], (D_MODEL, 2 * SB_HD), D_MODEL ** -0.5),
        "w_b_q": nrm(ks[14], (N_B, D_MODEL, SB_HD), D_MODEL ** -0.5),
        "w_b_o": nrm(ks[15], (N_B, SB_HD, D_MODEL), SB_HD ** -0.5),
        "sb_bias": SB_BIAS_INIT + nrm(ks[24], (N_B, SB_HEADS), 0.1),
        "g_mix": gain(ks[16], (DEPTH, D_MODEL)),
        "g_ffn": gain(ks[17], (DEPTH, D_MODEL)),
        "w_ffn_in": nrm(ks[18], (DEPTH, D_MODEL, 2 * D_FF), D_MODEL ** -0.5),
        "w_ffn_out": nrm(ks[19], (DEPTH, D_FF, D_MODEL), D_FF ** -0.5),
        "g_ple": gain(ks[20], (DEPTH, D_MODEL)),
        "w_ple_in": nrm(ks[21], (DEPTH, PLE_DIM, D_MODEL), PLE_DIM ** -0.5),
        "w_ple_gate": nrm(ks[22], (DEPTH, D_MODEL, D_MODEL), D_MODEL ** -0.5),
        "g_final": gain(ks[23], (D_MODEL,)),
    }

def reference(x_prompt, x_sample, p_prompt, p_sample, state_hgrn, cache_k, cache_v, page_table,
              a_lb, w_a_in, g_a_onorm, w_a_o, g_kv, w_kv, w_b_q, w_b_o, sb_bias, g_mix, g_ffn,
              w_ffn_in, w_ffn_out, g_ple, w_ple_in, w_ple_gate, g_final):
    lbs = jnp.cumsum(jax.nn.softmax(a_lb.astype(jnp.float32), axis=0), axis=0)[:N_A]

    s0_prompt = jnp.zeros((N_A, x_prompt.shape[0], A_HEADS, A_KDIM, A_VDIM), jnp.float32)
    y_prompt, st_prompt, k_prompt, v_prompt = trunk(
        x_prompt, p_prompt, s0_prompt, None, None, lbs, w_a_in, g_a_onorm, w_a_o, g_kv, w_kv,
        w_b_q, w_b_o, sb_bias, g_mix, g_ffn, w_ffn_in, w_ffn_out, g_ple, w_ple_in, w_ple_gate, g_final)

    db, n_pages = page_table.shape
    past_k = cache_k[page_table].reshape(db, n_pages * PAGE_SIZE, SB_HEADS, SB_HEAD_DIM)
    past_v = cache_v[page_table].reshape(db, n_pages * PAGE_SIZE, SB_HEADS, SB_HEAD_DIM)
    y_sample, st_sample, k_sample, v_sample = trunk(
        x_sample, p_sample, state_hgrn, past_k, past_v, lbs, w_a_in, g_a_onorm, w_a_o, g_kv, w_kv,
        w_b_q, w_b_o, sb_bias, g_mix, g_ffn, w_ffn_in, w_ffn_out, g_ple, w_ple_in, w_ple_gate, g_final)

    return (y_prompt, y_sample, st_prompt, st_sample, k_prompt, v_prompt, k_sample, v_sample)


_drawn_inputs = setup_inputs


def setup_inputs(seed=0):
    import zlib

    import numpy as np

    out = dict(_drawn_inputs(seed))
    spreads = {}
    factors = {'g_a_onorm': 5.338,
     'g_kv': 8.235,
     'sb_bias': 64.0,
     'g_mix': 2.714,
     'g_ffn': 3.393,
     'g_ple': 64.0,
     'g_final': 8.468,
     'w_b_q': 8.0,
     'w_b_o': 8.0}
    for name, (base, spread) in spreads.items():
        noise = np.random.default_rng([zlib.crc32(name.encode()), seed]).standard_normal(out[name].shape)
        drawn = base * np.exp(spread * noise) if base else spread * noise
        out[name] = __import__('jax').numpy.asarray(drawn.astype(out[name].dtype))
    for name, factor in factors.items():
        out[name] = (out[name] * factor).astype(out[name].dtype)
    return out
```

```python
from contextlib import ExitStack, contextmanager

import numpy as np

import concourse.bass as bass
from concourse import mybir

F32 = mybir.dt.float32
F32R = mybir.dt.float32r
BF16 = mybir.dt.bfloat16
I32 = mybir.dt.int32
ALU = mybir.AluOpType
ACT = mybir.ActivationFunctionType
AX_X = mybir.AxisListType.X

P = 128
D = 1024
KT = D // P
TP = 1024
NB, QS = 8, 4
TS = NB * QS
T = TP + TS
G = 3
GW = T // G
FF = 2816
FT = FF // P
PLE = 256
PK = PLE // P
HEADS_A = 8
HEADS_B = 16
PAIRS = HEADS_B // 2
HD = 64
NPG = 8
POOLPG = 80
EPS = 1e-6
SLAB = 8 * P
TILES_A = TP // P
LN_FLOOR = 7.6e-10
HALVES = (64, 32, 16, 8, 4)
NL = len(HALVES)
XQ, XK, XQD, XKD = NL, NL + 1, NL + 2, NL + 3
NX = NL + 4
GRP = 256
BIG = 1e30

N_A = HEADS_A * 6
N_F = FT * 3
N_P = KT * 2
N_KV = 16
N_Q = 8
N_O = 8
BEFORE = N_A + N_F + N_P + N_KV + N_Q
NSLAB = BEFORE + N_O + N_F + N_P


class Count:

    def __init__(self):
        self.n = 0
        self.off = 0

    def up(self, k=1):
        self.n += k
        return self.n + self.off

    def at(self):
        return self.n + self.off


@contextmanager
def looped(i, reps, **counts):
    for c, k in counts.values():
        c.off = i * k
    start = {n: c.n for n, (c, k) in counts.items()}
    yield
    for n, (c, k) in counts.items():
        assert c.n - start[n] == k, (n, c.n - start[n], k)
        c.n = start[n] + k * reps
        c.off = 0


def turns(eng, reps, peel, **counts):
    for t in range(peel):
        yield t
    with eng.Fori(peel, reps) as i, looped(i - peel, reps - peel, **counts):
        yield i


def wait(eng, sem, value):
    if isinstance(value, int) and value <= 0:
        return
    eng.wait_ge(sem, value)


def yoco_step(nc, wstream, xT, pT, state, kT_cache, v_cache, table, lbT, gains, g_on, sb_bias,
              yT, st_prompt, st_sample, kT_out, vT_out):
    with ExitStack() as ctx:
        def sb(name, shape, dt=F32):
            return ctx.enter_context(nc.sbuf_tensor(name, shape, dt))

        def sem(name):
            return ctx.enter_context(nc.semaphore(name))

        qT_scratch = nc.dram_tensor("qT_scratch", [D, T], F32, kind="Internal").ap()

        psum = ctx.enter_context(nc.psum_tensor("psum", [P, 8, 512], F32))
        bank = [psum[:, i, :] for i in range(8)]

        h = sb("h", [P, KT, T])
        xh = sb("xh", [P, KT, T], F32R)
        xl = sb("xl", [P, KT, T], F32R)
        raw = sb("raw", [P, 2, SLAB])
        wh = sb("wh", [P, 2, SLAB], F32R)
        wl = sb("wl", [P, 2, SLAB], F32R)
        ah = sb("ah", [P, 2, T], F32R)
        al = sb("al", [P, 2, T], F32R)
        rstd = sb("rstd", [P, T])
        ident = sb("ident", [P, P])
        ones = sb("ones", [P, P])
        gain = sb("gain", [P, 8, KT])
        gon = sb("gon", [P, HEADS_A])
        lbr = sb("lbr", [P, 2, KT])
        lb = sb("lb", [P, KT])
        omlb = sb("omlb", [P, KT])
        biasB = sb("biasB", [P, HEADS_B])
        c_eps = sb("c_eps", [P, 1])
        c_one = sb("c_one", [P, 1])
        c_epsv = sb("c_epsv", [P, 1])
        WORK = 12900
        work = sb("work", [P, WORK])

        class Carve:
            def __init__(self):
                self.at = 0

            def take(self, *shape):
                n = int(np.prod(shape))
                v = work[:, self.at:self.at + n]
                self.at += n
                assert self.at <= WORK, self.at
                if len(shape) == 2:
                    return v.rearrange("p (a b) -> p a b", a=shape[0])
                if len(shape) == 3:
                    return v.rearrange("p (a b c) -> p a b c", a=shape[0], b=shape[1])
                return v

        s_const = sem("s_const")
        s_cload = sem("s_cload")
        s_xload = sem("s_xload")
        landed = [sem("landed0"), sem("landed1")]
        split_go = sem("split_go")
        split_hi = sem("split_hi")
        w_ready = sem("w_ready")
        w_used = sem("w_used")
        unit_done = sem("unit_done")
        unit_free = sem("unit_free")
        xh_done = sem("xh_done")
        x_ready = sem("x_ready")
        sq_done = sem("sq_done")
        ssq_done = sem("ssq_done")
        nsum_done = sem("nsum_done")
        rstd_done = sem("rstd_done")
        dself = sem("dself")
        aself = sem("aself")
        act_in = sem("act_in")
        fg_done = sem("fg_done")
        g_done = sem("g_done")
        d_done = sem("d_done")
        e_done = sem("e_done")
        xg_ready = sem("xg_ready")
        pe_lev = sem("pe_lev")
        lev_free = sem("lev_free")
        att_done = sem("att_done")
        pe_kt = sem("pe_kt")
        kd_tok = sem("kd_tok")
        pe_u = sem("pe_u")
        s_done = sem("s_done")
        pe_o = sem("pe_o")
        o_copied = sem("o_copied")
        osq_done = sem("osq_done")
        pe_osum = sem("pe_osum")
        orstd_done = sem("orstd_done")
        on_done = sem("on_done")
        pe_vt = sem("pe_vt")
        v_tok_done = sem("v_tok_done")
        s0_in = sem("s0_in")
        s_out = sem("s_out")
        gate_act = sem("gate_act")
        a_prod = sem("a_prod")
        a_hi = sem("a_hi")
        a_ready = sem("a_ready")
        p_in = sem("p_in")
        stg_out = [sem("stg_out0"), sem("stg_out1")]
        y_done = sem("y_done")
        y_out = sem("y_out")
        pair_in = sem("pair_in")
        pair_free = sem("pair_free")
        pe_v8 = sem("pe_v8")
        v8_done = sem("v8_done")
        pe_z = sem("pe_z")
        min_done = sem("min_done")
        sp_in = sem("sp_in")
        la_mid = sem("la_mid")
        la_done = sem("la_done")
        aexp = sem("aexp")
        pe_at = sem("pe_at")
        at_done = sem("at_done")
        pe_av = sem("pe_av")
        av_done = sem("av_done")
        pe_ot = sem("pe_ot")
        o_hi = sem("o_hi")
        o_lo = sem("o_lo")
        work_free = sem("work_free")
        maskd = sem("maskd")
        tb_in = sem("tb_in")
        q_in = sem("q_in")
        pg_k = [sem("pg_k0"), sem("pg_k1")]
        pg_v = [sem("pg_v0"), sem("pg_v1")]
        kpg_free = sem("kpg_free")
        vpg_free = sem("vpg_free")
        qblk_done = sem("qblk_done")
        pe_vn = sem("pe_vn")
        vn_done = sem("vn_done")
        sz_done = sem("sz_done")
        sx_done = sem("sx_done")
        sl_done = sem("sl_done")
        ssp_done = sem("ssp_done")
        stail = sem("stail")
        sla = sem("sla")
        sexp = sem("sexp")
        sav = sem("sav")
        so_done = sem("so_done")

        w = Carve()
        tq, tf = w.take(T), w.take(T)
        qa, ka, ga = w.take(T), w.take(T), w.take(T)
        og = w.take(T)
        X = w.take(NX, GRP)
        tv = X.rearrange("p a b -> p (a b)")[:, 0:T]
        vb = X.rearrange("p a b -> p (a b)")[0:TS, 0:NB * P].rearrange("p (a b) -> p a b", a=NB)
        vtok = w.take(TILES_A + 1, P)
        kdt = w.take(P)
        prod = w.take(6, P)
        att = w.take(P)
        o_s, orst = w.take(GRP), w.take(GRP)
        S = w.take(P)
        S0 = w.take(NB, P)
        dec = w.take(16)
        bmask = w.take(NB)
        maskA = sb("maskA", [P, NL + 1, P], BF16)
        reset = sb("reset", [P, T], BF16)
        w = Carve()
        sq = w.take(KT, GW)
        ssq = w.take(G, GW)
        gate_s = w.take(T)
        up_s = w.take(T)
        praw = w.take(PK, T)
        stage = w.take(2, T)
        w = Carve()
        qc, kc, vc = w.take(TP), w.take(TP), w.take(TP)
        v8 = w.take(KT, P)
        lbuf = w.take(2, TP)
        spb = w.take(2, TP)
        tb_ = w.take(TP)
        aT = w.take(TP)
        o_t = w.take(P)
        tri_le = w.take(P)
        lim = w.take(P)
        ot_s = w.take(P)
        w = Carve()
        kpg = w.take(2, D)
        vpg = w.take(2, D)
        qs_ = w.take(PAIRS, TS)
        qblk = w.take(PAIRS, NB, 2 * QS)
        kn = w.take(PAIRS, TS)
        vnT = w.take(PAIRS, TS)
        vn = w.take(D)
        bcol = w.take(PAIRS * 2 * QS)
        szx = w.take(NPG + 1, 64)
        szl = w.take(NPG + 1, 64)
        ssp = w.take(NPG + 1, 64)
        suf = w.take(NPG, 64)
        sa = w.take(NPG + 1, 64)
        triP = w.take(P)
        mnew = w.take(NB * QS)
        lnew = w.take(NB * QS)
        osm = w.take(64)
        zer = w.take(P)
        tbl = sb("tbl", [1, NB * NPG], I32)

        U_A = HEADS_A * 36
        U_F0 = U_A + FT * 30
        U_P0 = U_F0 + KT * 6
        U_KV = U_P0 + 16 * G
        U_Q = U_KV + KT * G
        U_O = U_Q + KT * G
        U_F1 = U_O + FT * 30
        U_P1 = U_F1 + KT * 6
        G_MIX0, G_FFN0, G_PLE0, G_KV, G_MIX1, G_FFN1, G_PLE1, G_FIN = range(8)

        def cols(g):
            return slice(g * GW, (g + 1) * GW)

        def flat(ap):
            return ap.bitcast(F32)

        block = ctx.enter_context(nc.Block())

        @block.sync
        def _(sp):
            sp.dma_start(h[:, :, :], xT.rearrange("(k p) t -> p k t", p=P)).then_inc(s_xload, 16)
            n = Count()

            def load_slab(slot):
                i = n.up()
                wait(sp, w_ready, i - 2)
                src = wstream[bass.ds(i - 1, 1), :, :].rearrange("o p c -> (o p) c")
                sp.dma_start(raw[:, slot, :], src).then_inc(landed[slot], 16)

            load_slab(0)
            load_slab(1)
            with sp.Fori(0, BEFORE // 2 - 1) as i, looped(i, BEFORE // 2 - 1, n=(n, 2)):
                load_slab(0)
                load_slab(1)
            sp.wait_ge(stg_out[0], 16 * 12)
            sp.wait_ge(stg_out[1], 16 * 12)
            sp.dma_start(tbl[0:1, :], table).then_inc(tb_in, 16)
            with sp.Fori(0, PAIRS) as j:
                sp.wait_ge(pair_free, j + 1)
                for dst, src in ((qc, qT_scratch), (kc, kT_out), (vc, vT_out)):
                    sp.dma_start(dst, src[bass.ds(j * P, P), 0:TP]).then_inc(pair_in, 16)
            sp.wait_ge(pair_free, PAIRS + 1)
            sp.wait_ge(work_free, 1)
            for dst, src in ((qs_, qT_scratch), (kn, kT_out), (vnT, vT_out)):
                sp.dma_start(dst, src.rearrange("(j p) t -> p j t", p=P)[:, :, TP:T]).then_inc(q_in, 16)
            sp.wait_ge(tb_in, 16)
            with sp.Fori(0, NB) as b:
                for pg in range(NPG):
                    s = pg % 2
                    phys = sp.value_load(tbl[0:1, bass.ds(b * NPG + pg, 1)], min_val=0, max_val=POOLPG - 1)
                    sp.wait_ge(kpg_free, b * NPG + pg + 1)
                    sp.dma_start(kpg[:, s, :], kT_cache[bass.ds(phys, 1), :, :].rearrange("o p c -> (o p) c"))\
                        .then_inc(pg_k[s], 16)
                for pg in range(NPG):
                    s = pg % 2
                    phys = sp.value_load(tbl[0:1, bass.ds(b * NPG + pg, 1)], min_val=0, max_val=POOLPG - 1)
                    sp.wait_ge(vpg_free, b * NPG + pg + 1)
                    sp.dma_start(vpg[:, s, :], v_cache[bass.ds(phys, 1), :, :].rearrange("o p c -> (o p) c"))\
                        .then_inc(pg_v[s], 16)
            rest = (NSLAB - BEFORE) // 2
            with sp.Fori(0, rest) as i, looped(i, rest, n=(n, 2)):
                load_slab(0)
                load_slab(1)
            sp.wait_ge(y_done, KT)
            sp.dma_start(yT.rearrange("(k p) t -> p k t", p=P), h[:, :, :]).then_inc(y_out, 16)
            sp.wait_ge(y_out, 16)

        @block.gpsimd
        def _(pool):
            own = Count()

            def did(ins):
                ins.then_inc(s_const, 1)
                pool.wait_ge(s_const, own.up())

            did(nc.gpsimd.memset(ident[:, :], 0.0))
            did(nc.gpsimd.affine_select(out=ident[:, :], in_=ident[:, :], compare_op=ALU.not_equal, fill=1.0,
                                        base=0, pattern=[[-1, P]], channel_multiplier=1))
            did(nc.gpsimd.memset(ones[:, :], 1.0))
            did(nc.gpsimd.memset(c_eps[:, :], EPS))
            did(nc.gpsimd.memset(c_one[:, :], 1.0))
            did(nc.gpsimd.memset(c_epsv[:, :], 30.0))
            did(nc.gpsimd.memset(maskA[:, :, :], 1.0))
            for l, hf in enumerate(HALVES):
                nb = P // (2 * hf)
                m = maskA[:, l, :].rearrange("p (b r) -> p b r", b=nb)
                did(nc.gpsimd.affine_select(out=m, in_=m, compare_op=ALU.is_ge, fill=0.0, base=0,
                                            pattern=[[-2 * hf, nb], [0, 2 * hf]], channel_multiplier=1))
                did(nc.gpsimd.affine_select(out=m, in_=m, compare_op=ALU.is_ge, fill=0.0, base=hf - 1,
                                            pattern=[[2 * hf, nb], [0, 2 * hf]], channel_multiplier=-1))
                did(nc.gpsimd.memset(m[:, :, 0:hf], 0.0))
            m = maskA[:, NL, :].rearrange("p (b r) -> p b r", r=4)
            did(nc.gpsimd.affine_select(out=m, in_=m, compare_op=ALU.is_ge, fill=0.0, base=0,
                                        pattern=[[-4, P // 4], [0, 4]], channel_multiplier=1))
            did(nc.gpsimd.affine_select(out=m, in_=m, compare_op=ALU.is_ge, fill=0.0, base=0,
                                        pattern=[[4, P // 4], [1, 4]], channel_multiplier=-1))
            did(nc.gpsimd.memset(reset[:, :], 1.0))
            did(nc.gpsimd.memset(reset[:, 0:TP:P], 0.0))
            did(nc.gpsimd.memset(reset[:, TP:T:QS], 0.0))
            did(nc.gpsimd.memset(bmask, 1.0))
            did(nc.gpsimd.affine_select(out=bmask, in_=bmask, compare_op=ALU.is_ge, fill=0.0, base=0,
                                        pattern=[[-QS, NB]], channel_multiplier=1))
            did(nc.gpsimd.affine_select(out=bmask, in_=bmask, compare_op=ALU.is_ge, fill=0.0, base=QS - 1,
                                        pattern=[[QS, NB]], channel_multiplier=-1))
            n = Count()

            def split(slot):
                i = n.up()
                arrived = ((n.n - 1) // 2 + 1) * 16 + n.off * 8
                pool.wait_ge(landed[slot], arrived)
                wait(pool, w_used, i - 2)
                pool.sem_inc(split_go, 1)
                nc.gpsimd.tensor_copy(wh[:, slot, :], raw[:, slot, :]).then_inc(split_hi, 1)
                pool.wait_ge(split_hi, i)
                nc.gpsimd.tensor_tensor(wl[:, slot, :], raw[:, slot, :], flat(wh[:, slot, :]), ALU.subtract)\
                    .then_inc(w_ready, 1)

            split(0)
            split(1)
            pairs = BEFORE // 2 - 1
            with pool.Fori(0, pairs) as i, looped(i, pairs, n=(n, 2)):
                split(0)
                split(1)
            pool.wait_ge(stg_out[0], 16 * 12)
            pool.wait_ge(stg_out[1], 16 * 12)
            for m, val in ((tri_le, 1.0), (lim, BIG)):
                did(nc.gpsimd.memset(m, val))
                did(nc.gpsimd.affine_select(out=m, in_=m, compare_op=ALU.is_ge, fill=(0.0 if val == 1.0 else -BIG),
                                            base=-1, pattern=[[-1, P]], channel_multiplier=1))
            pool.sem_inc(maskd, 1)
            pool.sem_inc(pair_free, 1)
            pool.wait_ge(pair_free, PAIRS + 1)
            pool.wait_ge(o_lo, 8 * PAIRS)
            for m, val, fill in ((triP, 1.0, 0.0),):
                did(nc.gpsimd.memset(m, val))
                did(nc.gpsimd.affine_select(out=m, in_=m, compare_op=ALU.is_ge, fill=fill, base=0,
                                            pattern=[[-1, P]], channel_multiplier=1))
            for m, val, fill in ((mnew, 1.0, 0.0), (lnew, BIG, -BIG)):
                m3 = m.rearrange("p (b q) -> p b q", b=NB)
                did(nc.gpsimd.memset(m, val))
                did(nc.gpsimd.affine_select(out=m3, in_=m3, compare_op=ALU.is_ge, fill=fill, base=0,
                                            pattern=[[-QS, NB], [0, QS]], channel_multiplier=1))
                did(nc.gpsimd.affine_select(out=m3, in_=m3, compare_op=ALU.is_ge, fill=fill, base=-1,
                                            pattern=[[QS, NB], [1, QS]], channel_multiplier=-1))
            did(nc.gpsimd.memset(zer, 0.0))
            did(nc.gpsimd.memset(qblk, 0.0))
            pool.sem_inc(maskd, 1)
            pool.sem_inc(work_free, 1)
            pool.sem_inc(kpg_free, 2)
            pool.sem_inc(vpg_free, 2)
            rest = (NSLAB - BEFORE) // 2
            with pool.Fori(0, rest) as i, looped(i, rest, n=(n, 2)):
                split(0)
                split(1)

        @block.scalar
        def _(act):
            own, sqs, nsums = Count(), Count(), Count()
            units = Count()

            def did(ins):
                ins.then_inc(aself, 1)
                act.wait_ge(aself, own.up())

            act.dma_start(gain[:, :, :], gains).then_inc(s_cload, 16)
            act.dma_start(gon[:, :], g_on).then_inc(s_cload, 16)
            act.dma_start(lbr[:, :, :], lbT).then_inc(s_cload, 16)
            act.dma_start(biasB[:, :], sb_bias.broadcast_to([P, HEADS_B])).then_inc(s_cload, 16)
            act.wait_ge(s_cload, 64)
            act.wait_ge(s_const, 5)
            act.wait_ge(dself, 1)
            did(nc.scalar.activation(omlb[:, :], lb[:, :], ACT.Sigmoid, scale=-1.0))
            did(nc.scalar.activation(lb[:, :], lb[:, :], ACT.Sigmoid))

            def norm(gi):
                for g in range(G):
                    for k in range(KT if gi is not None else 0):
                        nc.scalar.activation(xh[:, k, cols(g)], h[:, k, cols(g)], ACT.Copy,
                                             scale=gain[:, gi, k:k + 1]).then_inc(xh_done, 1)
                    i = sqs.up()
                    wait(act, ssq_done, i - 1)
                    nc.scalar.activation(sq, h[:, :, cols(g)], ACT.Square).then_inc(sq_done, 1)
                for g in range(G):
                    act.wait_ge(nsum_done, nsums.up())
                    did(nc.scalar.activation(rstd[:, cols(g)], bank[4 + g][:, 0:GW], ACT.Ln,
                                             bias=c_eps[:, 0:1], scale=1.0 / D))
                    nc.scalar.activation(rstd[:, cols(g)], rstd[:, cols(g)], ACT.Exp, scale=-0.5)\
                        .then_inc(rstd_done, 1)

            act.wait_ge(s_xload, 16)
            norm(G_MIX0)

            forget, decays, exponents, kts, outs, osums, vts, states, heads, vtoks, ons = [Count() for _ in range(11)]

            def group_exps(first, width):
                act.wait_ge(d_done, exponents.up())
                nc.scalar.activation(X[:, first:NX, 0:width], X[:, first:NX, 0:width], ACT.Exp).then_inc(e_done, 1)

            def tile_copies(rows, at, fresh):
                i = kts.up()
                act.wait_ge(pe_kt, i)
                wait(act, pe_u, i - 1)
                nc.scalar.activation(kdt[0:rows, :], bank[5][0:rows, 0:P], ACT.Copy).then_inc(kd_tok, 1)
                act.wait_ge(pe_o, outs.up())
                if fresh:
                    wait(act, on_done, ons.up() - 1)
                nc.scalar.activation(o_s[:, at:at + rows], bank[7][:, at:at + rows], ACT.Copy).then_inc(o_copied, 1)

            def output_rms(width):
                act.wait_ge(pe_osum, osums.up())
                did(nc.scalar.activation(orst[:, 0:width], bank[7][:, GRP:GRP + width], ACT.Ln,
                                         bias=c_eps[:, 0:1], scale=1.0 / P))
                nc.scalar.activation(orst[:, 0:width], orst[:, 0:width], ACT.Exp, scale=-0.5).then_inc(orstd_done, 1)

            def v_copies():
                for c in range(TILES_A + 1):
                    rows = P if c < TILES_A else TS
                    act.wait_ge(pe_vt, vts.up())
                    nc.scalar.activation(vtok[0:rows, c, :], bank[5 + c % 2][0:rows, 0:P], ACT.Copy)\
                        .then_inc(v_tok_done, 1)

            def gate_act_og():
                act.wait_ge(unit_free, units.up(4 * G))
                nc.scalar.activation(og, og, ACT.Silu).then_inc(act_in, 1)

            def mix(head):
                wait(act, s_out, (heads.up() - 1) * 32)
                act.dma_start(S0, state[bass.ds(head, 1), :, :, :].rearrange("o p b v -> (o p) b v")).then_inc(s0_in, 16)
                nc.scalar.activation(qa, tq, ACT.Silu).then_inc(act_in, 1)
                nc.scalar.activation(tf, tf, ACT.Sigmoid).then_inc(act_in, 1)
                act.wait_ge(fg_done, forget.up())
                nc.scalar.activation(tf, tf, ACT.Ln).then_inc(act_in, 1)
                act.wait_ge(g_done, decays.up())
                nc.scalar.activation(dec[:, 0:TILES_A], ga[:, P - 1:TP:P], ACT.Exp)
                nc.scalar.activation(dec[:, TILES_A:16], ga[:, TP + QS - 1:T:QS], ACT.Exp).then_inc(e_done, 1)
                group_exps(0, GRP)
                for g in range(TP // GRP):
                    tile_copies(P, 0, True)
                    tile_copies(P, P, False)
                    if g < TP // GRP - 1:
                        group_exps(0, GRP)
                    else:
                        group_exps(XQ, TS)
                    output_rms(GRP)
                tile_copies(TS, 0, True)
                output_rms(TS)
                act.wait_ge(s_done, states.up(TILES_A + 2))
                act.dma_start(st_prompt[bass.ds(head, 1), :, :].rearrange("o p v -> (o p) v"), S).then_inc(s_out, 16)
                act.dma_start(st_sample[bass.ds(head, 1), :, :, :].rearrange("o p b v -> (o p) b v"), S0)\
                    .then_inc(s_out, 16)

            gate_act_og()
            v_copies()
            rounds = HEADS_A - 1
            for i in turns(
                    act, rounds, 1, own=(own, 5), fo=(forget, 1), de=(decays, 1), ex=(exponents, 5), kt=(kts, 9),
                    ou=(outs, 9), os=(osums, 5), vt=(vts, 9), st=(states, TILES_A + 2), he=(heads, 1), on=(ons, 5),
                    un=(units, 36)):
                mix(i)
                gate_act_og()
                v_copies()
                units.up(24)
            mix(rounds)
            units.up(24)

            gates, prods, ples = Count(), Count(), Count()

            def gate_groups(func):
                for g in range(G):
                    act.wait_ge(unit_free, units.up())
                    nc.scalar.activation(gate_s[:, cols(g)], gate_s[:, cols(g)], func).then_inc(gate_act, 1)

            def ffn(gi):
                act.wait_ge(unit_free, units.at())
                norm(gi)
                with act.Fori(0, FT // 2) as i, looped(i, FT // 2, un=(units, 60), pr=(prods, 6)):
                    for buf in range(2):
                        gate_groups(ACT.Silu)
                        for g in range(G):
                            act.wait_ge(a_prod, prods.up())
                            nc.scalar.activation(ah[:, buf, cols(g)], up_s[:, cols(g)], ACT.Copy).then_inc(a_hi, 1)
                        units.up(G)
                    units.up(2 * KT * G)

            def ple(gi, layer):
                act.wait_ge(unit_free, units.at())
                act.dma_start(praw, pT[bass.ds(layer, 1), :, :, :].rearrange("o p k t -> (o p) k t")).then_inc(p_in, 16)
                norm(gi)
                act.wait_ge(p_in, 16 * ples.up())
                nc.scalar.activation(ah[:, :, :], praw, ACT.Copy).then_inc(a_hi, 1)
                with act.Fori(0, KT) as i, looped(i, KT, un=(units, 6)):
                    gate_groups(ACT.Sigmoid)
                    units.up(G)

            def staged(dst):
                dst_t = dst.rearrange("(n p) t -> n p t", p=P)
                with act.Fori(0, KT // 2) as i, looped(i, KT // 2, un=(units, 2 * G)):
                    for s in range(2):
                        act.wait_ge(unit_free, units.up(G))
                        act.dma_start(dst_t[bass.ds(2 * i + s, 1), :, :].rearrange("o p t -> (o p) t"), stage[:, s, :])\
                            .then_inc(stg_out[s], 16)

            ffn(G_FFN0)
            ple(G_PLE0, 0)
            act.wait_ge(unit_free, units.at())
            norm(G_KV)
            staged(kT_out)
            staged(vT_out)
            act.wait_ge(w_used, BEFORE - N_Q)
            norm(G_MIX1)
            staged(qT_scratch)
            assert units.n == U_Q

            v8s, mins, las, avs, ots = [Count() for _ in range(5)]
            act.wait_ge(maskd, 1)
            for j in turns(act, PAIRS, 1, own=(own, 16), v8=(v8s, 8), mi=(mins, 16), la=(las, 16),
                                                 av=(avs, 16), ot=(ots, 8)):
                for c in range(8):
                    act.wait_ge(pe_v8, v8s.up())
                    nc.scalar.activation(v8[:, c, :], bank[6 + c % 2][:, 0:P], ACT.Copy).then_inc(v8_done, 1)
                for it in range(20):
                    if it < 16:
                        L = P * (it // 2 + 1)
                        lb_ = lbuf[:, it % 2, 0:L]
                        act.wait_ge(min_done, mins.up())
                        did(nc.scalar.activation(lb_, lb_, ACT.Exp))
                        nc.scalar.activation(lb_, lb_, ACT.Ln, bias=c_one[:, 0:1]).then_inc(sp_in, 1)
                    if 1 <= it < 17:
                        a = spb[:, (it - 1) % 2, 0:P * ((it - 1) // 2 + 1)]
                        act.wait_ge(la_done, las.up())
                        nc.scalar.activation(a, a, ACT.Exp).then_inc(aexp, 1)
                    if 3 <= it < 19:
                        hh, qt = (it - 3) % 2, (it - 3) // 2
                        act.wait_ge(pe_av, avs.up())
                        nc.scalar.activation(o_t[:, hh * HD:(hh + 1) * HD], bank[6][:, hh * HD:(hh + 1) * HD], ACT.Copy)\
                            .then_inc(av_done, 1)
                        if hh == 1:
                            act.wait_ge(pe_ot, ots.up())
                            nc.scalar.activation(
                                xh[:, bass.ds(j, 1), qt * P:(qt + 1) * P],
                                bank[7][:, P:2 * P].rearrange("p (o c) -> p o c", o=1), ACT.Copy).then_inc(o_hi, 1)

            for half in range(2):
                act.wait_ge(pe_vn, half + 1)
                nc.scalar.activation(vn[0:TS, half * 512:(half + 1) * 512], bank[6 + half][0:TS, :], ACT.Copy)\
                    .then_inc(vn_done, 1)
            seqs = Count()
            with act.Fori(0, NB) as b, looped(b, NB, own=(own, 1), se=(seqs, 1)):
                i = seqs.up()
                act.wait_ge(sx_done, i)
                nc.scalar.activation(szl[:, 0:NPG, :], szl[:, 0:NPG, :], ACT.Exp)
                did(nc.scalar.activation(szl[0:TS, NPG, :], szl[0:TS, NPG, :], ACT.Exp))
                nc.scalar.activation(szl[:, 0:NPG, :], szl[:, 0:NPG, :], ACT.Ln, bias=c_one[:, 0:1])
                nc.scalar.activation(szl[0:TS, NPG, :], szl[0:TS, NPG, :], ACT.Ln, bias=c_one[0:TS, 0:1])\
                    .then_inc(sl_done, 1)
                act.wait_ge(sla, i)
                nc.scalar.activation(sa[:, 0:NPG, :], sa[:, 0:NPG, :], ACT.Exp)
                nc.scalar.activation(sa[0:TS, NPG, :], sa[0:TS, NPG, :], ACT.Exp).then_inc(sexp, 1)

            units.up(KT * G)
            ffn(G_FFN1)
            ple(G_PLE1, 1)
            act.wait_ge(unit_free, units.at())
            assert units.n == U_P1
            norm(None)
            act.wait_ge(s_out, HEADS_A * 32)
            act.wait_ge(stg_out[0], 16 * 12)
            act.wait_ge(stg_out[1], 16 * 12)

        @block.vector
        def _(dve):
            own, units = Count(), Count()
            xhs, sqs, rst = Count(), Count(), Count()

            def did(ins):
                ins.then_inc(dself, 1)
                dve.wait_ge(dself, own.up())

            dve.wait_ge(s_cload, 64)
            did(nc.vector.tensor_tensor(lb[:, :], lbr[:, 0, :], lbr[:, 1, :], ALU.subtract))

            def evac(dst):
                for g in range(G):
                    dve.wait_ge(unit_done, units.up())
                    nc.vector.tensor_tensor(dst[:, cols(g)], bank[g][:, 0:GW], rstd[:, cols(g)], ALU.mult)\
                        .then_inc(unit_free, 1)

            def add_to_h(n):
                for g in range(G):
                    dve.wait_ge(unit_done, units.up())
                    nc.vector.tensor_tensor(h[:, n, cols(g)], h[:, n, cols(g)], bank[g][:, 0:GW], ALU.add)\
                        .then_inc(unit_free, 1)

            def norm(gi):
                wait(dve, unit_free, units.at())
                for g in range(G):
                    for k in range(KT if gi is not None else 0):
                        dve.wait_ge(xh_done, xhs.up())
                        nc.vector.scalar_tensor_tensor(xl[:, k, cols(g)], h[:, k, cols(g)], gain[:, gi, k:k + 1],
                                                       flat(xh[:, k, cols(g)]), ALU.mult, ALU.subtract)\
                            .then_inc(x_ready, 1)
                    dve.wait_ge(sq_done, sqs.up())
                    nc.vector.tensor_reduce(ssq[:, g, :], sq.rearrange("p k t -> p t k"), AX_X, ALU.add)\
                        .then_inc(ssq_done, 1)
                dve.wait_ge(rstd_done, rst.up(G))

            norm(G_MIX0)

            ins_, exps, levs, us, os_, oc, orst_, heads, vts, gs, souts, fgs, ons = [Count() for _ in range(13)]

            def by_group(ap, at, width, *shape):
                v = ap[:, at:at + width]
                if len(shape) == 1:
                    return v.rearrange("p (b r) -> p b r", r=shape[0])
                return v.rearrange("p (b t r) -> p b t r", t=2, r=shape[1])

            def exponents(at, width, levels):
                if levels:
                    for l, hf in enumerate(HALVES):
                        gv = by_group(ga, at, width, 2, hf)
                        xv = by_group(X[:, l, :], 0, width, 2, hf)
                        nb = width // (2 * hf)
                        ref = gv[:, :, 0, hf - 1:hf].broadcast_to([P, nb, hf])
                        nc.vector.tensor_tensor(xv[:, :, 0, :], ref, gv[:, :, 0, :], ALU.subtract)
                        nc.vector.tensor_tensor(xv[:, :, 1, :], gv[:, :, 1, :], ref, ALU.subtract)
                gv = by_group(ga, at, width, QS)
                ref = gv[:, :, 1:2].broadcast_to([P, width // QS, QS])
                nc.vector.tensor_tensor(by_group(X[:, XQ, :], 0, width, QS), gv, ref, ALU.subtract)
                nc.vector.tensor_tensor(by_group(X[:, XK, :], 0, width, QS), ref, gv, ALU.subtract)
                nc.vector.tensor_copy(X[:, XQD, 0:width], ga[:, at:at + width])
                span = P if levels else QS
                gv = by_group(ga, at, width, span)
                ref = gv[:, :, span - 1:span].broadcast_to([P, width // span, span])
                nc.vector.tensor_tensor(by_group(X[:, XKD, :], 0, width, span), ref, gv, ALU.subtract)\
                    .then_inc(d_done, 1)

            def operands(at, width, levels):
                dve.wait_ge(e_done, exps.up())
                if levels:
                    for l, hf in enumerate(HALVES):
                        xv = by_group(X[:, l, :], 0, width, 2, hf)
                        for t, src in ((0, ka), (1, qa)):
                            nc.vector.tensor_tensor(xv[:, :, t, :], xv[:, :, t, :],
                                                    by_group(src, at, width, 2, hf)[:, :, t, :], ALU.mult)
                for slot, src in ((XQ, qa), (XK, ka), (XQD, qa), (XKD, ka)):
                    last = nc.vector.tensor_tensor(X[:, slot, 0:width], X[:, slot, 0:width], src[:, at:at + width],
                                                   ALU.mult)
                last.then_inc(xg_ready, 1)

            def scores(tile):
                for half, bk in ((0, 3), (1, 4)):
                    dve.wait_ge(pe_lev, levs.up())
                    nc.vector.tensor_tensor(prod[:, 3 * half:3 * half + 3, :],
                                            bank[bk][:, 0:3 * P].rearrange("p (l t) -> p l t", l=3),
                                            maskA[:, 3 * half:3 * half + 3, :], ALU.mult).then_inc(lev_free, 1)
                dve.wait_ge(lev_free, levs.at())
                wait(dve, pe_o, os_.at())
                nc.vector.tensor_reduce(att, prod.rearrange("p l t -> p t l"), AX_X, ALU.add).then_inc(att_done, 1)

            def new_state(tile):
                dve.wait_ge(pe_u, us.up())
                dve.wait_ge(pe_o, os_.up())
                dve.wait_ge(s_done, gs.at())
                nc.vector.scalar_tensor_tensor(S, S, dec[:, tile:tile + 1], bank[6][:, 0:P], ALU.mult, ALU.add)\
                    .then_inc(s_done, 1)
                gs.up()

            def squares(width, tiles):
                dve.wait_ge(o_copied, oc.up(tiles))
                dve.wait_ge(att_done, levatt.at())
                nc.vector.tensor_tensor(prod.rearrange("p l t -> p (l t)")[:, 0:width], o_s[:, 0:width],
                                        o_s[:, 0:width], ALU.mult).then_inc(osq_done, 1)

            def normed(at, width, head):
                dve.wait_ge(orstd_done, orst_.up())
                o = o_s[:, 0:width]
                did(nc.vector.tensor_tensor(o, o, orst[:, 0:width], ALU.mult))
                did(nc.vector.scalar_tensor_tensor(o, o, gon[:, bass.ds(head, 1)], og[:, at:at + width],
                                                   ALU.mult, ALU.mult))
                did(nc.vector.tensor_copy(ah[:, 0, at:at + width], o))
                nc.vector.tensor_tensor(al[:, 0, at:at + width], o, flat(ah[:, 0, at:at + width]), ALU.subtract)\
                    .then_inc(on_done, 1)
                ons.up()

            levatt = Count()

            def mix(head, ahead):
                wait(dve, s_out, (heads.up() - 1) * 32)
                nc.vector.memset(S, 0.0).then_inc(s_done, 1)
                gs.up()
                dve.wait_ge(act_in, ins_.up(3))
                did(nc.vector.tensor_scalar(tf, tf, omlb[:, bass.ds(head, 1)], lb[:, bass.ds(head, 1)],
                                            ALU.mult, ALU.add))
                did(nc.vector.tensor_scalar(tf, tf, LN_FLOOR, None, ALU.max))
                nc.vector.tensor_scalar(ka, tf, -1.0, 1.0, ALU.mult, ALU.add).then_inc(fg_done, 1)
                dve.wait_ge(act_in, ins_.up())
                nc.vector.tensor_tensor_scan(ga, reset[:, :], tf, 0.0, ALU.mult, ALU.add).then_inc(g_done, 1)
                dve.wait_ge(g_done, fgs.up())
                dve.wait_ge(pe_vt, vts.up(9))
                exps.up()
                exponents(0, GRP, True)
                operands(0, GRP, True)
                if ahead:
                    evac(tq)
                for g in range(TP // GRP):
                    for c in range(2):
                        scores(2 * g + c)
                        levatt.up()
                        new_state(2 * g + c)
                    squares(GRP, 2)
                    if g < TP // GRP - 1:
                        exponents((g + 1) * GRP, GRP, True)
                        operands((g + 1) * GRP, GRP, True)
                    else:
                        exponents(TP, TS, False)
                        operands(TP, TS, False)
                    normed(g * GRP, GRP, head)
                    if g == 0 and ahead:
                        evac(tf)
                dve.wait_ge(pe_lev, levs.up())
                dve.wait_ge(pe_o, os_.at())
                nc.vector.tensor_tensor(att[0:TS, 0:TS], bank[4][0:TS, 0:TS], maskA[0:TS, NL, 0:TS], ALU.mult)\
                    .then_inc(lev_free, 1)
                dve.wait_ge(lev_free, levs.at())
                nc.vector.tensor_tensor(vb, vtok[0:TS, TILES_A:TILES_A + 1, :].broadcast_to([TS, NB, P]),
                                        bmask[0:TS, :].rearrange("p (b o) -> p b o", o=1).broadcast_to([TS, NB, P]),
                                        ALU.mult).then_inc(att_done, 1)
                levatt.up()
                dve.wait_ge(pe_u, us.up())
                dve.wait_ge(pe_o, os_.up())
                did(nc.vector.tensor_tensor(S0, S0, dec[:, TILES_A:16].rearrange("p (b o) -> p b o", o=1)
                                            .broadcast_to([P, NB, P]), ALU.mult))
                nc.vector.tensor_tensor(S0[:, 0:4, :], S0[:, 0:4, :], bank[3].rearrange("p (b v) -> p b v", b=4), ALU.add)
                nc.vector.tensor_tensor(S0[:, 4:8, :], S0[:, 4:8, :], bank[4].rearrange("p (b v) -> p b v", b=4), ALU.add)\
                    .then_inc(s_done, 1)
                gs.up()
                squares(TS, 1)
                normed(TP, TS, head)
                if ahead:
                    evac(tv)
                    dve.wait_ge(on_done, ons.at())
                    evac(og)
                for n in range(KT):
                    add_to_h(n)
            for dst in (tq, tf, tv, og):
                evac(dst)
            rounds = HEADS_A - 1
            for i in turns(
                    dve, rounds, 1, own=(own, 18), un=(units, 36), ins=(ins_, 4), ex=(exps, 6), le=(levs, 17), us=(us, 9),
                    os=(os_, 9), oc=(oc, 9), ors=(orst_, 5), he=(heads, 1), vt=(vts, 9), gs=(gs, 10), fg=(fgs, 1),
                    on=(ons, 5), la=(levatt, 9)):
                mix(i, True)
            mix(rounds, False)
            assert units.n == U_A

            gates, his = Count(), Count()

            def ffn(gi):
                norm(gi)
                with dve.Fori(0, FT // 2) as i, looped(i, FT // 2, un=(units, 60), ga=(gates, 6), hi=(his, 6)):
                    for buf in range(2):
                        evac(gate_s)
                        evac(up_s)
                        dve.wait_ge(unit_free, units.at())
                        for g in range(G):
                            dve.wait_ge(gate_act, gates.up())
                            nc.vector.tensor_tensor(up_s[:, cols(g)], up_s[:, cols(g)], gate_s[:, cols(g)], ALU.mult)\
                                .then_inc(a_prod, 1)
                        for g in range(G):
                            dve.wait_ge(a_hi, his.up())
                            nc.vector.tensor_tensor(al[:, buf, cols(g)], up_s[:, cols(g)], flat(ah[:, buf, cols(g)]),
                                                    ALU.subtract).then_inc(a_ready, 1)
                    for buf in range(2):
                        for n in range(KT):
                            add_to_h(n)

            def ple(gi):
                norm(gi)
                dve.wait_ge(a_hi, his.up())
                nc.vector.tensor_tensor(al[:, :, :], praw, flat(ah[:, :, :]), ALU.subtract).then_inc(a_ready, 1)
                with dve.Fori(0, KT) as n, looped(n, KT, un=(units, 6), ga=(gates, 3), own=(own, 3)):
                    evac(gate_s)
                    for g in range(G):
                        dve.wait_ge(gate_act, gates.up())
                        dve.wait_ge(unit_done, units.up())
                        did(nc.vector.tensor_tensor(gate_s[:, cols(g)], gate_s[:, cols(g)], bank[g][:, 0:GW], ALU.mult))
                        hv = h[:, bass.ds(n, 1), cols(g)].rearrange("p o t -> p (o t)")
                        nc.vector.tensor_tensor(hv, hv, gate_s[:, cols(g)], ALU.add).then_inc(unit_free, 1)

            tiles = Count()

            def stage_tiles(scale):
                for i in turns(dve, KT // 2, 1, un=(units, 2 * G), ti=(tiles, 2)):
                    for s in range(2):
                        t = tiles.up()
                        for g in range(G):
                            dve.wait_ge(unit_done, units.up())
                            if g == 0:
                                wait(dve, stg_out[s], ((tiles.n - 1) // 2) * 16 + tiles.off * 8)
                            nc.vector.scalar_tensor_tensor(stage[:, s, cols(g)], bank[g][:, 0:GW], scale,
                                                           rstd[:, cols(g)], ALU.mult, ALU.mult).then_inc(unit_free, 1)

            ffn(G_FFN0)
            ple(G_PLE0)
            norm(G_KV)
            stage_tiles(1.0)
            stage_tiles(1.0)
            norm(G_MIX1)
            stage_tiles(HD ** -0.5)
            assert units.n == U_Q

            zs, sps, ats, his_o = [Count() for _ in range(4)]
            las, pats = Count(), Count()
            dve.wait_ge(maskd, 1)
            for j in turns(dve, PAIRS, 1, own=(own, 48), zs=(zs, 16), sp=(sps, 16), at=(ats, 16),
                                                 hi=(his_o, 8)):
                for it in range(21):
                    if it < 16:
                        L = P * (it // 2 + 1)
                        z = psum[:, 2 * (it % 2):2 * (it % 2) + 2, :].rearrange("p a b -> p (a b)")[:, 0:L]
                        dve.wait_ge(pe_z, zs.up())
                        nc.vector.tensor_scalar(lbuf[:, it % 2, 0:L], z, biasB[:, bass.ds(2 * j + it % 2, 1)], 30.0,
                                                ALU.add, ALU.min).then_inc(min_done, 1)
                    if 1 <= it < 17:
                        n = it - 1
                        L = P * (n // 2 + 1)
                        z = psum[:, 2 * (n % 2):2 * (n % 2) + 2, :].rearrange("p a b -> p (a b)")[:, 0:L]
                        bias = biasB[:, bass.ds(2 * j + n % 2, 1)]
                        spn = spb[:, n % 2, 0:L]
                        diag = spb[:, n % 2, L - P:L]
                        dve.wait_ge(sp_in, sps.up())
                        wait(dve, pe_at, sps.at() - 2)
                        did(nc.vector.scalar_tensor_tensor(spn, z, bias, lbuf[:, n % 2, 0:L], ALU.add, ALU.max))
                        did(nc.vector.tensor_tensor(diag, diag, tri_le, ALU.mult))
                        did(nc.vector.tensor_tensor_scan(tb_[:, 0:L][:, ::-1], spn[:, ::-1], spn[:, ::-1], 0.0,
                                                         ALU.add, ALU.bypass))
                        nc.vector.scalar_tensor_tensor(spn, z, bias, tb_[:, 0:L], ALU.add, ALU.subtract)\
                            .then_inc(la_mid, 1)
                        dve.wait_ge(la_mid, sps.at())
                        nc.vector.tensor_tensor(diag, diag, lim, ALU.min).then_inc(la_done, 1)
                    if 2 <= it < 18:
                        L = P * ((it - 2) // 2 + 1)
                        i = ats.up()
                        dve.wait_ge(pe_at, i)
                        wait(dve, pe_av, i - 1)
                        nc.vector.tensor_copy(aT[:, 0:L], psum[:, 4:6, :].rearrange("p a b -> p (a b)")[:, 0:L])\
                            .then_inc(at_done, 1)
                    if 4 <= it < 20 and it % 2 == 1:
                        qt = (it - 4) // 2
                        dve.wait_ge(o_hi, his_o.up())
                        xs = slice(qt * P, (qt + 1) * P)
                        nc.vector.tensor_tensor(xl[:, bass.ds(j, 1), xs],
                                                bank[7][:, P:2 * P].rearrange("p (o c) -> p o c", o=1),
                                                flat(xh[:, bass.ds(j, 1), xs]), ALU.subtract).then_inc(o_lo, 1)

            dve.wait_ge(work_free, 1)
            dve.wait_ge(q_in, 48)
            for hh in range(2):
                r = slice(hh * HD, (hh + 1) * HD)
                nc.vector.tensor_copy(qblk[r, :, :, hh * QS:(hh + 1) * QS],
                                      qs_[r, :, :].rearrange("p j (b q) -> p j b q", b=NB))
            nc.vector.tensor_copy(bcol.rearrange("p (h q) -> p h q", q=QS),
                                  biasB[:, :].rearrange("p (h o) -> p h o", o=1).broadcast_to([P, HEADS_B, QS]))\
                .then_inc(qblk_done, 1)
            dve.wait_ge(qblk_done, 1)
            seqs = Count()
            new = slice(0, TS)

            with dve.Fori(0, NB) as b, looped(b, NB, own=(own, 14), se=(seqs, 1)):
                i = seqs.up()
                dve.wait_ge(sz_done, i)
                nc.vector.tensor_tensor(szx[:, 0:NPG, :], bank[0].rearrange("p (g c) -> p g c", g=NPG),
                                        bcol.rearrange("p (o c) -> p o c", o=1).broadcast_to([P, NPG, 64]), ALU.add)
                did(nc.vector.tensor_tensor(szx[new, NPG, :], bank[1][new, 0:64], bcol[new, :], ALU.add))
                nc.vector.tensor_scalar(szl[:, 0:NPG, :], szx[:, 0:NPG, :], 30.0, None, ALU.min)
                nc.vector.tensor_scalar(szl[new, NPG, :], szx[new, NPG, :], 30.0, None, ALU.min).then_inc(sx_done, 1)
                dve.wait_ge(sl_done, i)
                nc.vector.tensor_tensor(ssp[:, 0:NPG, :], szx[:, 0:NPG, :], szl[:, 0:NPG, :], ALU.max)
                did(nc.vector.tensor_tensor(ssp[new, NPG, :], szx[new, NPG, :], szl[new, NPG, :], ALU.max))
                mb = mnew[new, bass.ds(b * QS, QS)].rearrange("p (o q) -> p o q", o=1).broadcast_to([TS, HEADS_B, QS])
                lm = lnew[new, bass.ds(b * QS, QS)].rearrange("p (o q) -> p o q", o=1).broadcast_to([TS, HEADS_B, QS])
                sn = ssp[new, NPG, :].rearrange("p (h q) -> p h q", q=QS)
                did(nc.vector.tensor_tensor(sn, sn, mb, ALU.mult))
                did(nc.vector.memset(suf[:, NPG - 1, :], 0.0))
                for pg in range(NPG - 2, -1, -1):
                    ins = nc.vector.tensor_tensor(suf[:, pg, :], suf[:, pg + 1, :], ssp[:, pg + 1, :], ALU.add)
                    did(ins)
                dve.sem_inc(ssp_done, 1)
                dve.wait_ge(stail, i)
                nc.vector.tensor_tensor(sa[:, 0:NPG, :], szx[:, 0:NPG, :], bank[2].rearrange("p (g c) -> p g c", g=NPG),
                                        ALU.subtract)
                did(nc.vector.tensor_tensor(sa[new, NPG, :], szx[new, NPG, :], bank[3][new, 0:64], ALU.subtract))
                an = sa[new, NPG, :].rearrange("p (h q) -> p h q", q=QS)
                nc.vector.tensor_tensor(an, an, lm, ALU.min).then_inc(sla, 1)
                dve.wait_ge(sav, i)
                ov = bank[4][:, 0:64].rearrange("p (j e q) -> p j e q", e=2, q=QS)
                for hh in range(2):
                    r = slice(hh * HD, (hh + 1) * HD)
                    did(nc.vector.tensor_copy(xh[r, :, bass.ds(b * QS + TP, QS)], ov[r, :, hh, :]))
                for hh in range(2):
                    r = slice(hh * HD, (hh + 1) * HD)
                    last = nc.vector.tensor_tensor(xl[r, :, bass.ds(b * QS + TP, QS)], ov[r, :, hh, :],
                                                   flat(xh[r, :, bass.ds(b * QS + TP, QS)]), ALU.subtract)
                last.then_inc(so_done, 1)

            for n in range(KT):
                add_to_h(n)
            ffn(G_FFN1)
            ple(G_PLE1)
            norm(None)
            for k in range(KT):
                nc.vector.scalar_tensor_tensor(h[:, k, :], h[:, k, :], gain[:, G_FIN, k:k + 1], rstd[:, :],
                                               ALU.mult, ALU.mult).then_inc(y_done, 1)

        @block.tensor
        def _(pe):
            slabs, units, xs, norms = Count(), Count(), Count(), Count()
            mm = nc.tensor.matmul

            def slab():
                pe.wait_ge(w_ready, slabs.up())
                return (slabs.n - 1) % 2

            def unit_start():
                wait(pe, unit_free, units.up() - G)

            def exact(out, slot, tile, mh, ml, first, last):
                ws = slice(tile * P, (tile + 1) * P)
                mm(out, wh[:, slot, ws], mh, start=first, stop=False)
                mm(out, wh[:, slot, ws], ml, start=False, stop=False)
                return mm(out, wl[:, slot, ws], mh, start=False, stop=last)

            def product_x(n_tiles_k=KT):
                slot = slab()
                for g in range(G):
                    unit_start()
                    for k in range(KT):
                        last = exact(bank[g][:, 0:GW], slot, k, xh[:, k, cols(g)], xl[:, k, cols(g)], k == 0, k == KT - 1)
                    last.then_inc(unit_done, 1)
                release()

            def release():
                pe.wait_ge(unit_done, units.at())
                pe.sem_inc(w_used, 1)

            def product_a(slot, tile, buf, first=True, last=True):
                for g in range(G):
                    unit_start()
                    exact(bank[g][:, 0:GW], slot, tile, ah[:, buf, cols(g)], al[:, buf, cols(g)], True, True)\
                        .then_inc(unit_done, 1)

            def norm(x=True):
                for g in range(G):
                    pe.wait_ge(ssq_done, norms.up())
                    mm(bank[4 + g][:, 0:GW], ones[:, :], ssq[:, g, :], start=True, stop=True).then_inc(nsum_done, 1)
                if x:
                    pe.wait_ge(x_ready, xs.up(G * KT))

            pe.wait_ge(s_const, 5)
            norm()

            groups, levs, kts, us, outs, heads, sds, ons, vts, atts, osqs, vtk = [Count() for _ in range(12)]
            osum = Count()

            def level_scores(c):
                ts = slice(c % 2 * P, c % 2 * P + P)
                for half, bk in ((0, 3), (1, 4)):
                    wait(pe, lev_free, levs.up() - 2)
                    for l in range(3 * half, 3 * half + 3):
                        lhs, rhs = (X[:, l, ts], X[:, l, ts]) if l < NL else (X[:, XK, ts], X[:, XQ, ts])
                        last = mm(bank[bk][:, (l % 3) * P:(l % 3 + 1) * P], lhs, rhs, start=True, stop=True)
                    last.then_inc(pe_lev, 1)

            def keys_transposed(c, rows):
                at = c % 2 * P
                i = kts.up()
                wait(pe, kd_tok, i - 1)
                nc.tensor.transpose(bank[5][0:rows, 0:P], X[:, XKD, at:at + rows], ident[:, :]).then_inc(pe_kt, 1)

            def tile_output(c):
                at = c % 2 * P
                pe.wait_ge(kd_tok, us.up())
                pe.wait_ge(s_done, sds.up())
                mm(bank[6][:, 0:P], kdt[:, :], vtok[:, c, :], start=True, stop=True).then_inc(pe_u, 1)
                pe.wait_ge(att_done, atts.up())
                wait(pe, o_copied, outs.up() - 1)
                wait(pe, orstd_done, osqs.at())
                o = bank[7][:, at:at + P]
                mm(o, S, X[:, XQD, at:at + P], start=True, stop=False)
                mm(o, vtok[:, c, :], att[:, :], start=False, stop=True).then_inc(pe_o, 1)

            def output_sums(width):
                pe.wait_ge(osq_done, osqs.up())
                wait(pe, orstd_done, osqs.at() - 1)
                mm(bank[7][:, GRP:GRP + width], ones[:, :], prod.rearrange("p l t -> p (l t)")[:, 0:width],
                   start=True, stop=True).then_inc(pe_osum, 1)

            def v_transposed():
                pe.wait_ge(unit_free, units.at())
                for c in range(TILES_A + 1):
                    rows = P if c < TILES_A else TS
                    wait(pe, v_tok_done, vtk.up() - 2)
                    nc.tensor.transpose(bank[5 + c % 2][0:rows, 0:P], tv[:, c * P:c * P + rows], ident[:, :])\
                        .then_inc(pe_vt, 1)

            def mix(ahead):
                if ahead:
                    product_x()
                pe.wait_ge(v_tok_done, vts.up(9))
                for g in range(TP // GRP):
                    pe.wait_ge(xg_ready, groups.up())
                    c = 2 * g
                    level_scores(c)
                    keys_transposed(c, P)
                    level_scores(c + 1)
                    tile_output(c)
                    keys_transposed(c + 1, P)
                    tile_output(c + 1)
                    output_sums(GRP)
                    if g == 0 and ahead:
                        product_x()
                pe.wait_ge(xg_ready, groups.up())
                sds.up(2)
                pe.wait_ge(s_done, sds.at() - 1)
                pe.wait_ge(lev_free, levs.up() - 1)
                mm(bank[4][0:TS, 0:TS], X[:, XK, 0:TS], X[:, XQ, 0:TS], start=True, stop=True).then_inc(pe_lev, 1)
                keys_transposed(0, TS)
                pe.wait_ge(att_done, atts.up())
                wait(pe, o_copied, outs.up() - 1)
                pe.wait_ge(orstd_done, osqs.at())
                pe.wait_ge(s0_in, heads.up() * 16)
                pe.wait_ge(kd_tok, us.up())
                o = bank[7]
                mm(o[:, 0:TS], vtok[0:TS, TILES_A, :], att[0:TS, 0:TS], start=True, stop=False)
                for b in range(NB):
                    last = mm(o[:, QS * b:QS * b + QS], S0[:, b, :], X[:, XQD, QS * b:QS * b + QS], start=False,
                              stop=(b == NB - 1))
                last.then_inc(pe_o, 1)
                mm(bank[3][:, :], kdt[0:TS, :], vb[:, 0:4, :], start=True, stop=True)
                mm(bank[4][:, :], kdt[0:TS, :], vb[:, 4:8, :], start=True, stop=True).then_inc(pe_u, 1)
                output_sums(TS)
                if ahead:
                    product_x()
                    product_x()
                    v_transposed()
                pe.wait_ge(on_done, ons.up(5))
                for half in range(2):
                    slot = slab()
                    for n in range(4):
                        product_a(slot, n, 0)
                    release()

            for _ in range(4):
                product_x()
            v_transposed()
            rounds = HEADS_A - 1
            for i in turns(
                    pe, rounds, 1, sl=(slabs, 6), un=(units, 36), gr=(groups, 5), le=(levs, 17), kt=(kts, 9), us=(us, 9),
                    ou=(outs, 9), he=(heads, 1), sd=(sds, 10), on=(ons, 5), vt=(vts, 9), at=(atts, 9), os=(osqs, 5),
                    vk=(vtk, 9)):
                mix(True)
            mix(False)

            ars = Count()

            def ffn():
                norm()
                with pe.Fori(0, FT // 2) as i, looped(i, FT // 2, sl=(slabs, 6), un=(units, 60), ar=(ars, 6)):
                    for _ in range(4):
                        product_x()
                    for buf in range(2):
                        slot = slab()
                        pe.wait_ge(a_ready, ars.up(3))
                        for n in range(KT):
                            product_a(slot, n, buf)
                        release()

            def ple():
                norm()
                pe.wait_ge(a_ready, ars.up())
                with pe.Fori(0, KT) as i, looped(i, KT, sl=(slabs, 2), un=(units, 6)):
                    product_x()
                    slot = slab()
                    for g in range(G):
                        unit_start()
                        for k in range(PK):
                            last = exact(bank[g][:, 0:GW], slot, k, ah[:, k, cols(g)], al[:, k, cols(g)], k == 0,
                                         k == PK - 1)
                        last.then_inc(unit_done, 1)
                    release()

            def products(n):
                with pe.Fori(0, n // 2) as i, looped(i, n // 2, sl=(slabs, 2), un=(units, 6)):
                    product_x()
                    product_x()

            ffn()
            ple()
            norm()
            products(16)
            norm()
            products(KT)
            assert units.n == U_Q and slabs.n == BEFORE

            pairs, v8s, zs, ats, avs, ots, v8w = [Count() for _ in range(7)]
            pe.wait_ge(unit_free, units.at())
            for j in turns(pe, PAIRS, 1, pa=(pairs, 1), v8=(v8s, 8), zs=(zs, 16), at=(ats, 16),
                                                av=(avs, 16), ot=(ots, 8), vw=(v8w, 8)):
                pe.wait_ge(pair_in, pairs.up() * 48)
                wait(pe, o_lo, (pairs.at() - 1) * 8)
                for c in range(8):
                    wait(pe, v8_done, v8s.up() - 2)
                    nc.tensor.transpose(bank[6 + c % 2][:, 0:P], vc[:, c * P:(c + 1) * P], ident[:, :]).then_inc(pe_v8, 1)
                for it in range(20):
                    if it < 16:
                        qt, hh = it // 2, it % 2
                        L = P * (qt + 1)
                        r = slice(hh * HD, (hh + 1) * HD)
                        wait(pe, la_done, zs.up() - 2)
                        for half in range(-(-L // 512)):
                            n = min(512, L - 512 * half)
                            last = mm(bank[2 * hh + half][:, 0:n], qc[r, qt * P:(qt + 1) * P],
                                      kc[r, 512 * half:512 * half + n], start=True, stop=True)
                        last.then_inc(pe_z, 1)
                    if 2 <= it < 18:
                        n = it - 2
                        qt, hh = n // 2, n % 2
                        i = ats.up()
                        pe.wait_ge(aexp, i)
                        wait(pe, at_done, i - 1)
                        for c in range(qt + 1):
                            last = nc.tensor.transpose(bank[4 + c // 4][:, c % 4 * P:(c % 4 + 1) * P],
                                                       spb[:, n % 2, c * P:(c + 1) * P], ident[:, :])
                        last.then_inc(pe_at, 1)
                        if n == 0:
                            pe.wait_ge(v8_done, v8w.up(8))
                        pe.wait_ge(at_done, i)
                        wait(pe, av_done, avs.up() - 1)
                        for c in range(qt + 1):
                            last = mm(bank[6][:, hh * HD:(hh + 1) * HD], aT[:, c * P:(c + 1) * P],
                                      v8[:, c, hh * HD:(hh + 1) * HD], start=(c == 0), stop=(c == qt))
                        last.then_inc(pe_av, 1)
                    if 3 <= it < 19 and (it - 3) % 2 == 1:
                        q = ots.up()
                        pe.wait_ge(av_done, avs.at() - (1 if it < 18 else 0))
                        wait(pe, o_lo, q - 1)
                        nc.tensor.transpose(bank[7][:, P:2 * P], o_t, ident[:, :]).then_inc(pe_ot, 1)
                pe.wait_ge(pe_av, avs.at())
                pe.sem_inc(pair_free, 1)

            pe.wait_ge(work_free, 1)
            pe.wait_ge(q_in, 48)
            pe.wait_ge(qblk_done, 1)
            for j in range(PAIRS):
                last = nc.tensor.transpose(bank[6 + j // 4][0:TS, j % 4 * P:(j % 4 + 1) * P], vnT[:, j, :], ident[:, :])
                if j % 4 == 3:
                    last.then_inc(pe_vn, 1)
            pe.wait_ge(vn_done, 2)
            with pe.Fori(0, NB) as b:
                for pg in range(NPG):
                    s = pg % 2
                    pe.wait_ge(pg_k[s], b * 64 + (pg // 2 + 1) * 16)
                    for j in range(PAIRS):
                        at = pg * 64 + j * 8
                        last = mm(bank[0][:, at:at + 8], kpg[:, s, j * P:(j + 1) * P],
                                  qblk[:, j, bass.ds(b, 1), :].rearrange("p o c -> p (o c)"), start=True, stop=True)
                    last.then_inc(kpg_free, 1)
                for j in range(PAIRS):
                    last = mm(bank[1][0:TS, j * 8:j * 8 + 8], kn[:, j, :],
                              qblk[:, j, bass.ds(b, 1), :].rearrange("p o c -> p (o c)"), start=True, stop=True)
                last.then_inc(sz_done, 1)
                pe.wait_ge(ssp_done, b + 1)
                tail = bank[2].rearrange("p (g c) -> p g c", g=NPG)
                mm(tail, triP, ssp[:, 0:NPG, :], start=True, stop=False)
                mm(tail, ones[:, :], suf, start=False, stop=False)
                mm(tail, ones[0:TS, :], ssp[0:TS, NPG:NPG + 1, :].broadcast_to([TS, NPG, 64]), start=False, stop=True)
                mm(bank[3][0:TS, 0:64], triP[0:TS, 0:TS], ssp[0:TS, NPG, :], start=True, stop=True).then_inc(stail, 1)
                pe.wait_ge(sexp, b + 1)
                mm(bank[4][:, 0:64], zer, sa[:, 0, :], start=True, stop=False)
                for pg in range(NPG):
                    s = pg % 2
                    pe.wait_ge(pg_v[s], b * 64 + (pg // 2 + 1) * 16)
                    for j in range(PAIRS):
                        last = mm(bank[4][:, j * 8:j * 8 + 8], vpg[:, s, j * P:(j + 1) * P], sa[:, pg, j * 8:j * 8 + 8],
                                  start=False, stop=False)
                    last.then_inc(vpg_free, 1)
                for j in range(PAIRS):
                    last = mm(bank[4][:, j * 8:j * 8 + 8], vn[0:TS, j * P:(j + 1) * P], sa[0:TS, NPG, j * 8:j * 8 + 8],
                              start=False, stop=(j == PAIRS - 1))
                last.then_inc(sav, 1)

            pe.wait_ge(o_lo, 8 * PAIRS)
            pe.wait_ge(so_done, NB)
            products(N_O)
            ffn()
            ple()
            norm(False)


def kernel(x_prompt, x_sample, p_prompt, p_sample, state_hgrn, cache_k, cache_v, page_table, a_lb, w_a_in,
           g_a_onorm, w_a_o, g_kv, w_kv, w_b_q, w_b_o, sb_bias, g_mix, g_ffn, w_ffn_in, w_ffn_out, g_ple,
           w_ple_in, w_ple_gate, g_final):
    import numpy as _np
    import concourse.bacc as _bacc
    from concourse import mybir as _mybir
    from concourse.bass_utils import run_bass_kernel_spmd as _run

    f32 = _np.float32
    A = lambda a: _np.asarray(a)

    def tall(wt, col):
        return A(wt)[:, col * P:(col + 1) * P].reshape(-1, P, P).transpose(1, 0, 2)

    def wide(wt, row, c0, c1):
        return A(wt)[row * P:(row + 1) * P, c0:c1].reshape(P, -1, P)

    stream = _np.zeros((NSLAB, P, 8, P), f32)
    at = [0]

    def put(s):
        stream[at[0], :, :s.shape[1], :] = s
        at[0] += 1

    wa, wo = A(w_a_in)[0], A(w_a_o)[0]

    def ffn(l):
        wi, wu = A(w_ffn_in)[l], A(w_ffn_out)[l]
        for c in range(0, FT, 2):
            for t in (c, c + 1):
                put(tall(wi, t))
                put(tall(wi, FT + t))
            for t in (c, c + 1):
                put(wide(wu, t, 0, D))

    def ple(l):
        for n in range(KT):
            put(tall(A(w_ple_gate)[l], n))
            put(tall(A(w_ple_in)[l], n))

    for part in range(4):
        put(tall(wa, part * KT))
    for hd in range(HEADS_A):
        if hd + 1 < HEADS_A:
            for part in range(4):
                put(tall(wa, part * KT + hd + 1))
        put(wide(wo, hd, 0, 512))
        put(wide(wo, hd, 512, 1024))
    ffn(0)
    ple(0)
    for n in range(16):
        put(tall(w_kv, n))
    for n in range(KT):
        put(tall(A(w_b_q)[0], n))
    for n in range(KT):
        put(tall(A(w_b_o)[0], n))
    ffn(1)
    ple(1)
    assert at[0] == NSLAB

    def tokens_T(prompt, sample):
        return _np.concatenate([A(prompt).reshape(TP, -1), A(sample).reshape(TS, -1)]).T

    xT = _np.ascontiguousarray(tokens_T(x_prompt, x_sample))
    pT = _np.stack([tokens_T(A(p_prompt)[l], A(p_sample)[l]).reshape(PK, P, T).transpose(1, 0, 2) for l in range(2)])
    cols_ = lambda v: A(v).reshape(KT, P).T
    gm, gf, gp = A(g_mix), A(g_ffn), A(g_ple)
    gains = _np.stack([cols_(v) for v in (gm[0], gf[0], gp[0], g_kv, gm[1], gf[1], gp[1], g_final)], axis=1)
    ins = {
        "wstream": stream.reshape(NSLAB, P, SLAB),
        "xT": xT,
        "pT": pT,
        "state": A(state_hgrn)[0].transpose(1, 2, 0, 3),
        "kT_cache": A(cache_k).reshape(POOLPG, P, PAIRS, P).transpose(0, 3, 2, 1).reshape(POOLPG, P, D),
        "v_cache": A(cache_v).reshape(POOLPG, P, D),
        "table": A(page_table).reshape(1, NB * NPG),
        "lbT": A(a_lb).reshape(2, KT, P).transpose(2, 0, 1),
        "gains": gains,
        "g_on": A(g_a_onorm).reshape(HEADS_A, P).T,
        "sb_bias": A(sb_bias).reshape(1, HEADS_B),
    }
    outs = {
        "yT": (D, T), "st_prompt": (HEADS_A, P, P), "st_sample": (HEADS_A, P, NB, P), "kT_out": (D, T), "vT_out": (D, T),
    }
    nc = _bacc.Bacc("TRN2", target_bir_lowering=False, num_devices=1)
    arrays, args = {}, {}
    for name, a in ins.items():
        a = _np.ascontiguousarray(a)
        arrays[f"in_{name}"] = a
        args[name] = nc.dram_tensor(f"in_{name}", a.shape, _mybir.dt.from_np(a.dtype), kind="ExternalInput").ap()
    for name, shape in outs.items():
        args[name] = nc.dram_tensor(f"out_{name}", shape, _mybir.dt.float32, kind="ExternalOutput").ap()
    yoco_step(nc, **args)
    r = _run(nc, [arrays], core_ids=[0]).results[0]
    y, kk, vv = (_np.asarray(r[f"out_{n}"]).T for n in ("yT", "kT_out", "vT_out"))
    stp, sts = _np.asarray(r["out_st_prompt"]), _np.asarray(r["out_st_sample"])

    def split(a, *tail):
        return (_np.ascontiguousarray(a[:TP]).reshape(1, TP, *tail), _np.ascontiguousarray(a[TP:]).reshape(NB, QS, *tail))

    yp, ys = split(y, D)
    kp, ks = split(kk, HEADS_B, HD)
    vp, vs = split(vv, HEADS_B, HD)
    return (yp, ys, stp.reshape(1, 1, HEADS_A, P, P), _np.ascontiguousarray(sts.transpose(2, 0, 1, 3))[None],
            kp, vp, ks, vs)
```

```python
from contextlib import ExitStack, contextmanager

import numpy as np

import concourse.bass as bass
from concourse import mybir

F32 = mybir.dt.float32
F32R = mybir.dt.float32r
BF16 = mybir.dt.bfloat16
I32 = mybir.dt.int32
ALU = mybir.AluOpType
ACT = mybir.ActivationFunctionType
AX_X = mybir.AxisListType.X

P = 128
D = 1024
KT = D // P
TP = 1024
NB, QS = 8, 4
TS = NB * QS
T = TP + TS
G = 3
GW = T // G
FF = 2816
FT = FF // P
PLE = 256
PK = PLE // P
HEADS_A = 8
HEADS_B = 16
PAIRS = HEADS_B // 2
HD = 64
NPG = 8
POOLPG = 80
EPS = 1e-6
SLAB = 8 * P
TILES_A = TP // P
LN_FLOOR = 7.6e-10
HALVES = (64, 32, 16, 8, 4)
NL = len(HALVES)
XQ, XK, XQD, XKD = NL, NL + 1, NL + 2, NL + 3
NX = NL + 4
GRP = 256
BIG = 1e30
KRING = 4
VRING = 4

N_A = HEADS_A * 6
N_F = FT * 3
N_P = KT * 2
N_KV = 16
N_Q = 8
N_O = 8
BEFORE = N_A + N_F + N_P + N_KV + N_Q
NSLAB = BEFORE + N_O + N_F + N_P

STEPS = 20
PAGE_STEPS = {0: (0, 1), 1: (2, 3), 3: (4, 5), 4: (6, 7)}
SX_STEP = 5
SL_STEP = 9
SA_STEP = 10
SOWN = 5


class Count:

    def __init__(self):
        self.n = 0
        self.off = 0

    def up(self, k=1):
        self.n += k
        return self.n + self.off

    def at(self):
        return self.n + self.off


@contextmanager
def looped(i, reps, **counts):
    for c, k in counts.values():
        c.off = i * k
    start = {n: c.n for n, (c, k) in counts.items()}
    yield
    for n, (c, k) in counts.items():
        assert c.n - start[n] == k, (n, c.n - start[n], k)
        c.n = start[n] + k * reps
        c.off = 0


def turns(eng, reps, peel, **counts):
    for t in range(peel):
        yield t
    with eng.Fori(peel, reps) as i, looped(i - peel, reps - peel, **counts):
        yield i


def wait(eng, sem, value):
    if isinstance(value, int) and value <= 0:
        return
    eng.wait_ge(sem, value)


def yoco_step(nc, wstream, xT, pT, state, kT_cache, v_cache, table, lbT, gains, g_on, sb_bias,
              yT, st_prompt, st_sample, kT_out, vT_out):
    with ExitStack() as ctx:
        def sb(name, shape, dt=F32):
            return ctx.enter_context(nc.sbuf_tensor(name, shape, dt))

        def sem(name):
            return ctx.enter_context(nc.semaphore(name))

        h_scratch = nc.dram_tensor("h_scratch", [P, KT, T], F32, kind="Internal").ap()
        qT_scratch = nc.dram_tensor("qT_scratch", [D, T], F32, kind="Internal").ap()

        psum = ctx.enter_context(nc.psum_tensor("psum", [P, 8, 512], F32))
        bank = [psum[:, i, :] for i in range(8)]

        h = sb("h", [P, KT, T])
        xh = sb("xh", [P, KT, T], F32R)
        xl = sb("xl", [P, KT, T], F32R)
        raw = sb("raw", [P, 2, SLAB])
        wh = sb("wh", [P, 2, SLAB], F32R)
        wl = sb("wl", [P, 2, SLAB], F32R)
        ah = sb("ah", [P, 2, T], F32R)
        al = sb("al", [P, 2, T], F32R)
        rstd = sb("rstd", [P, T])
        ident = sb("ident", [P, P])
        ones = sb("ones", [P, P])
        gain = sb("gain", [P, 8, KT])
        gon = sb("gon", [P, HEADS_A])
        lbr = sb("lbr", [P, 2, KT])
        lb = sb("lb", [P, KT])
        omlb = sb("omlb", [P, KT])
        biasB = sb("biasB", [P, HEADS_B])
        c_eps = sb("c_eps", [P, 1])
        c_one = sb("c_one", [P, 1])
        c_epsv = sb("c_epsv", [P, 1])
        WORK = 12900
        work = sb("work", [P, WORK])

        class Carve:
            def __init__(self, place=None, size=WORK):
                self.at, self.place, self.size = 0, work if place is None else place, size

            def take(self, *shape):
                n = int(np.prod(shape))
                v = self.place[:, self.at:self.at + n]
                self.at += n
                assert self.at <= self.size, (self.at, self.size)
                if len(shape) == 2:
                    return v.rearrange("p (a b) -> p a b", a=shape[0])
                if len(shape) == 3:
                    return v.rearrange("p (a b c) -> p a b c", a=shape[0], b=shape[1])
                return v

        s_const = sem("s_const")
        s_cload = sem("s_cload")
        s_xload = sem("s_xload")
        landed = [sem("landed0"), sem("landed1")]
        split_go = sem("split_go")
        split_hi = sem("split_hi")
        w_ready = sem("w_ready")
        w_used = sem("w_used")
        unit_done = sem("unit_done")
        unit_free = sem("unit_free")
        xh_done = sem("xh_done")
        x_ready = sem("x_ready")
        sq_done = sem("sq_done")
        ssq_done = sem("ssq_done")
        nsum_done = sem("nsum_done")
        rstd_done = sem("rstd_done")
        dself = sem("dself")
        aself = sem("aself")
        act_in = sem("act_in")
        fg_done = sem("fg_done")
        g_done = sem("g_done")
        d_done = sem("d_done")
        e_done = sem("e_done")
        xg_ready = sem("xg_ready")
        pe_lev = sem("pe_lev")
        lev_free = sem("lev_free")
        att_done = sem("att_done")
        pe_kt = sem("pe_kt")
        kd_tok = sem("kd_tok")
        pe_u = sem("pe_u")
        s_done = sem("s_done")
        pe_o = sem("pe_o")
        o_copied = sem("o_copied")
        osq_done = sem("osq_done")
        pe_osum = sem("pe_osum")
        orstd_done = sem("orstd_done")
        on_done = sem("on_done")
        pe_vt = sem("pe_vt")
        v_tok_done = sem("v_tok_done")
        s0_in = sem("s0_in")
        s_out = sem("s_out")
        gate_act = sem("gate_act")
        a_prod = sem("a_prod")
        a_hi = sem("a_hi")
        a_ready = sem("a_ready")
        p_in = sem("p_in")
        stg_out = [sem("stg_out0"), sem("stg_out1")]
        y_done = sem("y_done")
        y_out = sem("y_out")
        h_away = sem("h_away")
        h_back = [sem(f"h_back{k}") for k in range(KT)]
        pair_in = sem("pair_in")
        pe_v8 = sem("pe_v8")
        v8_done = sem("v8_done")
        pe_z = sem("pe_z")
        min_done = sem("min_done")
        sp_in = sem("sp_in")
        la_done = sem("la_done")
        aexp = sem("aexp")
        pe_at = sem("pe_at")
        at_act = sem("at_act")
        at_dve = sem("at_dve")
        pe_av = sem("pe_av")
        av_done = sem("av_done")
        pe_ot = sem("pe_ot")
        o_hi = sem("o_hi")
        o_lo = sem("o_lo")
        maskd = sem("maskd")
        tb_in = sem("tb_in")
        q_in = sem("q_in")
        pg_k = [sem(f"pg_k{i}") for i in range(KRING)]
        pg_v = [sem(f"pg_v{i}") for i in range(VRING)]
        kpg_free = sem("kpg_free")
        vpg_free = sem("vpg_free")
        qblk_done = sem("qblk_done")
        pe_vn = sem("pe_vn")
        vn_done = sem("vn_done")
        sz_done = sem("sz_done")
        sx_done = sem("sx_done")
        sl_exp = sem("sl_exp")
        sl_done = sem("sl_done")
        suf_step = sem("suf_step")
        stail = sem("stail")
        sla = sem("sla")
        sexp = sem("sexp")
        sav = sem("sav")
        so_done = sem("so_done")

        w = Carve()
        tq, tf = w.take(T), w.take(T)
        qa, ka, ga = w.take(T), w.take(T), w.take(T)
        og = w.take(T)
        X = w.take(NX, GRP)
        tv = X.rearrange("p a b -> p (a b)")[:, 0:T]
        vb = X.rearrange("p a b -> p (a b)")[0:TS, 0:NB * P].rearrange("p (a b) -> p a b", a=NB)
        vtok = w.take(TILES_A + 1, P)
        kdt = w.take(P)
        prod = w.take(6, P)
        att = w.take(P)
        o_s, orst = w.take(GRP), w.take(GRP)
        S = w.take(P)
        S0 = w.take(NB, P)
        dec = w.take(16)
        bmask = w.take(NB)
        maskA = sb("maskA", [P, NL + 1, P], BF16)
        reset = sb("reset", [P, T], BF16)
        w = Carve()
        sq = w.take(KT, GW)
        ssq = w.take(G, GW)
        gate_s = w.take(T)
        up_s = w.take(T)
        praw = w.take(PK, T)
        stage = w.take(2, T)
        w = Carve()
        qc, kc, vc = w.take(TP), w.take(TP), w.take(TP)
        v8 = w.take(KT, P)
        wt = w.take(3, TP)
        tb_ = w.take(TP)
        aT = w.take(TP)
        o_t = w.take(KT, P)
        negm = w.take(P)
        triP = w.take(P)
        mnew = w.take(TS)
        lnew = w.take(TS)
        bcol = w.take(PAIRS * 2 * QS)
        zer = w.take(P)
        suf = w.take(NPG, 64)
        szx = w.take(NPG + 1, 64)
        hw = Carve(h[:, :, :].rearrange("p k t -> p (k t)"), KT * T)
        kpg = hw.take(KRING, D)
        ssp = hw.take(NPG + 1, 64)
        szl = hw.take(NPG + 1, 64)
        vpg = hw.take(VRING - 1, D)
        vlast = w.take(D)
        qblk = sb("qblk", [P, PAIRS, NB, 2 * QS])
        vn = sb("vn", [TS, D])
        qs_, _, vnT = [tb_[:, i * PAIRS * TS:(i + 1) * PAIRS * TS].rearrange("p (a b) -> p a b", a=PAIRS)
                         for i in range(3)]
        kn = sb("kn", [P, PAIRS, TS])
        tbl = sb("tbl", [1, NB * NPG], I32)

        U_A = HEADS_A * 36
        U_F0 = U_A + FT * 30
        U_P0 = U_F0 + KT * 6
        U_KV = U_P0 + 16 * G
        U_Q = U_KV + KT * G
        U_O = U_Q + KT * G
        U_F1 = U_O + FT * 30
        U_P1 = U_F1 + KT * 6
        G_MIX0, G_FFN0, G_PLE0, G_KV, G_MIX1, G_FFN1, G_PLE1, G_FIN = range(8)

        def cols(g):
            return slice(g * GW, (g + 1) * GW)

        def flat(ap):
            return ap.bitcast(F32)

        def vslot(s):
            return vpg[:, s, :] if s < VRING - 1 else vlast

        block = ctx.enter_context(nc.Block())

        @block.sync
        def _(sp):
            sp.dma_start(h[:, :, :], xT.rearrange("(k p) t -> p k t", p=P)).then_inc(s_xload, 16)
            n = Count()

            def load_slab(slot):
                i = n.up()
                wait(sp, w_ready, i - 2)
                src = wstream[bass.ds(i - 1, 1), :, :].rearrange("o p c -> (o p) c")
                sp.dma_start(raw[:, slot, :], src).then_inc(landed[slot], 16)

            load_slab(0)
            load_slab(1)
            with sp.Fori(0, BEFORE // 2 - 1) as i, looped(i, BEFORE // 2 - 1, n=(n, 2)):
                load_slab(0)
                load_slab(1)
            sp.wait_ge(rstd_done, 4 * G)
            sp.wait_ge(x_ready, 4 * G * KT)
            sp.wait_ge(xh_done, 4 * G * KT)
            sp.dma_start(h_scratch, h[:, :, :]).then_inc(h_away, 16)
            sp.dma_start(tbl[0:1, :], table).then_inc(tb_in, 16)
            sp.wait_ge(stg_out[0], 16 * 12)
            sp.wait_ge(stg_out[1], 16 * 12)
            for dst, src in ((qs_, qT_scratch), (kn[:, :, :], kT_out), (vnT, vT_out)):
                sp.dma_start(dst, src.rearrange("(j p) t -> p j t", p=P)[:, :, TP:T]).then_inc(q_in, 16)
            sp.wait_ge(h_away, 16)
            sp.wait_ge(tb_in, 16)

            def page(kind, m, p):
                ring, free, came, dst, src = ((KRING, kpg_free, pg_k, kpg, kT_cache) if kind == "k" else
                                              (VRING, vpg_free, pg_v, vpg, v_cache))
                phys = sp.value_load(tbl[0:1, bass.ds(m, 1)], min_val=0, max_val=POOLPG - 1)
                wait(sp, free, m - ring + 1)
                sp.dma_start(vslot(p % ring) if kind == "v" else dst[:, p % ring, :],
                             src[bass.ds(phys, 1), :, :].rearrange("o p c -> (o p) c")).then_inc(came[p % ring], 16)

            for m in range(KRING):
                page("k", m, m)
            for j in turns(sp, PAIRS - 1, 1):
                wait(sp, pe_z, j * 16)
                for dst, src in ((qc, qT_scratch), (kc, kT_out), (vc, vT_out)):
                    sp.dma_start(dst, src[bass.ds(j * P, P), 0:TP]).then_inc(pair_in, 16)
                for m in range(KRING, NPG):
                    page("k", j * NPG + m, m)
                for m in range(NPG):
                    page("v", j * NPG + m, m)
                for m in range(NPG, NPG + KRING):
                    page("k", j * NPG + m, m)
            j = PAIRS - 1
            sp.wait_ge(pe_z, j * 16)
            for dst, src in ((qc, qT_scratch), (kc, kT_out), (vc, vT_out)):
                sp.dma_start(dst, src[bass.ds(j * P, P), 0:TP]).then_inc(pair_in, 16)
            for m in range(KRING, NPG):
                page("k", j * NPG + m, m)
            for m in range(NPG):
                page("v", j * NPG + m, m)
            sp.wait_ge(sav, NB)
            for k in range(KT):
                sp.dma_start(h[:, k, :], h_scratch[:, k, :]).then_inc(h_back[k], 16)
            rest = (NSLAB - BEFORE) // 2
            with sp.Fori(0, rest) as i, looped(i, rest, n=(n, 2)):
                load_slab(0)
                load_slab(1)
            sp.wait_ge(y_done, KT)
            sp.dma_start(yT.rearrange("(k p) t -> p k t", p=P), h[:, :, :]).then_inc(y_out, 16)
            sp.wait_ge(y_out, 16)

        @block.gpsimd
        def _(pool):
            own = Count()

            def did(ins):
                ins.then_inc(s_const, 1)
                pool.wait_ge(s_const, own.up())

            did(nc.gpsimd.memset(ident[:, :], 0.0))
            did(nc.gpsimd.affine_select(out=ident[:, :], in_=ident[:, :], compare_op=ALU.not_equal, fill=1.0,
                                        base=0, pattern=[[-1, P]], channel_multiplier=1))
            did(nc.gpsimd.memset(ones[:, :], 1.0))
            did(nc.gpsimd.memset(c_eps[:, :], EPS))
            did(nc.gpsimd.memset(c_one[:, :], 1.0))
            did(nc.gpsimd.memset(c_epsv[:, :], 30.0))
            did(nc.gpsimd.memset(maskA[:, :, :], 1.0))
            for l, hf in enumerate(HALVES):
                nb = P // (2 * hf)
                m = maskA[:, l, :].rearrange("p (b r) -> p b r", b=nb)
                did(nc.gpsimd.affine_select(out=m, in_=m, compare_op=ALU.is_ge, fill=0.0, base=0,
                                            pattern=[[-2 * hf, nb], [0, 2 * hf]], channel_multiplier=1))
                did(nc.gpsimd.affine_select(out=m, in_=m, compare_op=ALU.is_ge, fill=0.0, base=hf - 1,
                                            pattern=[[2 * hf, nb], [0, 2 * hf]], channel_multiplier=-1))
                did(nc.gpsimd.memset(m[:, :, 0:hf], 0.0))
            m = maskA[:, NL, :].rearrange("p (b r) -> p b r", r=4)
            did(nc.gpsimd.affine_select(out=m, in_=m, compare_op=ALU.is_ge, fill=0.0, base=0,
                                        pattern=[[-4, P // 4], [0, 4]], channel_multiplier=1))
            did(nc.gpsimd.affine_select(out=m, in_=m, compare_op=ALU.is_ge, fill=0.0, base=0,
                                        pattern=[[4, P // 4], [1, 4]], channel_multiplier=-1))
            did(nc.gpsimd.memset(reset[:, :], 1.0))
            did(nc.gpsimd.memset(reset[:, 0:TP:P], 0.0))
            did(nc.gpsimd.memset(reset[:, TP:T:QS], 0.0))
            did(nc.gpsimd.memset(bmask, 1.0))
            did(nc.gpsimd.affine_select(out=bmask, in_=bmask, compare_op=ALU.is_ge, fill=0.0, base=0,
                                        pattern=[[-QS, NB]], channel_multiplier=1))
            did(nc.gpsimd.affine_select(out=bmask, in_=bmask, compare_op=ALU.is_ge, fill=0.0, base=QS - 1,
                                        pattern=[[QS, NB]], channel_multiplier=-1))
            n = Count()

            def split(slot):
                i = n.up()
                arrived = ((n.n - 1) // 2 + 1) * 16 + n.off * 8
                pool.wait_ge(landed[slot], arrived)
                wait(pool, w_used, i - 1 if not isinstance(i, int) or i > 2 else 0)
                pool.sem_inc(split_go, 1)
                nc.gpsimd.tensor_copy(wh[:, slot, :], raw[:, slot, :]).then_inc(split_hi, 1)
                pool.wait_ge(split_hi, i)
                nc.gpsimd.tensor_tensor(wl[:, slot, :], raw[:, slot, :], flat(wh[:, slot, :]), ALU.subtract)\
                    .then_inc(w_ready, 1)

            split(0)
            split(1)
            pairs = BEFORE // 2 - 1
            with pool.Fori(0, pairs) as i, looped(i, pairs, n=(n, 2)):
                split(0)
                split(1)
            pool.wait_ge(stg_out[0], 16 * 12)
            pool.wait_ge(stg_out[1], 16 * 12)
            for m, val, fill, base in ((negm, 0.0, -BIG, -1), (triP, 1.0, 0.0, 0)):
                did(nc.gpsimd.memset(m, val))
                did(nc.gpsimd.affine_select(out=m, in_=m, compare_op=ALU.is_ge, fill=fill, base=base,
                                            pattern=[[-1, P]], channel_multiplier=1))
            for m, val, fill in ((mnew, 1.0, 0.0), (lnew, BIG, -BIG)):
                m3 = m.rearrange("p (b q) -> p b q", b=NB)
                did(nc.gpsimd.memset(m, val))
                did(nc.gpsimd.affine_select(out=m3, in_=m3, compare_op=ALU.is_ge, fill=fill, base=0,
                                            pattern=[[-QS, NB], [0, QS]], channel_multiplier=1))
                did(nc.gpsimd.affine_select(out=m3, in_=m3, compare_op=ALU.is_ge, fill=fill, base=-1,
                                            pattern=[[QS, NB], [1, QS]], channel_multiplier=-1))
            did(nc.gpsimd.memset(zer, 0.0))
            did(nc.gpsimd.memset(suf[:, NPG - 1, :], 0.0))
            did(nc.gpsimd.memset(qblk[:, :, :, :], 0.0))
            pool.sem_inc(maskd, 1)
            rest = (NSLAB - BEFORE) // 2
            with pool.Fori(0, rest) as i, looped(i, rest, n=(n, 2)):
                split(0)
                split(1)

        @block.scalar
        def _(act):
            own, sqs, nsums = Count(), Count(), Count()
            units = Count()

            def did(ins):
                ins.then_inc(aself, 1)
                act.wait_ge(aself, own.up())

            act.dma_start(gain[:, :, :], gains).then_inc(s_cload, 16)
            act.dma_start(gon[:, :], g_on).then_inc(s_cload, 16)
            act.dma_start(lbr[:, :, :], lbT).then_inc(s_cload, 16)
            act.dma_start(biasB[:, :], sb_bias.broadcast_to([P, HEADS_B])).then_inc(s_cload, 16)
            act.wait_ge(s_cload, 64)
            act.wait_ge(s_const, 5)
            act.wait_ge(dself, 1)
            did(nc.scalar.activation(omlb[:, :], lb[:, :], ACT.Sigmoid, scale=-1.0))
            did(nc.scalar.activation(lb[:, :], lb[:, :], ACT.Sigmoid))

            def norm(gi):
                for g in range(G):
                    for k in range(KT if gi is not None else 0):
                        nc.scalar.activation(xh[:, k, cols(g)], h[:, k, cols(g)], ACT.Copy,
                                             scale=gain[:, gi, k:k + 1]).then_inc(xh_done, 1)
                    i = sqs.up()
                    wait(act, ssq_done, i - 1)
                    nc.scalar.activation(sq, h[:, :, cols(g)], ACT.Square).then_inc(sq_done, 1)
                for g in range(G):
                    act.wait_ge(nsum_done, nsums.up())
                    did(nc.scalar.activation(rstd[:, cols(g)], bank[4 + g][:, 0:GW], ACT.Ln,
                                             bias=c_eps[:, 0:1], scale=1.0 / D))
                    nc.scalar.activation(rstd[:, cols(g)], rstd[:, cols(g)], ACT.Exp, scale=-0.5)\
                        .then_inc(rstd_done, 1)

            act.wait_ge(s_xload, 16)
            norm(G_MIX0)

            forget, decays, exponents, kts, outs, osums, vts, states, heads, vtoks, ons = [Count() for _ in range(11)]

            def group_exps(first, width):
                act.wait_ge(d_done, exponents.up())
                nc.scalar.activation(X[:, first:NX, 0:width], X[:, first:NX, 0:width], ACT.Exp).then_inc(e_done, 1)

            def tile_copies(rows, at, fresh):
                i = kts.up()
                act.wait_ge(pe_kt, i)
                wait(act, pe_u, i - 1)
                nc.scalar.activation(kdt[0:rows, :], bank[5][0:rows, 0:P], ACT.Copy).then_inc(kd_tok, 1)
                act.wait_ge(pe_o, outs.up())
                if fresh:
                    wait(act, on_done, ons.up() - 1)
                nc.scalar.activation(o_s[:, at:at + rows], bank[7][:, at:at + rows], ACT.Copy).then_inc(o_copied, 1)

            def output_rms(width):
                act.wait_ge(pe_osum, osums.up())
                did(nc.scalar.activation(orst[:, 0:width], bank[7][:, GRP:GRP + width], ACT.Ln,
                                         bias=c_eps[:, 0:1], scale=1.0 / P))
                nc.scalar.activation(orst[:, 0:width], orst[:, 0:width], ACT.Exp, scale=-0.5).then_inc(orstd_done, 1)

            def v_copies():
                for c in range(TILES_A + 1):
                    rows = P if c < TILES_A else TS
                    act.wait_ge(pe_vt, vts.up())
                    nc.scalar.activation(vtok[0:rows, c, :], bank[5 + c % 2][0:rows, 0:P], ACT.Copy)\
                        .then_inc(v_tok_done, 1)

            def gate_act_og():
                act.wait_ge(unit_free, units.up(4 * G))
                nc.scalar.activation(og, og, ACT.Silu).then_inc(act_in, 1)

            def mix(head):
                wait(act, s_out, (heads.up() - 1) * 32)
                act.dma_start(S0, state[bass.ds(head, 1), :, :, :].rearrange("o p b v -> (o p) b v")).then_inc(s0_in, 16)
                nc.scalar.activation(qa, tq, ACT.Silu).then_inc(act_in, 1)
                nc.scalar.activation(tf, tf, ACT.Sigmoid).then_inc(act_in, 1)
                act.wait_ge(fg_done, forget.up())
                nc.scalar.activation(tf, tf, ACT.Ln).then_inc(act_in, 1)
                act.wait_ge(g_done, decays.up())
                nc.scalar.activation(dec[:, 0:TILES_A], ga[:, P - 1:TP:P], ACT.Exp)
                nc.scalar.activation(dec[:, TILES_A:16], ga[:, TP + QS - 1:T:QS], ACT.Exp).then_inc(e_done, 1)
                group_exps(0, GRP)
                for g in range(TP // GRP):
                    tile_copies(P, 0, True)
                    tile_copies(P, P, False)
                    if g < TP // GRP - 1:
                        group_exps(0, GRP)
                    else:
                        group_exps(XQ, TS)
                    output_rms(GRP)
                tile_copies(TS, 0, True)
                output_rms(TS)
                act.wait_ge(s_done, states.up(TILES_A + 2))
                act.dma_start(st_prompt[bass.ds(head, 1), :, :].rearrange("o p v -> (o p) v"), S).then_inc(s_out, 16)
                act.dma_start(st_sample[bass.ds(head, 1), :, :, :].rearrange("o p b v -> (o p) b v"), S0)\
                    .then_inc(s_out, 16)

            gate_act_og()
            v_copies()
            rounds = HEADS_A - 1
            for i in turns(
                    act, rounds, 1, own=(own, 5), fo=(forget, 1), de=(decays, 1), ex=(exponents, 5), kt=(kts, 9),
                    ou=(outs, 9), os=(osums, 5), vt=(vts, 9), st=(states, TILES_A + 2), he=(heads, 1), on=(ons, 5),
                    un=(units, 36)):
                mix(i)
                gate_act_og()
                v_copies()
                units.up(24)
            mix(rounds)
            units.up(24)

            gates, prods, ples = Count(), Count(), Count()

            def gate_groups(func):
                for g in range(G):
                    act.wait_ge(unit_free, units.up())
                    nc.scalar.activation(gate_s[:, cols(g)], gate_s[:, cols(g)], func).then_inc(gate_act, 1)

            def ffn(gi):
                act.wait_ge(unit_free, units.at())
                norm(gi)
                with act.Fori(0, FT // 2) as i, looped(i, FT // 2, un=(units, 60), pr=(prods, 6)):
                    for buf in range(2):
                        gate_groups(ACT.Silu)
                        for g in range(G):
                            act.wait_ge(a_prod, prods.up())
                            nc.scalar.activation(ah[:, buf, cols(g)], up_s[:, cols(g)], ACT.Copy).then_inc(a_hi, 1)
                        units.up(G)
                    units.up(2 * KT * G)

            def ple(gi, layer):
                act.wait_ge(unit_free, units.at())
                act.dma_start(praw, pT[bass.ds(layer, 1), :, :, :].rearrange("o p k t -> (o p) k t")).then_inc(p_in, 16)
                norm(gi)
                act.wait_ge(p_in, 16 * ples.up())
                nc.scalar.activation(ah[:, :, :], praw, ACT.Copy).then_inc(a_hi, 1)
                with act.Fori(0, KT) as i, looped(i, KT, un=(units, 6)):
                    gate_groups(ACT.Sigmoid)
                    units.up(G)

            def staged(dst):
                dst_t = dst.rearrange("(n p) t -> n p t", p=P)
                with act.Fori(0, KT // 2) as i, looped(i, KT // 2, un=(units, 2 * G)):
                    for s in range(2):
                        act.wait_ge(unit_free, units.up(G))
                        act.dma_start(dst_t[bass.ds(2 * i + s, 1), :, :].rearrange("o p t -> (o p) t"), stage[:, s, :])\
                            .then_inc(stg_out[s], 16)

            ffn(G_FFN0)
            ple(G_PLE0, 0)
            act.wait_ge(unit_free, units.at())
            norm(G_KV)
            staged(kT_out)
            staged(vT_out)
            act.wait_ge(unit_free, units.at())
            norm(G_MIX1)
            staged(qT_scratch)
            assert units.n == U_Q

            act.preload_act_table_set("natural_log_exp_and_others")
            mins, las, avs, seqs, ats = [Count() for _ in range(5)]
            act.wait_ge(maskd, 1)
            for half in range(2):
                act.wait_ge(pe_vn, half + 1)
                nc.scalar.activation(vn[0:TS, half * 512:(half + 1) * 512], bank[4 + half][0:TS, :], ACT.Copy)\
                    .then_inc(vn_done, 1)
            for j in turns(act, PAIRS, 1, own=(own, 16), mi=(mins, 16), la=(las, 16), av=(avs, 16), se=(seqs, 1),
                           at=(ats, 16)):
                seq = seqs.up()
                act.wait_ge(pe_v8, seq)
                nc.scalar.activation(v8, psum[:, 4:6, :].rearrange("p a (b c) -> p (a b) c", c=P), ACT.Copy)\
                    .then_inc(v8_done, 1)
                for it in range(STEPS):
                    if it < 16:
                        L = P * (it // 2 + 1)
                        lb_ = wt[:, it % 3, 0:L]
                        act.wait_ge(min_done, mins.up())
                        did(nc.scalar.activation(lb_, lb_, ACT.Exp))
                        nc.scalar.activation(lb_, lb_, ACT.Ln, bias=c_one[:, 0:1]).then_inc(sp_in, 1)
                    if it == SX_STEP + 1:
                        act.wait_ge(sx_done, seq)
                        nc.scalar.activation(szl[:, 0:NPG, :], szl[:, 0:NPG, :], ACT.Exp)
                        nc.scalar.activation(szl[0:TS, NPG, :], szl[0:TS, NPG, :], ACT.Exp).then_inc(sl_exp, 1)
                        act.wait_ge(sl_exp, seq)
                        nc.scalar.activation(szl[:, 0:NPG, :], szl[:, 0:NPG, :], ACT.Ln, bias=c_one[:, 0:1])
                        nc.scalar.activation(szl[0:TS, NPG, :], szl[0:TS, NPG, :], ACT.Ln, bias=c_one[0:TS, 0:1])\
                            .then_inc(sl_done, 1)
                    if it == SA_STEP:
                        act.wait_ge(sla, seq)
                        nc.scalar.activation(szl[:, 0:NPG, :], szl[:, 0:NPG, :], ACT.Exp)
                        nc.scalar.activation(szl[0:TS, NPG, :], szl[0:TS, NPG, :], ACT.Exp).then_inc(sexp, 1)
                    if 1 <= it < 17:
                        n = it - 1
                        a = wt[:, n % 3, 0:P * (n // 2 + 1)]
                        act.wait_ge(la_done, las.up())
                        nc.scalar.activation(a, a, ACT.Exp).then_inc(aexp, 1)
                    if 2 <= it < 18:
                        n = it - 2
                        L = min(P * (n // 2 + 1), 512)
                        i = ats.up()
                        act.wait_ge(pe_at, i)
                        wait(act, pe_av, i - 1)
                        nc.scalar.activation(aT[:, 0:L], bank[4][:, 0:L], ACT.Copy).then_inc(at_act, 1)
                    if 3 <= it < 19:
                        n = it - 3
                        act.wait_ge(pe_av, avs.up())
                        if n == 0:
                            wait(act, pe_ot, seq - 1)
                        nc.scalar.activation(o_t[:, n // 2, n % 2 * HD:(n % 2 + 1) * HD], bank[6][:, 0:HD], ACT.Copy)\
                            .then_inc(av_done, 1)
                act.wait_ge(pe_ot, seq)
                nc.scalar.activation(xh[:, bass.ds(j, 1), 0:TP].rearrange("p o t -> p (o t)"),
                                     psum[:, 4:6, :].rearrange("p a b -> p (a b)"), ACT.Copy).then_inc(o_hi, 1)

            units.up(KT * G)
            ffn(G_FFN1)
            ple(G_PLE1, 1)
            act.wait_ge(unit_free, units.at())
            assert units.n == U_P1
            norm(None)
            act.wait_ge(s_out, HEADS_A * 32)
            act.wait_ge(stg_out[0], 16 * 12)
            act.wait_ge(stg_out[1], 16 * 12)

        @block.vector
        def _(dve):
            own, units = Count(), Count()
            xhs, sqs, rst = Count(), Count(), Count()

            def did(ins):
                ins.then_inc(dself, 1)
                dve.wait_ge(dself, own.up())

            dve.wait_ge(s_cload, 64)
            did(nc.vector.tensor_tensor(lb[:, :], lbr[:, 0, :], lbr[:, 1, :], ALU.subtract))

            def evac(dst):
                for g in range(G):
                    dve.wait_ge(unit_done, units.up())
                    nc.vector.tensor_tensor(dst[:, cols(g)], bank[g][:, 0:GW], rstd[:, cols(g)], ALU.mult)\
                        .then_inc(unit_free, 1)

            def add_to_h(n):
                for g in range(G):
                    dve.wait_ge(unit_done, units.up())
                    nc.vector.tensor_tensor(h[:, n, cols(g)], h[:, n, cols(g)], bank[g][:, 0:GW], ALU.add)\
                        .then_inc(unit_free, 1)

            def norm(gi):
                wait(dve, unit_free, units.at())
                for g in range(G):
                    for k in range(KT if gi is not None else 0):
                        dve.wait_ge(xh_done, xhs.up())
                        nc.vector.scalar_tensor_tensor(xl[:, k, cols(g)], h[:, k, cols(g)], gain[:, gi, k:k + 1],
                                                       flat(xh[:, k, cols(g)]), ALU.mult, ALU.subtract)\
                            .then_inc(x_ready, 1)
                    dve.wait_ge(sq_done, sqs.up())
                    nc.vector.tensor_reduce(ssq[:, g, :], sq.rearrange("p k t -> p t k"), AX_X, ALU.add)\
                        .then_inc(ssq_done, 1)
                dve.wait_ge(rstd_done, rst.up(G))

            norm(G_MIX0)

            ins_, exps, levs, us, os_, oc, orst_, heads, vts, gs, souts, fgs, ons = [Count() for _ in range(13)]

            def by_group(ap, at, width, *shape):
                v = ap[:, at:at + width]
                if len(shape) == 1:
                    return v.rearrange("p (b r) -> p b r", r=shape[0])
                return v.rearrange("p (b t r) -> p b t r", t=2, r=shape[1])

            def exponents(at, width, levels):
                if levels:
                    for l, hf in enumerate(HALVES):
                        gv = by_group(ga, at, width, 2, hf)
                        xv = by_group(X[:, l, :], 0, width, 2, hf)
                        nb = width // (2 * hf)
                        ref = gv[:, :, 0, hf - 1:hf].broadcast_to([P, nb, hf])
                        nc.vector.tensor_tensor(xv[:, :, 0, :], ref, gv[:, :, 0, :], ALU.subtract)
                        nc.vector.tensor_tensor(xv[:, :, 1, :], gv[:, :, 1, :], ref, ALU.subtract)
                gv = by_group(ga, at, width, QS)
                ref = gv[:, :, 1:2].broadcast_to([P, width // QS, QS])
                nc.vector.tensor_tensor(by_group(X[:, XQ, :], 0, width, QS), gv, ref, ALU.subtract)
                nc.vector.tensor_tensor(by_group(X[:, XK, :], 0, width, QS), ref, gv, ALU.subtract)
                nc.vector.tensor_copy(X[:, XQD, 0:width], ga[:, at:at + width])
                span = P if levels else QS
                gv = by_group(ga, at, width, span)
                ref = gv[:, :, span - 1:span].broadcast_to([P, width // span, span])
                nc.vector.tensor_tensor(by_group(X[:, XKD, :], 0, width, span), ref, gv, ALU.subtract)\
                    .then_inc(d_done, 1)

            def operands(at, width, levels):
                dve.wait_ge(e_done, exps.up())
                if levels:
                    for l, hf in enumerate(HALVES):
                        xv = by_group(X[:, l, :], 0, width, 2, hf)
                        for t, src in ((0, ka), (1, qa)):
                            nc.vector.tensor_tensor(xv[:, :, t, :], xv[:, :, t, :],
                                                    by_group(src, at, width, 2, hf)[:, :, t, :], ALU.mult)
                for slot, src in ((XQ, qa), (XK, ka), (XQD, qa), (XKD, ka)):
                    last = nc.vector.tensor_tensor(X[:, slot, 0:width], X[:, slot, 0:width], src[:, at:at + width],
                                                   ALU.mult)
                last.then_inc(xg_ready, 1)

            def scores(tile):
                for half, bk in ((0, 3), (1, 4)):
                    dve.wait_ge(pe_lev, levs.up())
                    nc.vector.tensor_tensor(prod[:, 3 * half:3 * half + 3, :],
                                            bank[bk][:, 0:3 * P].rearrange("p (l t) -> p l t", l=3),
                                            maskA[:, 3 * half:3 * half + 3, :], ALU.mult).then_inc(lev_free, 1)
                dve.wait_ge(lev_free, levs.at())
                wait(dve, pe_o, os_.at())
                nc.vector.tensor_reduce(att, prod.rearrange("p l t -> p t l"), AX_X, ALU.add).then_inc(att_done, 1)

            def new_state(tile):
                dve.wait_ge(pe_u, us.up())
                dve.wait_ge(pe_o, os_.up())
                dve.wait_ge(s_done, gs.at())
                nc.vector.scalar_tensor_tensor(S, S, dec[:, tile:tile + 1], bank[6][:, 0:P], ALU.mult, ALU.add)\
                    .then_inc(s_done, 1)
                gs.up()

            def squares(width, tiles):
                dve.wait_ge(o_copied, oc.up(tiles))
                dve.wait_ge(att_done, levatt.at())
                nc.vector.tensor_tensor(prod.rearrange("p l t -> p (l t)")[:, 0:width], o_s[:, 0:width],
                                        o_s[:, 0:width], ALU.mult).then_inc(osq_done, 1)

            def normed(at, width, head):
                dve.wait_ge(orstd_done, orst_.up())
                o = o_s[:, 0:width]
                did(nc.vector.tensor_tensor(o, o, orst[:, 0:width], ALU.mult))
                did(nc.vector.scalar_tensor_tensor(o, o, gon[:, bass.ds(head, 1)], og[:, at:at + width],
                                                   ALU.mult, ALU.mult))
                did(nc.vector.tensor_copy(ah[:, 0, at:at + width], o))
                nc.vector.tensor_tensor(al[:, 0, at:at + width], o, flat(ah[:, 0, at:at + width]), ALU.subtract)\
                    .then_inc(on_done, 1)
                ons.up()

            levatt = Count()

            def mix(head, ahead):
                wait(dve, s_out, (heads.up() - 1) * 32)
                nc.vector.memset(S, 0.0).then_inc(s_done, 1)
                gs.up()
                dve.wait_ge(act_in, ins_.up(3))
                did(nc.vector.tensor_scalar(tf, tf, omlb[:, bass.ds(head, 1)], lb[:, bass.ds(head, 1)],
                                            ALU.mult, ALU.add))
                did(nc.vector.tensor_scalar(tf, tf, LN_FLOOR, None, ALU.max))
                nc.vector.tensor_scalar(ka, tf, -1.0, 1.0, ALU.mult, ALU.add).then_inc(fg_done, 1)
                dve.wait_ge(act_in, ins_.up())
                nc.vector.tensor_tensor_scan(ga, reset[:, :], tf, 0.0, ALU.mult, ALU.add).then_inc(g_done, 1)
                dve.wait_ge(g_done, fgs.up())
                dve.wait_ge(pe_vt, vts.up(9))
                exps.up()
                exponents(0, GRP, True)
                operands(0, GRP, True)
                if ahead:
                    evac(tq)
                for g in range(TP // GRP):
                    for c in range(2):
                        scores(2 * g + c)
                        levatt.up()
                        new_state(2 * g + c)
                    squares(GRP, 2)
                    if g < TP // GRP - 1:
                        exponents((g + 1) * GRP, GRP, True)
                        operands((g + 1) * GRP, GRP, True)
                    else:
                        exponents(TP, TS, False)
                        operands(TP, TS, False)
                    normed(g * GRP, GRP, head)
                    if g == 0 and ahead:
                        evac(tf)
                dve.wait_ge(pe_lev, levs.up())
                dve.wait_ge(pe_o, os_.at())
                nc.vector.tensor_tensor(att[0:TS, 0:TS], bank[4][0:TS, 0:TS], maskA[0:TS, NL, 0:TS], ALU.mult)\
                    .then_inc(lev_free, 1)
                dve.wait_ge(lev_free, levs.at())
                nc.vector.tensor_tensor(vb, vtok[0:TS, TILES_A:TILES_A + 1, :].broadcast_to([TS, NB, P]),
                                        bmask[0:TS, :].rearrange("p (b o) -> p b o", o=1).broadcast_to([TS, NB, P]),
                                        ALU.mult).then_inc(att_done, 1)
                levatt.up()
                dve.wait_ge(pe_u, us.up())
                dve.wait_ge(pe_o, os_.up())
                did(nc.vector.tensor_tensor(S0, S0, dec[:, TILES_A:16].rearrange("p (b o) -> p b o", o=1)
                                            .broadcast_to([P, NB, P]), ALU.mult))
                nc.vector.tensor_tensor(S0[:, 0:4, :], S0[:, 0:4, :], bank[3].rearrange("p (b v) -> p b v", b=4), ALU.add)
                nc.vector.tensor_tensor(S0[:, 4:8, :], S0[:, 4:8, :], bank[4].rearrange("p (b v) -> p b v", b=4), ALU.add)\
                    .then_inc(s_done, 1)
                gs.up()
                squares(TS, 1)
                normed(TP, TS, head)
                if ahead:
                    evac(tv)
                    dve.wait_ge(on_done, ons.at())
                    evac(og)
                for n in range(KT):
                    add_to_h(n)
            for dst in (tq, tf, tv, og):
                evac(dst)
            rounds = HEADS_A - 1
            for i in turns(
                    dve, rounds, 1, own=(own, 18), un=(units, 36), ins=(ins_, 4), ex=(exps, 6), le=(levs, 17), us=(us, 9),
                    os=(os_, 9), oc=(oc, 9), ors=(orst_, 5), he=(heads, 1), vt=(vts, 9), gs=(gs, 10), fg=(fgs, 1),
                    on=(ons, 5), la=(levatt, 9)):
                mix(i, True)
            mix(rounds, False)
            assert units.n == U_A

            gates, his = Count(), Count()

            def ffn(gi):
                norm(gi)
                with dve.Fori(0, FT // 2) as i, looped(i, FT // 2, un=(units, 60), ga=(gates, 6), hi=(his, 6)):
                    for buf in range(2):
                        evac(gate_s)
                        evac(up_s)
                        dve.wait_ge(unit_free, units.at())
                        for g in range(G):
                            dve.wait_ge(gate_act, gates.up())
                            nc.vector.tensor_tensor(up_s[:, cols(g)], up_s[:, cols(g)], gate_s[:, cols(g)], ALU.mult)\
                                .then_inc(a_prod, 1)
                        for g in range(G):
                            dve.wait_ge(a_hi, his.up())
                            nc.vector.tensor_tensor(al[:, buf, cols(g)], up_s[:, cols(g)], flat(ah[:, buf, cols(g)]),
                                                    ALU.subtract).then_inc(a_ready, 1)
                    for buf in range(2):
                        for n in range(KT):
                            add_to_h(n)

            def ple(gi):
                norm(gi)
                dve.wait_ge(a_hi, his.up())
                nc.vector.tensor_tensor(al[:, :, :], praw, flat(ah[:, :, :]), ALU.subtract).then_inc(a_ready, 1)
                with dve.Fori(0, KT) as n, looped(n, KT, un=(units, 6), ga=(gates, 3), own=(own, 3)):
                    evac(gate_s)
                    for g in range(G):
                        dve.wait_ge(gate_act, gates.up())
                        dve.wait_ge(unit_done, units.up())
                        did(nc.vector.tensor_tensor(gate_s[:, cols(g)], gate_s[:, cols(g)], bank[g][:, 0:GW], ALU.mult))
                        hv = h[:, bass.ds(n, 1), cols(g)].rearrange("p o t -> p (o t)")
                        nc.vector.tensor_tensor(hv, hv, gate_s[:, cols(g)], ALU.add).then_inc(unit_free, 1)

            tiles = Count()

            def stage_tiles(scale):
                for i in turns(dve, KT // 2, 1, un=(units, 2 * G), ti=(tiles, 2)):
                    for s in range(2):
                        t = tiles.up()
                        for g in range(G):
                            dve.wait_ge(unit_done, units.up())
                            if g == 0:
                                wait(dve, stg_out[s], ((tiles.n - 1) // 2) * 16 + tiles.off * 8)
                            nc.vector.scalar_tensor_tensor(stage[:, s, cols(g)], bank[g][:, 0:GW], scale,
                                                           rstd[:, cols(g)], ALU.mult, ALU.mult).then_inc(unit_free, 1)

            ffn(G_FFN0)
            ple(G_PLE0)
            norm(G_KV)
            stage_tiles(1.0)
            stage_tiles(1.0)
            norm(G_MIX1)
            stage_tiles(HD ** -0.5)
            assert units.n == U_Q

            zs, sps, seqs, sufs, ats, hard = [Count() for _ in range(6)]
            new = slice(0, TS)
            dve.wait_ge(maskd, 1)
            dve.wait_ge(q_in, 48)
            for hh in range(2):
                r = slice(hh * HD, (hh + 1) * HD)
                nc.vector.tensor_copy(qblk[r, :, :, hh * QS:(hh + 1) * QS],
                                      qs_[r, :, :].rearrange("p j (b q) -> p j b q", b=NB))
            nc.vector.tensor_copy(bcol.rearrange("p (h q) -> p h q", q=QS),
                                  biasB[:, :].rearrange("p (h o) -> p h o", o=1).broadcast_to([P, HEADS_B, QS]))\
                .then_inc(qblk_done, 1)
            dve.wait_ge(qblk_done, 1)
            dve.wait_ge(pe_vn, 2)

            def scores_of(n):
                L = P * (n // 2 + 1)
                return psum[:, 2 * (n % 2):2 * (n % 2) + 2, :].rearrange("p a b -> p (a b)")[:, 0:L]

            for j in turns(dve, PAIRS, 1, own=(own, 32 + SOWN), zs=(zs, 16), sp=(sps, 16), se=(seqs, 1),
                           su=(sufs, NPG), at=(ats, 8)):
                seq = seqs.up()
                for it in range(STEPS):
                    if it == SL_STEP:
                        dve.wait_ge(stail, seq)
                        lm = lnew[new, bass.ds(j * QS, QS)].rearrange("p (o q) -> p o q", o=1)\
                            .broadcast_to([TS, HEADS_B, QS])
                        nc.vector.tensor_tensor(szl[:, 0:NPG, :], szx[:, 0:NPG, :],
                                                bank[7].rearrange("p (g c) -> p g c", g=NPG), ALU.subtract)
                        did(nc.vector.tensor_tensor(szl[new, NPG, :], szx[new, NPG, :], bank[3][new, 0:64],
                                                    ALU.subtract))
                        an = szl[new, NPG, :].rearrange("p (h q) -> p h q", q=QS)
                        nc.vector.tensor_tensor(an, an, lm, ALU.min).then_inc(sla, 1)
                    if it < 16:
                        i = zs.up()
                        dve.wait_ge(pe_z, i)
                        wait(dve, pe_at, i - 3)
                        nc.vector.tensor_scalar(wt[:, it % 3, 0:P * (it // 2 + 1)], scores_of(it),
                                                biasB[:, bass.ds(2 * j + it % 2, 1)], 30.0,
                                                ALU.add, ALU.min).then_inc(min_done, 1)
                    if 1 <= it < 17:
                        n = it - 1
                        L = P * (n // 2 + 1)
                        z, item = scores_of(n), wt[:, n % 3, 0:L]
                        bias = biasB[:, bass.ds(2 * j + n % 2, 1)]
                        dve.wait_ge(sp_in, sps.up())
                        did(nc.vector.scalar_tensor_tensor(item, z, bias, item, ALU.add, ALU.max))
                        did(nc.vector.tensor_tensor_scan(tb_[:, 0:L][:, ::-1], item[:, ::-1], item[:, ::-1], 0.0,
                                                         ALU.add, ALU.bypass))
                        nc.vector.scalar_tensor_tensor(item, z, bias, tb_[:, 0:L], ALU.add, ALU.subtract)\
                            .then_inc(la_done, 1)
                    if 10 <= it < 18:
                        n = it - 2
                        L = P * (n // 2 + 1)
                        i = ats.up()
                        dve.wait_ge(pe_at, zs.n - 16 + zs.off + n + 1 if it >= 16 else zs.at() - 2)
                        dve.wait_ge(pe_av, zs.n - 16 + zs.off + n if it >= 16 else zs.at() - 3)
                        nc.vector.tensor_copy(aT[:, 512:L], bank[5][:, 0:L - 512]).then_inc(at_dve, 1)
                    if it == SX_STEP:
                        dve.wait_ge(sz_done, seq)
                        nc.vector.tensor_tensor(szx[:, 0:NPG, :], bank[7].rearrange("p (g c) -> p g c", g=NPG),
                                                bcol.rearrange("p (o c) -> p o c", o=1).broadcast_to([P, NPG, 64]),
                                                ALU.add)
                        did(nc.vector.tensor_tensor(szx[new, NPG, :], bank[1][new, 0:64], bcol[new, :], ALU.add))
                        nc.vector.tensor_scalar(szl[:, 0:NPG, :], szx[:, 0:NPG, :], 30.0, None, ALU.min)
                        nc.vector.tensor_scalar(szl[new, NPG, :], szx[new, NPG, :], 30.0, None, ALU.min)\
                            .then_inc(sx_done, 1)
                    if it == SX_STEP + 2:
                        dve.wait_ge(sl_done, seq)
                        nc.vector.tensor_tensor(ssp[:, 0:NPG, :], szx[:, 0:NPG, :], szl[:, 0:NPG, :], ALU.max)
                        did(nc.vector.tensor_tensor(ssp[new, NPG, :], szx[new, NPG, :], szl[new, NPG, :], ALU.max))
                        mb = mnew[new, bass.ds(j * QS, QS)].rearrange("p (o q) -> p o q", o=1)\
                            .broadcast_to([TS, HEADS_B, QS])
                        sn = ssp[new, NPG, :].rearrange("p (h q) -> p h q", q=QS)
                        nc.vector.tensor_tensor(sn, sn, mb, ALU.mult).then_inc(suf_step, 1)
                        sufs.up()
                        for pg in range(NPG - 2, -1, -1):
                            dve.wait_ge(suf_step, sufs.at())
                            nc.vector.tensor_tensor(suf[:, pg, :], suf[:, pg + 1, :], ssp[:, pg + 1, :], ALU.add)\
                                .then_inc(suf_step, 1)
                            sufs.up()
                    if it == STEPS - 1:
                        dve.wait_ge(sav, seq)
                        ov = bank[7][:, 0:64].rearrange("p (j e q) -> p j e q", e=2, q=QS)
                        for hh in range(2):
                            r = slice(hh * HD, (hh + 1) * HD)
                            did(nc.vector.tensor_copy(xh[r, :, bass.ds(j * QS + TP, QS)], ov[r, :, hh, :]))
                        for hh in range(2):
                            r = slice(hh * HD, (hh + 1) * HD)
                            last = nc.vector.tensor_tensor(xl[r, :, bass.ds(j * QS + TP, QS)], ov[r, :, hh, :],
                                                           flat(xh[r, :, bass.ds(j * QS + TP, QS)]), ALU.subtract)
                        last.then_inc(so_done, 1)
                dve.wait_ge(o_hi, seq)
                nc.vector.tensor_tensor(xl[:, bass.ds(j, 1), 0:TP].rearrange("p o t -> p (o t)"),
                                        psum[:, 4:6, :].rearrange("p a b -> p (a b)"),
                                        flat(xh[:, bass.ds(j, 1), 0:TP].rearrange("p o t -> p (o t)")),
                                        ALU.subtract).then_inc(o_lo, 1)

            for n in range(KT):
                dve.wait_ge(h_back[n], 16)
                add_to_h(n)
            ffn(G_FFN1)
            ple(G_PLE1)
            norm(None)
            for k in range(KT):
                nc.vector.scalar_tensor_tensor(h[:, k, :], h[:, k, :], gain[:, G_FIN, k:k + 1], rstd[:, :],
                                               ALU.mult, ALU.mult).then_inc(y_done, 1)

        @block.tensor
        def _(pe):
            slabs, units, xs, norms = Count(), Count(), Count(), Count()
            mm = nc.tensor.matmul

            def slab():
                pe.wait_ge(w_ready, slabs.up())
                fresh[0] = True
                return (slabs.n - 1) % 2

            fresh = [False]

            def unit_start():
                wait(pe, unit_free, units.up() - G)

            def exact(out, slot, tile, mh, ml, first, last):
                ws = slice(tile * P, (tile + 1) * P)
                ins = mm(out, wh[:, slot, ws], mh, start=first, stop=False)
                if fresh[0]:
                    ins.then_inc(w_used, 1)
                    fresh[0] = False
                mm(out, wh[:, slot, ws], ml, start=False, stop=False)
                return mm(out, wl[:, slot, ws], mh, start=False, stop=last)

            def product_x(n_tiles_k=KT):
                slot = slab()
                for g in range(G):
                    unit_start()
                    for k in range(KT):
                        last = exact(bank[g][:, 0:GW], slot, k, xh[:, k, cols(g)], xl[:, k, cols(g)], k == 0, k == KT - 1)
                    last.then_inc(unit_done, 1)
            def product_a(slot, tile, buf, first=True, last=True):
                for g in range(G):
                    unit_start()
                    exact(bank[g][:, 0:GW], slot, tile, ah[:, buf, cols(g)], al[:, buf, cols(g)], True, True)\
                        .then_inc(unit_done, 1)

            def norm(x=True):
                for g in range(G):
                    pe.wait_ge(ssq_done, norms.up())
                    mm(bank[4 + g][:, 0:GW], ones[:, :], ssq[:, g, :], start=True, stop=True).then_inc(nsum_done, 1)
                if x:
                    pe.wait_ge(x_ready, xs.up(G * KT))

            pe.wait_ge(s_const, 5)
            norm()

            groups, levs, kts, us, outs, heads, sds, ons, vts, atts, osqs, vtk = [Count() for _ in range(12)]
            osum = Count()

            def level_scores(c):
                ts = slice(c % 2 * P, c % 2 * P + P)
                for half, bk in ((0, 3), (1, 4)):
                    wait(pe, lev_free, levs.up() - 2)
                    for l in range(3 * half, 3 * half + 3):
                        lhs, rhs = (X[:, l, ts], X[:, l, ts]) if l < NL else (X[:, XK, ts], X[:, XQ, ts])
                        last = mm(bank[bk][:, (l % 3) * P:(l % 3 + 1) * P], lhs, rhs, start=True, stop=True)
                    last.then_inc(pe_lev, 1)

            def keys_transposed(c, rows):
                at = c % 2 * P
                i = kts.up()
                wait(pe, kd_tok, i - 1)
                nc.tensor.transpose(bank[5][0:rows, 0:P], X[:, XKD, at:at + rows], ident[:, :]).then_inc(pe_kt, 1)

            def tile_output(c):
                at = c % 2 * P
                pe.wait_ge(kd_tok, us.up())
                pe.wait_ge(s_done, sds.up())
                mm(bank[6][:, 0:P], kdt[:, :], vtok[:, c, :], start=True, stop=True).then_inc(pe_u, 1)
                pe.wait_ge(att_done, atts.up())
                wait(pe, o_copied, outs.up() - 1)
                wait(pe, orstd_done, osqs.at())
                o = bank[7][:, at:at + P]
                mm(o, S, X[:, XQD, at:at + P], start=True, stop=False)
                mm(o, vtok[:, c, :], att[:, :], start=False, stop=True).then_inc(pe_o, 1)

            def output_sums(width):
                pe.wait_ge(osq_done, osqs.up())
                wait(pe, orstd_done, osqs.at() - 1)
                mm(bank[7][:, GRP:GRP + width], ones[:, :], prod.rearrange("p l t -> p (l t)")[:, 0:width],
                   start=True, stop=True).then_inc(pe_osum, 1)

            def v_transposed():
                pe.wait_ge(unit_free, units.at())
                for c in range(TILES_A + 1):
                    rows = P if c < TILES_A else TS
                    wait(pe, v_tok_done, vtk.up() - 2)
                    nc.tensor.transpose(bank[5 + c % 2][0:rows, 0:P], tv[:, c * P:c * P + rows], ident[:, :])\
                        .then_inc(pe_vt, 1)

            def mix(ahead):
                if ahead:
                    product_x()
                pe.wait_ge(v_tok_done, vts.up(9))
                for g in range(TP // GRP):
                    pe.wait_ge(xg_ready, groups.up())
                    c = 2 * g
                    level_scores(c)
                    keys_transposed(c, P)
                    level_scores(c + 1)
                    tile_output(c)
                    keys_transposed(c + 1, P)
                    tile_output(c + 1)
                    output_sums(GRP)
                    if g == 0 and ahead:
                        product_x()
                pe.wait_ge(xg_ready, groups.up())
                sds.up(2)
                pe.wait_ge(s_done, sds.at() - 1)
                pe.wait_ge(lev_free, levs.up() - 1)
                mm(bank[4][0:TS, 0:TS], X[:, XK, 0:TS], X[:, XQ, 0:TS], start=True, stop=True).then_inc(pe_lev, 1)
                keys_transposed(0, TS)
                pe.wait_ge(att_done, atts.up())
                wait(pe, o_copied, outs.up() - 1)
                pe.wait_ge(orstd_done, osqs.at())
                pe.wait_ge(s0_in, heads.up() * 16)
                pe.wait_ge(kd_tok, us.up())
                o = bank[7]
                mm(o[:, 0:TS], vtok[0:TS, TILES_A, :], att[0:TS, 0:TS], start=True, stop=False)
                for b in range(NB):
                    last = mm(o[:, QS * b:QS * b + QS], S0[:, b, :], X[:, XQD, QS * b:QS * b + QS], start=False,
                              stop=(b == NB - 1))
                last.then_inc(pe_o, 1)
                mm(bank[3][:, :], kdt[0:TS, :], vb[:, 0:4, :], start=True, stop=True)
                mm(bank[4][:, :], kdt[0:TS, :], vb[:, 4:8, :], start=True, stop=True).then_inc(pe_u, 1)
                output_sums(TS)
                if ahead:
                    product_x()
                    product_x()
                    v_transposed()
                pe.wait_ge(on_done, ons.up(5))
                for half in range(2):
                    slot = slab()
                    for n in range(4):
                        product_a(slot, n, 0)

            for _ in range(4):
                product_x()
            v_transposed()
            rounds = HEADS_A - 1
            for i in turns(
                    pe, rounds, 1, sl=(slabs, 6), un=(units, 36), gr=(groups, 5), le=(levs, 17), kt=(kts, 9), us=(us, 9),
                    ou=(outs, 9), he=(heads, 1), sd=(sds, 10), on=(ons, 5), vt=(vts, 9), at=(atts, 9), os=(osqs, 5),
                    vk=(vtk, 9)):
                mix(True)
            mix(False)

            ars = Count()

            def ffn():
                norm()
                with pe.Fori(0, FT // 2) as i, looped(i, FT // 2, sl=(slabs, 6), un=(units, 60), ar=(ars, 6)):
                    for _ in range(4):
                        product_x()
                    for buf in range(2):
                        slot = slab()
                        pe.wait_ge(a_ready, ars.up(3))
                        for n in range(KT):
                            product_a(slot, n, buf)
    
            def ple():
                norm()
                pe.wait_ge(a_ready, ars.up())
                with pe.Fori(0, KT) as i, looped(i, KT, sl=(slabs, 2), un=(units, 6)):
                    product_x()
                    slot = slab()
                    for g in range(G):
                        unit_start()
                        for k in range(PK):
                            last = exact(bank[g][:, 0:GW], slot, k, ah[:, k, cols(g)], al[:, k, cols(g)], k == 0,
                                         k == PK - 1)
                        last.then_inc(unit_done, 1)

            def products(n):
                with pe.Fori(0, n // 2) as i, looped(i, n // 2, sl=(slabs, 2), un=(units, 6)):
                    product_x()
                    product_x()

            ffn()
            ple()
            norm()
            products(16)
            norm()
            products(KT)
            assert units.n == U_Q and slabs.n == BEFORE

            pairs, zs, ats, avs, vpgs = [Count() for _ in range(5)]
            tr = nc.tensor.transpose
            pe.wait_ge(unit_free, units.at())
            pe.wait_ge(q_in, 48)
            for j in range(PAIRS):
                last = tr(bank[4 + j // 4][0:TS, j % 4 * P:(j % 4 + 1) * P], vnT[:, j, :], ident[:, :])
                if j % 4 == 3:
                    last.then_inc(pe_vn, 1)
            pe.wait_ge(vn_done, 2)
            pe.wait_ge(qblk_done, 1)
            pe.wait_ge(maskd, 1)
            for b in turns(pe, PAIRS, 1, pa=(pairs, 1), zs=(zs, 16), at=(ats, 16), av=(avs, 16), vp=(vpgs, 8)):
                seq = pairs.up()

                def sample_scores(pages):
                    for pg in pages:
                        pe.wait_ge(pg_k[pg % KRING], (pg // KRING + 1) * 16 + b * (NPG // KRING * 16))
                        for jj in range(PAIRS):
                            at = pg * 64 + jj * 8
                            last = mm(bank[7][:, at:at + 8], kpg[:, pg % KRING, jj * P:(jj + 1) * P],
                                      qblk[:, jj, bass.ds(b, 1), :].rearrange("p o c -> p (o c)"), start=True, stop=True)
                        last.then_inc(kpg_free, 1)

                pe.wait_ge(pair_in, seq * 48)
                wait(pe, o_lo, seq - 1)
                for c in range(KT):
                    last = tr(bank[4 + c // 4][:, c % 4 * P:(c % 4 + 1) * P], vc[:, c * P:(c + 1) * P], ident[:, :])
                last.then_inc(pe_v8, 1)
                for it in range(STEPS):
                    if it < 16:
                        qt, hh = it // 2, it % 2
                        L = P * (qt + 1)
                        r = slice(hh * HD, (hh + 1) * HD)
                        wait(pe, la_done, zs.up() - 2)
                        if it == SL_STEP:
                            pe.wait_ge(sla, seq)
                        for half in range(-(-(L - P) // 512)):
                            n = min(512, L - P - 512 * half)
                            mm(bank[2 * hh + half][:, 0:n], qc[r, qt * P:(qt + 1) * P],
                               kc[r, 512 * half:512 * half + n], start=True, stop=True)
                        at = (L - P) % 512
                        own = bank[2 * hh + (L - P) // 512][:, at:at + P]
                        mm(own, qc[r, qt * P:(qt + 1) * P], kc[r, L - P:L], start=True, stop=False)
                        mm(own, ident[:, :], negm, start=False, stop=True).then_inc(pe_z, 1)
                    if 3 <= it < 19:
                        n = it - 3
                        qt, hh = n // 2, n % 2
                        if n == 0:
                            pe.wait_ge(v8_done, seq)
                        i = avs.up()
                        pe.wait_ge(at_act, i)
                        if n >= 8:
                            pe.wait_ge(at_dve, n - 7 + (b * 8))
                        wait(pe, av_done, i - 1)
                        for c in range(qt + 1):
                            last = mm(bank[6][:, 0:HD], aT[:, c * P:(c + 1) * P],
                                      v8[:, c, hh * HD:(hh + 1) * HD], start=(c == 0), stop=(c == qt))
                        last.then_inc(pe_av, 1)
                    if 2 <= it < 18:
                        n = it - 2
                        qt, hh = n // 2, n % 2
                        i = ats.up()
                        pe.wait_ge(aexp, i)
                        if n == 0:
                            pe.wait_ge(v8_done, seq)
                        wait(pe, at_act, i - 1)
                        if n >= 9:
                            pe.wait_ge(at_dve, n - 8 + (b * 8))
                        for c in range(qt + 1):
                            last = tr(bank[4 + c // 4][:, c % 4 * P:(c % 4 + 1) * P],
                                      wt[:, n % 3, c * P:(c + 1) * P], ident[:, :])
                        last.then_inc(pe_at, 1)
                    if it in PAGE_STEPS:
                        if it == 0:
                            wait(pe, so_done, seq - 1)
                        sample_scores(PAGE_STEPS[it])
                    if it == SX_STEP - 1:
                        for jj in range(PAIRS):
                            last = mm(bank[1][0:TS, jj * 8:jj * 8 + 8], kn[:, jj, :],
                                      qblk[:, jj, bass.ds(b, 1), :].rearrange("p o c -> p (o c)"), start=True, stop=True)
                        last.then_inc(sz_done, 1)
                    if it == SL_STEP - 1:
                        pe.wait_ge(suf_step, (b + 1) * NPG)
                        tail = bank[7].rearrange("p (g c) -> p g c", g=NPG)
                        mm(tail, triP, ssp[:, 0:NPG, :], start=True, stop=False)
                        mm(tail, ones[:, :], suf, start=False, stop=False)
                        mm(tail, ones[0:TS, :], ssp[0:TS, NPG:NPG + 1, :].broadcast_to([TS, NPG, 64]),
                           start=False, stop=True)
                        mm(bank[3][0:TS, 0:64], triP[0:TS, 0:TS], ssp[0:TS, NPG, :], start=True, stop=True)\
                            .then_inc(stail, 1)
                    if SA_STEP < it <= SA_STEP + NPG:
                        pg = it - SA_STEP - 1
                        if pg == 0:
                            pe.wait_ge(sexp, seq)
                            mm(bank[7][:, 0:64], zer, szl[:, 0, :], start=True, stop=False)
                        pe.wait_ge(pg_v[pg % VRING], (pg // VRING + 1) * 16 + b * (NPG // VRING * 16))
                        for jj in range(PAIRS):
                            last = mm(bank[7][:, jj * 8:jj * 8 + 8], vslot(pg % VRING)[:, jj * P:(jj + 1) * P],
                                      szl[:, pg, jj * 8:jj * 8 + 8], start=False, stop=False)
                        last.then_inc(vpg_free, 1)
                        vpgs.up()
                        if pg == NPG - 1:
                            for jj in range(PAIRS):
                                last = mm(bank[7][:, jj * 8:jj * 8 + 8], vn[0:TS, jj * P:(jj + 1) * P],
                                          szl[0:TS, NPG, jj * 8:jj * 8 + 8], start=False, stop=(jj == PAIRS - 1))
                            last.then_inc(sav, 1)
                pe.wait_ge(av_done, avs.at())
                for c in range(KT):
                    last = tr(bank[4 + c // 4][:, c % 4 * P:(c % 4 + 1) * P], o_t[:, c, :], ident[:, :])
                last.then_inc(pe_ot, 1)

            pe.wait_ge(o_lo, PAIRS)
            pe.wait_ge(so_done, NB)
            products(N_O)
            ffn()
            ple()
            norm(False)


def kernel(x_prompt, x_sample, p_prompt, p_sample, state_hgrn, cache_k, cache_v, page_table, a_lb, w_a_in,
           g_a_onorm, w_a_o, g_kv, w_kv, w_b_q, w_b_o, sb_bias, g_mix, g_ffn, w_ffn_in, w_ffn_out, g_ple,
           w_ple_in, w_ple_gate, g_final):
    import numpy as _np
    import concourse.bacc as _bacc
    from concourse import mybir as _mybir
    from concourse.bass_utils import run_bass_kernel_spmd as _run

    f32 = _np.float32
    A = lambda a: _np.asarray(a)

    def tall(wt, col):
        return A(wt)[:, col * P:(col + 1) * P].reshape(-1, P, P).transpose(1, 0, 2)

    def wide(wt, row, c0, c1):
        return A(wt)[row * P:(row + 1) * P, c0:c1].reshape(P, -1, P)

    stream = _np.zeros((NSLAB, P, 8, P), f32)
    at = [0]

    def put(s):
        stream[at[0], :, :s.shape[1], :] = s
        at[0] += 1

    wa, wo = A(w_a_in)[0], A(w_a_o)[0]

    def ffn(l):
        wi, wu = A(w_ffn_in)[l], A(w_ffn_out)[l]
        for c in range(0, FT, 2):
            for t in (c, c + 1):
                put(tall(wi, t))
                put(tall(wi, FT + t))
            for t in (c, c + 1):
                put(wide(wu, t, 0, D))

    def ple(l):
        for n in range(KT):
            put(tall(A(w_ple_gate)[l], n))
            put(tall(A(w_ple_in)[l], n))

    for part in range(4):
        put(tall(wa, part * KT))
    for hd in range(HEADS_A):
        if hd + 1 < HEADS_A:
            for part in range(4):
                put(tall(wa, part * KT + hd + 1))
        put(wide(wo, hd, 0, 512))
        put(wide(wo, hd, 512, 1024))
    ffn(0)
    ple(0)
    for n in range(16):
        put(tall(w_kv, n))
    for n in range(KT):
        put(tall(A(w_b_q)[0], n))
    for n in range(KT):
        put(tall(A(w_b_o)[0], n))
    ffn(1)
    ple(1)
    assert at[0] == NSLAB

    def tokens_T(prompt, sample):
        return _np.concatenate([A(prompt).reshape(TP, -1), A(sample).reshape(TS, -1)]).T

    xT = _np.ascontiguousarray(tokens_T(x_prompt, x_sample))
    pT = _np.stack([tokens_T(A(p_prompt)[l], A(p_sample)[l]).reshape(PK, P, T).transpose(1, 0, 2) for l in range(2)])
    cols_ = lambda v: A(v).reshape(KT, P).T
    gm, gf, gp = A(g_mix), A(g_ffn), A(g_ple)
    gains = _np.stack([cols_(v) for v in (gm[0], gf[0], gp[0], g_kv, gm[1], gf[1], gp[1], g_final)], axis=1)
    ins = {
        "wstream": stream.reshape(NSLAB, P, SLAB),
        "xT": xT,
        "pT": pT,
        "state": A(state_hgrn)[0].transpose(1, 2, 0, 3),
        "kT_cache": A(cache_k).reshape(POOLPG, P, PAIRS, P).transpose(0, 3, 2, 1).reshape(POOLPG, P, D),
        "v_cache": A(cache_v).reshape(POOLPG, P, D),
        "table": A(page_table).reshape(1, NB * NPG),
        "lbT": A(a_lb).reshape(2, KT, P).transpose(2, 0, 1),
        "gains": gains,
        "g_on": A(g_a_onorm).reshape(HEADS_A, P).T,
        "sb_bias": A(sb_bias).reshape(1, HEADS_B),
    }
    outs = {
        "yT": (D, T), "st_prompt": (HEADS_A, P, P), "st_sample": (HEADS_A, P, NB, P), "kT_out": (D, T), "vT_out": (D, T),
    }
    nc = _bacc.Bacc("TRN2", target_bir_lowering=False, num_devices=1)
    arrays, args = {}, {}
    for name, a in ins.items():
        a = _np.ascontiguousarray(a)
        arrays[f"in_{name}"] = a
        args[name] = nc.dram_tensor(f"in_{name}", a.shape, _mybir.dt.from_np(a.dtype), kind="ExternalInput").ap()
    for name, shape in outs.items():
        args[name] = nc.dram_tensor(f"out_{name}", shape, _mybir.dt.float32, kind="ExternalOutput").ap()
    yoco_step(nc, **args)
    r = _run(nc, [arrays], core_ids=[0]).results[0]
    y, kk, vv = (_np.asarray(r[f"out_{n}"]).T for n in ("yT", "kT_out", "vT_out"))
    stp, sts = _np.asarray(r["out_st_prompt"]), _np.asarray(r["out_st_sample"])

    def split(a, *tail):
        return (_np.ascontiguousarray(a[:TP]).reshape(1, TP, *tail), _np.ascontiguousarray(a[TP:]).reshape(NB, QS, *tail))

    yp, ys = split(y, D)
    kp, ks = split(kk, HEADS_B, HD)
    vp, vs = split(vv, HEADS_B, HD)
    return (yp, ys, stp.reshape(1, 1, HEADS_A, P, P), _np.ascontiguousarray(sts.transpose(2, 0, 1, 3))[None],
            kp, vp, ks, vs)
```

```python
from contextlib import ExitStack, contextmanager

import numpy as np

import concourse.bass as bass
from concourse import mybir

F32 = mybir.dt.float32
F32R = mybir.dt.float32r
BF16 = mybir.dt.bfloat16
I32 = mybir.dt.int32
ALU = mybir.AluOpType
ACT = mybir.ActivationFunctionType
AX_X = mybir.AxisListType.X

P = 128
D = 1024
KT = D // P
TP = 1024
NB, QS = 8, 4
TS = NB * QS
T = TP + TS
G = 3
GW = T // G
FF = 2816
FT = FF // P
PLE = 256
PK = PLE // P
HEADS_A = 8
HEADS_B = 16
PAIRS = HEADS_B // 2
HD = 64
NPG = 8
POOLPG = 80
EPS = 1e-6
SLAB = 8 * P
TILES_A = TP // P
LN_FLOOR = 7.6e-10
HALVES = (64, 32, 16, 8, 4)
NL = len(HALVES)
XQ, XK, XQD, XKD = NL, NL + 1, NL + 2, NL + 3
NX = NL + 4
PARTS = ((0, 3), (3, NL + 2), (NL + 2, NX))
GRP = 256
BIG = 1e30
KRING = 4
VRING = 4

N_A = HEADS_A * 6
N_F = FT * 3
N_P = KT * 2
N_KV = 16
N_Q = 8
N_O = 8
BEFORE = N_A + N_F + N_P + N_KV + N_Q
NSLAB = BEFORE + N_O + N_F + N_P

STEPS = 20
PAGE_STEPS = {0: (0, 1), 1: (2, 3), 3: (4, 5), 4: (6, 7)}
SX_STEP = 5
SL_STEP = 9
SA_STEP = 10
SOWN = 5


class Count:

    def __init__(self):
        self.n = 0
        self.off = 0

    def up(self, k=1):
        self.n += k
        return self.n + self.off

    def at(self):
        return self.n + self.off


@contextmanager
def looped(i, reps, **counts):
    for c, k in counts.values():
        c.off = i * k
    start = {n: c.n for n, (c, k) in counts.items()}
    yield
    for n, (c, k) in counts.items():
        assert c.n - start[n] == k, (n, c.n - start[n], k)
        c.n = start[n] + k * reps
        c.off = 0


def turns(eng, reps, peel, **counts):
    for t in range(peel):
        yield t
    with eng.Fori(peel, reps) as i, looped(i - peel, reps - peel, **counts):
        yield i


def wait(eng, sem, value):
    if isinstance(value, int) and value <= 0:
        return
    eng.wait_ge(sem, value)


def yoco_step(nc, wstream, xT, pT, state, kT_cache, v_cache, table, lbT, gains, g_on, sb_bias,
              yT, st_prompt, st_sample, kT_out, vT_out):
    with ExitStack() as ctx:
        def sb(name, shape, dt=F32):
            return ctx.enter_context(nc.sbuf_tensor(name, shape, dt))

        def sem(name):
            return ctx.enter_context(nc.semaphore(name))

        h_scratch = nc.dram_tensor("h_scratch", [P, KT, T], F32, kind="Internal").ap()
        qT_scratch = nc.dram_tensor("qT_scratch", [D, T], F32, kind="Internal").ap()

        psum = ctx.enter_context(nc.psum_tensor("psum", [P, 8, 512], F32))
        bank = [psum[:, i, :] for i in range(8)]

        h = sb("h", [P, KT, T])
        xh = sb("xh", [P, KT, T], F32R)
        xl = sb("xl", [P, KT, T], F32R)
        raw = sb("raw", [P, 2, SLAB])
        wh = sb("wh", [P, 2, SLAB], F32R)
        wl = sb("wl", [P, 2, SLAB], F32R)
        ah = sb("ah", [P, 2, T], F32R)
        al = sb("al", [P, 2, T], F32R)
        rstd = sb("rstd", [P, T])
        ident = sb("ident", [P, P])
        ones = sb("ones", [P, P])
        gain = sb("gain", [P, 8, KT])
        gon = sb("gon", [P, HEADS_A])
        lbr = sb("lbr", [P, 2, KT])
        lb = sb("lb", [P, KT])
        omlb = sb("omlb", [P, KT])
        biasB = sb("biasB", [P, HEADS_B])
        c_eps = sb("c_eps", [P, 1])
        c_one = sb("c_one", [P, 1])
        c_epsv = sb("c_epsv", [P, 1])
        WORK = 12900
        work = sb("work", [P, WORK])

        class Carve:
            def __init__(self, place=None, size=WORK):
                self.at, self.place, self.size = 0, work if place is None else place, size

            def take(self, *shape):
                n = int(np.prod(shape))
                v = self.place[:, self.at:self.at + n]
                self.at += n
                assert self.at <= self.size, (self.at, self.size)
                if len(shape) == 2:
                    return v.rearrange("p (a b) -> p a b", a=shape[0])
                if len(shape) == 3:
                    return v.rearrange("p (a b c) -> p a b c", a=shape[0], b=shape[1])
                return v

        s_const = sem("s_const")
        s_cload = sem("s_cload")
        s_xload = [sem(f"s_xload{g}") for g in range(G)]
        landed = [sem("landed0"), sem("landed1")]
        split_go = sem("split_go")
        split_hi = sem("split_hi")
        w_ready = sem("w_ready")
        w_used = sem("w_used")
        unit_done = sem("unit_done")
        unit_free = sem("unit_free")
        xh_done = sem("xh_done")
        x_ready = sem("x_ready")
        sq_done = sem("sq_done")
        ssq_done = sem("ssq_done")
        nsum_done = sem("nsum_done")
        rstd_done = sem("rstd_done")
        dself = sem("dself")
        aself = sem("aself")
        act_in = sem("act_in")
        fg_done = sem("fg_done")
        g_done = sem("g_done")
        d_done = sem("d_done")
        e_done = sem("e_done")
        xg_ready = sem("xg_ready")
        pe_lev = sem("pe_lev")
        lev_free = sem("lev_free")
        att_done = sem("att_done")
        pe_kt = sem("pe_kt")
        kd_tok = sem("kd_tok")
        pe_u = sem("pe_u")
        s_done = sem("s_done")
        pe_o = sem("pe_o")
        o_copied = sem("o_copied")
        osq_done = sem("osq_done")
        pe_osum = sem("pe_osum")
        orstd_done = sem("orstd_done")
        on_done = sem("on_done")
        pe_vt = sem("pe_vt")
        v_tok_done = sem("v_tok_done")
        s0_in = sem("s0_in")
        s_out = sem("s_out")
        gate_act = sem("gate_act")
        a_prod = sem("a_prod")
        a_hi = sem("a_hi")
        a_ready = sem("a_ready")
        p_in = sem("p_in")
        stg_out = [sem("stg_out0"), sem("stg_out1")]
        y_done = sem("y_done")
        y_out = sem("y_out")
        h_away = sem("h_away")
        h_back = [sem(f"h_back{k}") for k in range(KT)]
        kq_in = [sem("kq_in0"), sem("kq_in1")]
        kq_hi = sem("kq_hi")
        kq_split = sem("kq_split")
        v_in = sem("v_in")
        pe_v8 = sem("pe_v8")
        v8_done = sem("v8_done")
        pe_z = sem("pe_z")
        min_done = sem("min_done")
        sp_in = sem("sp_in")
        la_done = sem("la_done")
        aexp = sem("aexp")
        pe_at = sem("pe_at")
        at_act = sem("at_act")
        at_dve = sem("at_dve")
        pe_av = sem("pe_av")
        o_hi = sem("o_hi")
        o_lo = sem("o_lo")
        maskd = sem("maskd")
        tb_in = sem("tb_in")
        q_in = sem("q_in")
        pg_k = [sem(f"pg_k{i}") for i in range(KRING)]
        pg_v = [sem(f"pg_v{i}") for i in range(VRING)]
        kpg_free = sem("kpg_free")
        vpg_free = sem("vpg_free")
        qblk_done = sem("qblk_done")
        pe_vn = sem("pe_vn")
        vn_done = sem("vn_done")
        sz_done = sem("sz_done")
        sx_done = sem("sx_done")
        sl_exp = sem("sl_exp")
        sl_done = sem("sl_done")
        suf_step = sem("suf_step")
        stail = sem("stail")
        sla = sem("sla")
        sexp = sem("sexp")
        sav = sem("sav")
        so_done = sem("so_done")

        w = Carve()
        tq, tf = w.take(T), w.take(T)
        qa, ka, ga = w.take(T), w.take(T), w.take(T)
        og = w.take(T)
        X = w.take(NX, GRP)
        tv = X.rearrange("p a b -> p (a b)")[:, 0:T]
        vb = X.rearrange("p a b -> p (a b)")[0:TS, 0:NB * P].rearrange("p (a b) -> p a b", a=NB)
        vtok = w.take(TILES_A + 1, P)
        kdt = w.take(P)
        prod = w.take(6, P)
        att = w.take(P)
        o_s, orst = w.take(GRP), w.take(GRP)
        S = w.take(P)
        S0 = w.take(NB, P)
        dec = w.take(16)
        bmask = w.take(NB)
        maskA = sb("maskA", [P, NL + 1, P], BF16)
        reset = sb("reset", [P, T], BF16)
        w = Carve()
        sq = w.take(KT, GW)
        ssq = w.take(G, GW)
        gate_s = w.take(T)
        up_s = w.take(T)
        praw = w.take(PK, T)
        stage = w.take(2, T)
        w = Carve()
        vc = w.take(TP)
        v8 = w.take(KT, P)
        wt = w.take(3, TP)
        tb_ = w.take(TP)
        aT = w.take(2, TP)
        kq1 = w.take(2, TP)
        negm = sb("negm", [P, P], BF16)
        ident_b = sb("ident_b", [P, P], BF16)
        triP = w.take(P)
        mnew = w.take(TS)
        lnew = w.take(TS)
        bcol = w.take(PAIRS * 2 * QS)
        zer = w.take(P)
        suf = w.take(NPG, 64)
        szx = w.take(NPG + 1, 64)
        hw = Carve(h[:, :, :].rearrange("p k t -> p (k t)"), KT * T)
        kpg = hw.take(KRING, D)
        ssp = hw.take(NPG + 1, 64)
        szl = hw.take(NPG + 1, 64)
        vpg = hw.take(VRING - 1, D)
        vlast = w.take(D)
        qblk = sb("qblk", [P, PAIRS, NB, 2 * QS])
        vn = sb("vn", [TS, D])
        qs_, _, vnT = [tb_[:, i * PAIRS * TS:(i + 1) * PAIRS * TS].rearrange("p (a b) -> p a b", a=PAIRS)
                         for i in range(3)]
        kn = sb("kn", [P, PAIRS, TS])
        k_hi = [wh[:, e, :] for e in range(2)]
        k_lo = [wl[:, e, :] for e in range(2)]
        q_hl = [ah[:, e, 0:TP] for e in range(2)]

        def kq_raw(e, which):
            return raw[:, which, :] if e == 0 else kq1[:, which, :]

        tbl = sb("tbl", [1, NB * NPG], I32)

        U_A = HEADS_A * 36
        U_F0 = U_A + FT * 30
        U_P0 = U_F0 + KT * 6
        U_KV = U_P0 + 16 * G
        U_Q = U_KV + KT * G
        U_O = U_Q + KT * G
        U_F1 = U_O + FT * 30
        U_P1 = U_F1 + KT * 6
        STORES = 3 * KT // 2
        G_MIX0, G_FFN0, G_PLE0, G_KV, G_MIX1, G_FFN1, G_PLE1, G_FIN = range(8)

        def cols(g):
            return slice(g * GW, (g + 1) * GW)

        def flat(ap):
            return ap.bitcast(F32)

        def vslot(s):
            return vpg[:, s, :] if s < VRING - 1 else vlast

        block = ctx.enter_context(nc.Block())

        @block.sync
        def _(sp):
            for g in range(G):
                sp.dma_start(h[:, :, cols(g)], xT.rearrange("(k p) t -> p k t", p=P)[:, :, cols(g)])\
                    .then_inc(s_xload[g], 16)
            n = Count()

            def load_slab(slot):
                i = n.up()
                wait(sp, w_ready, i - 2)
                src = wstream[bass.ds(i - 1, 1), :, :].rearrange("o p c -> (o p) c")
                sp.dma_start(raw[:, slot, :], src).then_inc(landed[slot], 16)

            load_slab(0)
            load_slab(1)
            with sp.Fori(0, BEFORE // 2 - 1) as i, looped(i, BEFORE // 2 - 1, n=(n, 2)):
                load_slab(0)
                load_slab(1)
            sp.wait_ge(rstd_done, 4 * G)
            sp.wait_ge(x_ready, 4 * G * KT)
            sp.wait_ge(xh_done, 4 * G * KT)
            sp.dma_start(h_scratch, h[:, :, :]).then_inc(h_away, 16)
            sp.dma_start(tbl[0:1, :], table).then_inc(tb_in, 16)
            sp.wait_ge(stg_out[0], 16 * STORES)
            sp.wait_ge(stg_out[1], 16 * STORES)
            for dst, src in ((qs_, qT_scratch), (kn[:, :, :], kT_out), (vnT, vT_out)):
                sp.dma_start(dst, src.rearrange("(j p) t -> p j t", p=P)[:, :, TP:T]).then_inc(q_in, 16)
            sp.wait_ge(h_away, 16)
            sp.wait_ge(tb_in, 16)

            def page(kind, m, p):
                ring, free, came, dst, src = ((KRING, kpg_free, pg_k, kpg, kT_cache) if kind == "k" else
                                              (VRING, vpg_free, pg_v, vpg, v_cache))
                phys = sp.value_load(tbl[0:1, bass.ds(m, 1)], min_val=0, max_val=POOLPG - 1)
                wait(sp, free, m - ring + 1)
                sp.dma_start(vslot(p % ring) if kind == "v" else dst[:, p % ring, :],
                             src[bass.ds(phys, 1), :, :].rearrange("o p c -> (o p) c")).then_inc(came[p % ring], 16)

            def load_head(j, e):
                wait(sp, kq_split, 2 * (j - 1) + e + 1 if not isinstance(j, int) or j > 0 else 0)
                for slot, src in ((0, kT_out), (1, qT_scratch)):
                    for half in range(2):
                        sp.dma_start(kq_raw(e, slot)[half * HD:(half + 1) * HD, :],
                                     src[bass.ds(j * P + e * HD, HD), 0:TP]).then_inc(kq_in[e], 16)

            def load_v(j):
                wait(sp, pe_v8, j)
                sp.dma_start(vc, vT_out[bass.ds(j * P, P), 0:TP]).then_inc(v_in, 16)

            sp.wait_ge(w_ready, BEFORE)
            load_head(0, 0)
            load_head(0, 1)
            for m in range(KRING):
                page("k", m, m)
            for j in turns(sp, PAIRS - 1, 1):
                load_v(j)
                for m in range(KRING, NPG):
                    page("k", j * NPG + m, m)
                for m in range(NPG):
                    page("v", j * NPG + m, m)
                load_head(j + 1, 0)
                load_head(j + 1, 1)
                for m in range(NPG, NPG + KRING):
                    page("k", j * NPG + m, m)
            j = PAIRS - 1
            load_v(j)
            for m in range(KRING, NPG):
                page("k", j * NPG + m, m)
            for m in range(NPG):
                page("v", j * NPG + m, m)
            sp.wait_ge(kq_split, HEADS_B)
            load_slab(0)
            load_slab(1)
            sp.wait_ge(sav, NB)
            for k in range(KT):
                sp.dma_start(h[:, k, :], h_scratch[:, k, :]).then_inc(h_back[k], 16)
            rest = (NSLAB - BEFORE) // 2 - 1
            with sp.Fori(0, rest) as i, looped(i, rest, n=(n, 2)):
                load_slab(0)
                load_slab(1)
            sp.wait_ge(y_done, KT)
            sp.dma_start(yT.rearrange("(k p) t -> p k t", p=P), h[:, :, :]).then_inc(y_out, 16)
            sp.wait_ge(y_out, 16)

        @block.gpsimd
        def _(pool):
            own = Count()

            def did(ins):
                ins.then_inc(s_const, 1)
                pool.wait_ge(s_const, own.up())

            did(nc.gpsimd.memset(ident[:, :], 0.0))
            did(nc.gpsimd.affine_select(out=ident[:, :], in_=ident[:, :], compare_op=ALU.not_equal, fill=1.0,
                                        base=0, pattern=[[-1, P]], channel_multiplier=1))
            did(nc.gpsimd.memset(ones[:, :], 1.0))
            did(nc.gpsimd.memset(c_eps[:, :], EPS))
            did(nc.gpsimd.memset(c_one[:, :], 1.0))
            did(nc.gpsimd.memset(c_epsv[:, :], 30.0))
            did(nc.gpsimd.memset(maskA[:, :, :], 1.0))
            for l, hf in enumerate(HALVES):
                nb = P // (2 * hf)
                m = maskA[:, l, :].rearrange("p (b r) -> p b r", b=nb)
                did(nc.gpsimd.affine_select(out=m, in_=m, compare_op=ALU.is_ge, fill=0.0, base=0,
                                            pattern=[[-2 * hf, nb], [0, 2 * hf]], channel_multiplier=1))
                did(nc.gpsimd.affine_select(out=m, in_=m, compare_op=ALU.is_ge, fill=0.0, base=hf - 1,
                                            pattern=[[2 * hf, nb], [0, 2 * hf]], channel_multiplier=-1))
                did(nc.gpsimd.memset(m[:, :, 0:hf], 0.0))
            m = maskA[:, NL, :].rearrange("p (b r) -> p b r", r=4)
            did(nc.gpsimd.affine_select(out=m, in_=m, compare_op=ALU.is_ge, fill=0.0, base=0,
                                        pattern=[[-4, P // 4], [0, 4]], channel_multiplier=1))
            did(nc.gpsimd.affine_select(out=m, in_=m, compare_op=ALU.is_ge, fill=0.0, base=0,
                                        pattern=[[4, P // 4], [1, 4]], channel_multiplier=-1))
            did(nc.gpsimd.memset(reset[:, :], 1.0))
            did(nc.gpsimd.memset(reset[:, 0:TP:P], 0.0))
            did(nc.gpsimd.memset(reset[:, TP:T:QS], 0.0))
            did(nc.gpsimd.memset(bmask, 1.0))
            did(nc.gpsimd.affine_select(out=bmask, in_=bmask, compare_op=ALU.is_ge, fill=0.0, base=0,
                                        pattern=[[-QS, NB]], channel_multiplier=1))
            did(nc.gpsimd.affine_select(out=bmask, in_=bmask, compare_op=ALU.is_ge, fill=0.0, base=QS - 1,
                                        pattern=[[QS, NB]], channel_multiplier=-1))
            n = Count()

            def split(slot):
                i = n.up()
                arrived = ((n.n - 1) // 2 + 1) * 16 + n.off * 8
                pool.wait_ge(landed[slot], arrived)
                wait(pool, w_used, i - 1 if not isinstance(i, int) or i > 2 else 0)
                pool.sem_inc(split_go, 1)
                nc.gpsimd.tensor_copy(wh[:, slot, :], raw[:, slot, :]).then_inc(split_hi, 1)
                pool.wait_ge(split_hi, i)
                nc.gpsimd.tensor_tensor(wl[:, slot, :], raw[:, slot, :], flat(wh[:, slot, :]), ALU.subtract)\
                    .then_inc(w_ready, 1)

            split(0)
            split(1)
            pairs = BEFORE // 2 - 1
            with pool.Fori(0, pairs) as i, looped(i, pairs, n=(n, 2)):
                split(0)
                split(1)
            pool.wait_ge(stg_out[0], 16 * STORES)
            pool.wait_ge(stg_out[1], 16 * STORES)
            did(nc.gpsimd.tensor_copy(ident_b[:, :], ident[:, :]))
            for m, val, fill, base in ((negm[:, :], 0.0, -BIG, -1), (triP, 1.0, 0.0, 0)):
                did(nc.gpsimd.memset(m, val))
                did(nc.gpsimd.affine_select(out=m, in_=m, compare_op=ALU.is_ge, fill=fill, base=base,
                                            pattern=[[-1, P]], channel_multiplier=1))
            for m, val, fill in ((mnew, 1.0, 0.0), (lnew, BIG, -BIG)):
                m3 = m.rearrange("p (b q) -> p b q", b=NB)
                did(nc.gpsimd.memset(m, val))
                did(nc.gpsimd.affine_select(out=m3, in_=m3, compare_op=ALU.is_ge, fill=fill, base=0,
                                            pattern=[[-QS, NB], [0, QS]], channel_multiplier=1))
                did(nc.gpsimd.affine_select(out=m3, in_=m3, compare_op=ALU.is_ge, fill=fill, base=-1,
                                            pattern=[[QS, NB], [1, QS]], channel_multiplier=-1))
            did(nc.gpsimd.memset(zer, 0.0))
            did(nc.gpsimd.memset(suf[:, NPG - 1, :], 0.0))
            did(nc.gpsimd.memset(qblk[:, :, :, :], 0.0))
            pool.sem_inc(maskd, 1)
            pool.wait_ge(pe_z, 16 * PAIRS)
            rest = (NSLAB - BEFORE) // 2
            with pool.Fori(0, rest) as i, looped(i, rest, n=(n, 2)):
                split(0)
                split(1)

        @block.scalar
        def _(act):
            own, sqs, nsums = Count(), Count(), Count()
            units = Count()

            def did(ins):
                ins.then_inc(aself, 1)
                act.wait_ge(aself, own.up())

            act.dma_start(gain[:, :, :], gains).then_inc(s_cload, 16)
            act.dma_start(gon[:, :], g_on).then_inc(s_cload, 16)
            act.dma_start(lbr[:, :, :], lbT).then_inc(s_cload, 16)
            act.dma_start(biasB[:, :], sb_bias.broadcast_to([P, HEADS_B])).then_inc(s_cload, 16)
            act.wait_ge(s_cload, 64)
            act.wait_ge(s_const, 5)
            act.wait_ge(dself, 1)
            did(nc.scalar.activation(omlb[:, :], lb[:, :], ACT.Sigmoid, scale=-1.0))
            did(nc.scalar.activation(lb[:, :], lb[:, :], ACT.Sigmoid))

            def norm(gi):
                for g in range(G):
                    if gi == G_MIX0:
                        act.wait_ge(s_xload[g], 16)
                    for k in range(KT if gi is not None else 0):
                        nc.scalar.activation(xh[:, k, cols(g)], h[:, k, cols(g)], ACT.Copy,
                                             scale=gain[:, gi, k:k + 1]).then_inc(xh_done, 1)
                    i = sqs.up()
                    wait(act, ssq_done, i - 1)
                    nc.scalar.activation(sq, h[:, :, cols(g)], ACT.Square).then_inc(sq_done, 1)
                for g in range(G):
                    act.wait_ge(nsum_done, nsums.up())
                    did(nc.scalar.activation(rstd[:, cols(g)], bank[4 + g][:, 0:GW], ACT.Ln,
                                             bias=c_eps[:, 0:1], scale=1.0 / D))
                    nc.scalar.activation(rstd[:, cols(g)], rstd[:, cols(g)], ACT.Exp, scale=-0.5)\
                        .then_inc(rstd_done, 1)

            norm(G_MIX0)

            forget, decays, exponents, kts, outs, osums, vts, states, heads, ons = [Count() for _ in range(10)]

            def group_exps(at, width, levels):
                for lo, hi in PARTS[:2] if levels else PARTS[1:2]:
                    act.wait_ge(d_done, exponents.up())
                    lo = lo if levels else XQ
                    nc.scalar.activation(X[:, lo:hi, 0:width], X[:, lo:hi, 0:width], ACT.Exp).then_inc(e_done, 1)
                act.wait_ge(d_done, exponents.up())
                nc.scalar.activation(X[:, XQD, 0:width], ga[:, at:at + width], ACT.Exp)
                nc.scalar.activation(X[:, XKD, 0:width], X[:, XKD, 0:width], ACT.Exp).then_inc(e_done, 1)

            def tile_copies(rows, at, fresh):
                i = kts.up()
                act.wait_ge(pe_kt, i)
                wait(act, pe_u, i - 1)
                nc.scalar.activation(kdt[0:rows, :], bank[5][0:rows, 0:P], ACT.Copy).then_inc(kd_tok, 1)
                act.wait_ge(pe_o, outs.up())
                if fresh:
                    wait(act, on_done, ons.up() - 1)
                nc.scalar.activation(o_s[:, at:at + rows], bank[7][:, at:at + rows], ACT.Copy).then_inc(o_copied, 1)

            def output_rms(width):
                act.wait_ge(pe_osum, osums.up())
                did(nc.scalar.activation(orst[:, 0:width], bank[7][:, GRP:GRP + width], ACT.Ln,
                                         bias=c_eps[:, 0:1], scale=1.0 / P))
                nc.scalar.activation(orst[:, 0:width], orst[:, 0:width], ACT.Exp, scale=-0.5).then_inc(orstd_done, 1)

            def v_copies():
                for c in range(TILES_A + 1):
                    rows = P if c < TILES_A else TS
                    act.wait_ge(pe_vt, vts.up())
                    nc.scalar.activation(vtok[0:rows, c, :], bank[5 + c % 2][0:rows, 0:P], ACT.Copy)\
                        .then_inc(v_tok_done, 1)

            def gate_act_og():
                act.wait_ge(unit_free, units.up(4 * G))
                nc.scalar.activation(og, og, ACT.Silu).then_inc(act_in, 1)

            def mix(head):
                wait(act, s_out, (heads.up() - 1) * 32)
                act.dma_start(S0, state[bass.ds(head, 1), :, :, :].rearrange("o p b v -> (o p) b v")).then_inc(s0_in, 16)
                nc.scalar.activation(qa, tq, ACT.Silu).then_inc(act_in, 1)
                nc.scalar.activation(tf, tf, ACT.Sigmoid).then_inc(act_in, 1)
                act.preload_act_table_set("natural_log_exp_and_others")
                act.wait_ge(fg_done, forget.up())
                nc.scalar.activation(tf, tf, ACT.Ln).then_inc(act_in, 1)
                act.wait_ge(g_done, decays.up())
                nc.scalar.activation(dec[:, 0:TILES_A], ga[:, P - 1:TP:P], ACT.Exp)
                nc.scalar.activation(dec[:, TILES_A:16], ga[:, TP + QS - 1:T:QS], ACT.Exp).then_inc(e_done, 1)
                group_exps(0, GRP, True)
                for g in range(TP // GRP):
                    tile_copies(P, 0, True)
                    tile_copies(P, P, False)
                    if g < TP // GRP - 1:
                        group_exps((g + 1) * GRP, GRP, True)
                    else:
                        group_exps(TP, TS, False)
                    output_rms(GRP)
                tile_copies(TS, 0, True)
                output_rms(TS)
                act.wait_ge(s_done, states.up(TILES_A + 2))
                act.dma_start(st_prompt[bass.ds(head, 1), :, :].rearrange("o p v -> (o p) v"), S).then_inc(s_out, 16)
                act.dma_start(st_sample[bass.ds(head, 1), :, :, :].rearrange("o p b v -> (o p) b v"), S0)\
                    .then_inc(s_out, 16)

            gate_act_og()
            v_copies()
            rounds = HEADS_A - 1
            for i in turns(
                    act, rounds, 1, own=(own, 5), fo=(forget, 1), de=(decays, 1), ex=(exponents, 14), kt=(kts, 9),
                    ou=(outs, 9), os=(osums, 5), vt=(vts, 9), st=(states, TILES_A + 2), he=(heads, 1), on=(ons, 5),
                    un=(units, 36)):
                mix(i)
                gate_act_og()
                v_copies()
                units.up(24)
            mix(rounds)
            units.up(24)

            gates, prods, ples = Count(), Count(), Count()

            def gate_groups(func):
                for g in range(G):
                    act.wait_ge(unit_free, units.up())
                    nc.scalar.activation(gate_s[:, cols(g)], gate_s[:, cols(g)], func).then_inc(gate_act, 1)

            def ffn(gi):
                act.wait_ge(unit_free, units.at())
                norm(gi)
                with act.Fori(0, FT // 2) as i, looped(i, FT // 2, un=(units, 60), pr=(prods, 6)):
                    for buf in range(2):
                        gate_groups(ACT.Silu)
                        for g in range(G):
                            act.wait_ge(a_prod, prods.up())
                            nc.scalar.activation(ah[:, buf, cols(g)], up_s[:, cols(g)], ACT.Copy).then_inc(a_hi, 1)
                        units.up(G)
                    units.up(2 * KT * G)

            def ple(gi, layer):
                act.wait_ge(unit_free, units.at())
                act.dma_start(praw, pT[bass.ds(layer, 1), :, :, :].rearrange("o p k t -> (o p) k t")).then_inc(p_in, 16)
                norm(gi)
                act.wait_ge(p_in, 16 * ples.up())
                nc.scalar.activation(ah[:, :, :], praw, ACT.Copy).then_inc(a_hi, 1)
                with act.Fori(0, KT) as i, looped(i, KT, un=(units, 6)):
                    gate_groups(ACT.Sigmoid)
                    units.up(G)

            def staged(dst):
                dst_t = dst.rearrange("(n p) t -> n p t", p=P)
                with act.Fori(0, KT // 2) as i, looped(i, KT // 2, un=(units, 2 * G)):
                    for s in range(2):
                        act.wait_ge(unit_free, units.up(G))
                        act.dma_start(dst_t[bass.ds(2 * i + s, 1), :, :].rearrange("o p t -> (o p) t"), stage[:, s, :])\
                            .then_inc(stg_out[s], 16)

            ffn(G_FFN0)
            ple(G_PLE0, 0)
            act.wait_ge(unit_free, units.at())
            norm(G_KV)
            staged(kT_out)
            staged(vT_out)
            act.wait_ge(unit_free, units.at())
            norm(G_MIX1)
            staged(qT_scratch)
            assert units.n == U_Q

            act.preload_act_table_set("natural_log_exp_and_others")
            mins, las, avs, seqs, ats = [Count() for _ in range(5)]
            act.wait_ge(maskd, 1)
            for half in range(2):
                act.wait_ge(pe_vn, half + 1)
                nc.scalar.activation(vn[0:TS, half * 512:(half + 1) * 512], bank[4 + half][0:TS, :], ACT.Copy)\
                    .then_inc(vn_done, 1)
            for j in turns(act, PAIRS, 1, own=(own, 16), mi=(mins, 16), la=(las, 16), av=(avs, 16), se=(seqs, 1),
                           at=(ats, 16)):
                seq = seqs.up()
                for e in range(2):
                    act.wait_ge(kq_in[e], 64 * seq)
                    if not isinstance(j, int) or j > 0:
                        act.wait_ge(pe_z, j * 16 - 1 + e)
                    nc.scalar.activation(q_hl[e], kq_raw(e, 1), ACT.Copy)
                    nc.scalar.activation(k_hi[e], kq_raw(e, 0), ACT.Copy).then_inc(kq_hi, 1)
                act.wait_ge(pe_v8, seq)
                nc.scalar.activation(v8, psum[:, 4:6, :].rearrange("p a (b c) -> p (a b) c", c=P), ACT.Copy)\
                    .then_inc(v8_done, 1)
                for it in range(STEPS):
                    if it < 16:
                        L = P * (it // 2 + 1)
                        lb_ = wt[:, it % 3, 0:L]
                        act.wait_ge(min_done, mins.up())
                        did(nc.scalar.activation(lb_, lb_, ACT.Exp))
                        nc.scalar.activation(lb_, lb_, ACT.Ln, bias=c_one[:, 0:1]).then_inc(sp_in, 1)
                    if it == SX_STEP + 1:
                        act.wait_ge(sx_done, seq)
                        nc.scalar.activation(szl[:, 0:NPG, :], szl[:, 0:NPG, :], ACT.Exp)
                        nc.scalar.activation(szl[0:TS, NPG, :], szl[0:TS, NPG, :], ACT.Exp).then_inc(sl_exp, 1)
                        act.wait_ge(sl_exp, seq)
                        nc.scalar.activation(szl[:, 0:NPG, :], szl[:, 0:NPG, :], ACT.Ln, bias=c_one[:, 0:1])
                        nc.scalar.activation(szl[0:TS, NPG, :], szl[0:TS, NPG, :], ACT.Ln, bias=c_one[0:TS, 0:1])\
                            .then_inc(sl_done, 1)
                    if it == SA_STEP:
                        act.wait_ge(sla, seq)
                        nc.scalar.activation(szl[:, 0:NPG, :], szl[:, 0:NPG, :], ACT.Exp)
                        nc.scalar.activation(szl[0:TS, NPG, :], szl[0:TS, NPG, :], ACT.Exp).then_inc(sexp, 1)
                    if 1 <= it < 17:
                        n = it - 1
                        a = wt[:, n % 3, 0:P * (n // 2 + 1)]
                        act.wait_ge(la_done, las.up())
                        nc.scalar.activation(a, a, ACT.Exp).then_inc(aexp, 1)
                    if 2 <= it < 18:
                        n = it - 2
                        L = min(P * (n // 2 + 1), 512)
                        i = ats.up()
                        act.wait_ge(pe_at, i)
                        wait(act, pe_av, i - 2)
                        nc.scalar.activation(aT[:, n % 2, 0:L], bank[4][:, 0:L], ACT.Copy).then_inc(at_act, 1)
                    if 3 <= it < 19:
                        n = it - 3
                        r = slice(n % 2 * HD, (n % 2 + 1) * HD)
                        act.wait_ge(pe_av, avs.up())
                        nc.scalar.activation(xh[r, bass.ds(j, 1), n // 2 * P:(n // 2 + 1) * P],
                                             bank[6][r, 0:P].rearrange("p (o t) -> p o t", o=1), ACT.Copy)\
                            .then_inc(o_hi, 1)

            units.up(KT * G)
            ffn(G_FFN1)
            ple(G_PLE1, 1)
            act.wait_ge(unit_free, units.at())
            assert units.n == U_P1
            norm(None)
            act.wait_ge(s_out, HEADS_A * 32)
            act.wait_ge(stg_out[0], 16 * STORES)
            act.wait_ge(stg_out[1], 16 * STORES)

        @block.vector
        def _(dve):
            own, units = Count(), Count()
            xhs, sqs, rst = Count(), Count(), Count()

            def did(ins):
                ins.then_inc(dself, 1)
                dve.wait_ge(dself, own.up())

            dve.wait_ge(s_cload, 64)
            did(nc.vector.tensor_tensor(lb[:, :], lbr[:, 0, :], lbr[:, 1, :], ALU.subtract))

            def evac(dst):
                for g in range(G):
                    dve.wait_ge(unit_done, units.up())
                    nc.vector.tensor_tensor(dst[:, cols(g)], bank[g][:, 0:GW], rstd[:, cols(g)], ALU.mult)\
                        .then_inc(unit_free, 1)

            def add_to_h(n):
                for g in range(G):
                    dve.wait_ge(unit_done, units.up())
                    nc.vector.tensor_tensor(h[:, n, cols(g)], h[:, n, cols(g)], bank[g][:, 0:GW], ALU.add)\
                        .then_inc(unit_free, 1)

            def norm(gi):
                wait(dve, unit_free, units.at())
                for g in range(G):
                    for k in range(KT if gi is not None else 0):
                        dve.wait_ge(xh_done, xhs.up())
                        nc.vector.scalar_tensor_tensor(xl[:, k, cols(g)], h[:, k, cols(g)], gain[:, gi, k:k + 1],
                                                       flat(xh[:, k, cols(g)]), ALU.mult, ALU.subtract)\
                            .then_inc(x_ready, 1)
                    dve.wait_ge(sq_done, sqs.up())
                    nc.vector.tensor_reduce(ssq[:, g, :], sq.rearrange("p k t -> p t k"), AX_X, ALU.add)\
                        .then_inc(ssq_done, 1)
                dve.wait_ge(rstd_done, rst.up(G))

            norm(G_MIX0)

            ins_, exps, levs, us, os_, oc, orst_, heads, vts, gs, fgs, ons = [Count() for _ in range(12)]

            def by_group(ap, at, width, *shape):
                v = ap[:, at:at + width]
                if len(shape) == 1:
                    return v.rearrange("p (b r) -> p b r", r=shape[0])
                return v.rearrange("p (b t r) -> p b t r", t=2, r=shape[1])

            def exponents(part, at, width, levels):
                for l in range(*PARTS[part]):
                    if l < NL and levels:
                        hf = HALVES[l]
                        gv = by_group(ga, at, width, 2, hf)
                        xv = by_group(X[:, l, :], 0, width, 2, hf)
                        nb = width // (2 * hf)
                        ref = gv[:, :, 0, hf - 1:hf].broadcast_to([P, nb, hf])
                        nc.vector.tensor_tensor(xv[:, :, 0, :], ref, gv[:, :, 0, :], ALU.subtract)
                        last = nc.vector.tensor_tensor(xv[:, :, 1, :], gv[:, :, 1, :], ref, ALU.subtract)
                    if l in (XQ, XK):
                        gv = by_group(ga, at, width, QS)
                        ref = gv[:, :, 1:2].broadcast_to([P, width // QS, QS])
                        a, b = (gv, ref) if l == XQ else (ref, gv)
                        last = nc.vector.tensor_tensor(by_group(X[:, l, :], 0, width, QS), a, b, ALU.subtract)
                    if l == XKD:
                        span = P if levels else QS
                        gv = by_group(ga, at, width, span)
                        ref = gv[:, :, span - 1:span].broadcast_to([P, width // span, span])
                        last = nc.vector.tensor_tensor(by_group(X[:, XKD, :], 0, width, span), ref, gv, ALU.subtract)
                last.then_inc(d_done, 1)

            def operands(at, width, levels):
                for part in range(0 if levels else 1, 3):
                    dve.wait_ge(e_done, exps.up())
                    for l in range(*PARTS[part]):
                        if l < NL and levels:
                            hf = HALVES[l]
                            xv = by_group(X[:, l, :], 0, width, 2, hf)
                            for t, src in ((0, ka), (1, qa)):
                                nc.vector.tensor_tensor(xv[:, :, t, :], xv[:, :, t, :],
                                                        by_group(src, at, width, 2, hf)[:, :, t, :], ALU.mult)
                        if l >= NL:
                            src = qa if l in (XQ, XQD) else ka
                            last = nc.vector.tensor_tensor(X[:, l, 0:width], X[:, l, 0:width], src[:, at:at + width],
                                                           ALU.mult)
                last.then_inc(xg_ready, 1)

            def scores(tile):
                for half, bk in ((0, 3), (1, 4)):
                    dve.wait_ge(pe_lev, levs.up())
                    nc.vector.tensor_tensor(prod[:, 3 * half:3 * half + 3, :],
                                            bank[bk][:, 0:3 * P].rearrange("p (l t) -> p l t", l=3),
                                            maskA[:, 3 * half:3 * half + 3, :], ALU.mult).then_inc(lev_free, 1)
                dve.wait_ge(lev_free, levs.at())
                wait(dve, pe_o, os_.at())
                nc.vector.tensor_reduce(att, prod.rearrange("p l t -> p t l"), AX_X, ALU.add).then_inc(att_done, 1)

            def new_state(tile):
                dve.wait_ge(pe_u, us.up())
                dve.wait_ge(pe_o, os_.up())
                dve.wait_ge(s_done, gs.at())
                nc.vector.scalar_tensor_tensor(S, S, dec[:, tile:tile + 1], bank[6][:, 0:P], ALU.mult, ALU.add)\
                    .then_inc(s_done, 1)
                gs.up()

            def squares(width, tiles):
                dve.wait_ge(o_copied, oc.up(tiles))
                dve.wait_ge(att_done, levatt.at())
                nc.vector.tensor_tensor(prod.rearrange("p l t -> p (l t)")[:, 0:width], o_s[:, 0:width],
                                        o_s[:, 0:width], ALU.mult).then_inc(osq_done, 1)

            def normed(at, width, head):
                dve.wait_ge(orstd_done, orst_.up())
                o = o_s[:, 0:width]
                did(nc.vector.tensor_tensor(o, o, orst[:, 0:width], ALU.mult))
                did(nc.vector.scalar_tensor_tensor(o, o, gon[:, bass.ds(head, 1)], og[:, at:at + width],
                                                   ALU.mult, ALU.mult))
                did(nc.vector.tensor_copy(ah[:, 0, at:at + width], o))
                nc.vector.tensor_tensor(al[:, 0, at:at + width], o, flat(ah[:, 0, at:at + width]), ALU.subtract)\
                    .then_inc(on_done, 1)
                ons.up()

            levatt = Count()

            def mix(head, ahead):
                wait(dve, s_out, (heads.up() - 1) * 32)
                nc.vector.memset(S, 0.0).then_inc(s_done, 1)
                gs.up()
                dve.wait_ge(act_in, ins_.up(3))
                did(nc.vector.tensor_scalar(tf, tf, omlb[:, bass.ds(head, 1)], lb[:, bass.ds(head, 1)],
                                            ALU.mult, ALU.add))
                did(nc.vector.tensor_scalar(tf, tf, LN_FLOOR, None, ALU.max))
                nc.vector.tensor_scalar(ka, tf, -1.0, 1.0, ALU.mult, ALU.add).then_inc(fg_done, 1)
                dve.wait_ge(act_in, ins_.up())
                nc.vector.tensor_tensor_scan(ga, reset[:, :], tf, 0.0, ALU.mult, ALU.add).then_inc(g_done, 1)
                dve.wait_ge(g_done, fgs.up())
                dve.wait_ge(pe_vt, vts.up(9))
                exps.up()
                for part in range(3):
                    exponents(part, 0, GRP, True)
                operands(0, GRP, True)
                if ahead:
                    evac(tq)
                for g in range(TP // GRP):
                    after = ((g + 1) * GRP, GRP, True) if g < TP // GRP - 1 else (TP, TS, False)
                    scores(2 * g)
                    levatt.up()
                    new_state(2 * g)
                    scores(2 * g + 1)
                    levatt.up()
                    for part in range(0 if after[2] else 1, 2):
                        exponents(part, *after)
                    new_state(2 * g + 1)
                    squares(GRP, 2)
                    exponents(2, *after)
                    operands(*after)
                    normed(g * GRP, GRP, head)
                    if g == 0 and ahead:
                        evac(tf)
                dve.wait_ge(pe_lev, levs.up())
                dve.wait_ge(pe_o, os_.at())
                nc.vector.tensor_tensor(att[0:TS, 0:TS], bank[4][0:TS, 0:TS], maskA[0:TS, NL, 0:TS], ALU.mult)\
                    .then_inc(lev_free, 1)
                dve.wait_ge(lev_free, levs.at())
                nc.vector.tensor_tensor(vb, vtok[0:TS, TILES_A:TILES_A + 1, :].broadcast_to([TS, NB, P]),
                                        bmask[0:TS, :].rearrange("p (b o) -> p b o", o=1).broadcast_to([TS, NB, P]),
                                        ALU.mult).then_inc(att_done, 1)
                levatt.up()
                dve.wait_ge(pe_u, us.up())
                dve.wait_ge(pe_o, os_.up())
                did(nc.vector.tensor_tensor(S0, S0, dec[:, TILES_A:16].rearrange("p (b o) -> p b o", o=1)
                                            .broadcast_to([P, NB, P]), ALU.mult))
                nc.vector.tensor_tensor(S0[:, 0:4, :], S0[:, 0:4, :], bank[3].rearrange("p (b v) -> p b v", b=4), ALU.add)
                nc.vector.tensor_tensor(S0[:, 4:8, :], S0[:, 4:8, :], bank[4].rearrange("p (b v) -> p b v", b=4), ALU.add)\
                    .then_inc(s_done, 1)
                gs.up()
                squares(TS, 1)
                normed(TP, TS, head)
                if ahead:
                    evac(tv)
                    dve.wait_ge(on_done, ons.at())
                    evac(og)
                for n in range(KT):
                    add_to_h(n)
            for dst in (tq, tf, tv, og):
                evac(dst)
            rounds = HEADS_A - 1
            for i in turns(
                    dve, rounds, 1, own=(own, 18), un=(units, 36), ins=(ins_, 4), ex=(exps, 15), le=(levs, 17), us=(us, 9),
                    os=(os_, 9), oc=(oc, 9), ors=(orst_, 5), he=(heads, 1), vt=(vts, 9), gs=(gs, 10), fg=(fgs, 1),
                    on=(ons, 5), la=(levatt, 9)):
                mix(i, True)
            mix(rounds, False)
            assert units.n == U_A

            gates, his = Count(), Count()

            def ffn(gi):
                norm(gi)
                with dve.Fori(0, FT // 2) as i, looped(i, FT // 2, un=(units, 60), ga=(gates, 6), hi=(his, 6)):
                    for buf in range(2):
                        evac(gate_s)
                        evac(up_s)
                        dve.wait_ge(unit_free, units.at())
                        for g in range(G):
                            dve.wait_ge(gate_act, gates.up())
                            nc.vector.tensor_tensor(up_s[:, cols(g)], up_s[:, cols(g)], gate_s[:, cols(g)], ALU.mult)\
                                .then_inc(a_prod, 1)
                        for g in range(G):
                            dve.wait_ge(a_hi, his.up())
                            nc.vector.tensor_tensor(al[:, buf, cols(g)], up_s[:, cols(g)], flat(ah[:, buf, cols(g)]),
                                                    ALU.subtract).then_inc(a_ready, 1)
                    for buf in range(2):
                        for n in range(KT):
                            add_to_h(n)

            def ple(gi):
                norm(gi)
                dve.wait_ge(a_hi, his.up())
                nc.vector.tensor_tensor(al[:, :, :], praw, flat(ah[:, :, :]), ALU.subtract).then_inc(a_ready, 1)
                with dve.Fori(0, KT) as n, looped(n, KT, un=(units, 6), ga=(gates, 3), own=(own, 3)):
                    evac(gate_s)
                    for g in range(G):
                        dve.wait_ge(gate_act, gates.up())
                        dve.wait_ge(unit_done, units.up())
                        did(nc.vector.tensor_tensor(gate_s[:, cols(g)], gate_s[:, cols(g)], bank[g][:, 0:GW], ALU.mult))
                        hv = h[:, bass.ds(n, 1), cols(g)].rearrange("p o t -> p (o t)")
                        nc.vector.tensor_tensor(hv, hv, gate_s[:, cols(g)], ALU.add).then_inc(unit_free, 1)

            tiles = Count()

            def stage_tiles(scale):
                for i in turns(dve, KT // 2, 1, un=(units, 2 * G), ti=(tiles, 2)):
                    for s in range(2):
                        t = tiles.up()
                        for g in range(G):
                            dve.wait_ge(unit_done, units.up())
                            if g == 0:
                                wait(dve, stg_out[s], ((tiles.n - 1) // 2) * 16 + tiles.off * 8)
                            nc.vector.scalar_tensor_tensor(stage[:, s, cols(g)], bank[g][:, 0:GW], scale,
                                                           rstd[:, cols(g)], ALU.mult, ALU.mult).then_inc(unit_free, 1)

            ffn(G_FFN0)
            ple(G_PLE0)
            norm(G_KV)
            stage_tiles(1.0)
            stage_tiles(1.0)
            norm(G_MIX1)
            stage_tiles(HD ** -0.5)
            assert units.n == U_Q

            zs, sps, seqs, sufs, ats, outs = [Count() for _ in range(6)]
            new = slice(0, TS)
            dve.wait_ge(maskd, 1)
            dve.wait_ge(q_in, 48)
            for hh in range(2):
                r = slice(hh * HD, (hh + 1) * HD)
                nc.vector.tensor_copy(qblk[r, :, :, hh * QS:(hh + 1) * QS],
                                      qs_[r, :, :].rearrange("p j (b q) -> p j b q", b=NB))
            nc.vector.tensor_copy(bcol.rearrange("p (h q) -> p h q", q=QS),
                                  biasB[:, :].rearrange("p (h o) -> p h o", o=1).broadcast_to([P, HEADS_B, QS]))\
                .then_inc(qblk_done, 1)
            dve.wait_ge(qblk_done, 1)
            dve.wait_ge(pe_vn, 2)

            def scores_of(n):
                L = P * (n // 2 + 1)
                return psum[:, 2 * (n % 2):2 * (n % 2) + 2, :].rearrange("p a b -> p (a b)")[:, 0:L]

            for j in turns(dve, PAIRS, 1, own=(own, 32 + SOWN), zs=(zs, 16), sp=(sps, 16), se=(seqs, 1),
                           su=(sufs, NPG), at=(ats, 16), ou=(outs, 16)):
                seq = seqs.up()
                for e in range(2):
                    dve.wait_ge(kq_hi, 2 * seq - 1 + e)
                    low = slice(HD, P)
                    nc.vector.tensor_tensor(q_hl[e][low, :], kq_raw(e, 1)[low, :], flat(q_hl[e][low, :]), ALU.subtract)
                    nc.vector.tensor_tensor(k_lo[e], kq_raw(e, 0), flat(k_hi[e]), ALU.subtract).then_inc(kq_split, 1)
                for it in range(STEPS):
                    if 4 <= it < 20:
                        n = it - 4
                        r = slice(n % 2 * HD, (n % 2 + 1) * HD)
                        dve.wait_ge(o_hi, outs.up())
                        at = (r, bass.ds(j, 1), slice(n // 2 * P, (n // 2 + 1) * P))
                        nc.vector.tensor_tensor(xl[at], bank[6][r, 0:P].rearrange("p (o t) -> p o t", o=1),
                                                flat(xh[at]), ALU.subtract).then_inc(o_lo, 1)
                    if it == SL_STEP:
                        dve.wait_ge(stail, seq)
                        lm = lnew[new, bass.ds(j * QS, QS)].rearrange("p (o q) -> p o q", o=1)\
                            .broadcast_to([TS, HEADS_B, QS])
                        nc.vector.tensor_tensor(szl[:, 0:NPG, :], szx[:, 0:NPG, :],
                                                bank[7].rearrange("p (g c) -> p g c", g=NPG), ALU.subtract)
                        did(nc.vector.tensor_tensor(szl[new, NPG, :], szx[new, NPG, :], bank[3][new, 0:64],
                                                    ALU.subtract))
                        an = szl[new, NPG, :].rearrange("p (h q) -> p h q", q=QS)
                        nc.vector.tensor_tensor(an, an, lm, ALU.min).then_inc(sla, 1)
                    if it < 16:
                        i = zs.up()
                        dve.wait_ge(pe_z, i)
                        wait(dve, pe_at, i - 3)
                        nc.vector.tensor_scalar(wt[:, it % 3, 0:P * (it // 2 + 1)], scores_of(it),
                                                biasB[:, bass.ds(2 * j + it % 2, 1)], 30.0,
                                                ALU.add, ALU.min).then_inc(min_done, 1)
                    if 1 <= it < 17:
                        n = it - 1
                        L = P * (n // 2 + 1)
                        z, item = scores_of(n), wt[:, n % 3, 0:L]
                        bias = biasB[:, bass.ds(2 * j + n % 2, 1)]
                        dve.wait_ge(sp_in, sps.up())
                        did(nc.vector.scalar_tensor_tensor(item, z, bias, item, ALU.add, ALU.max))
                        did(nc.vector.tensor_tensor_scan(tb_[:, 0:L][:, ::-1], item[:, ::-1], item[:, ::-1], 0.0,
                                                         ALU.add, ALU.bypass))
                        nc.vector.scalar_tensor_tensor(item, z, bias, tb_[:, 0:L], ALU.add, ALU.subtract)\
                            .then_inc(la_done, 1)
                    if 2 <= it < 18:
                        n = it - 2
                        i = ats.up()
                        if n >= 8:
                            L = P * (n // 2 + 1)
                            dve.wait_ge(pe_at, i)
                            dve.wait_ge(pe_av, i - 2)
                            nc.vector.tensor_copy(aT[:, n % 2, 512:L], bank[5][:, 0:L - 512]).then_inc(at_dve, 1)
                    if it == SX_STEP:
                        dve.wait_ge(sz_done, seq)
                        nc.vector.tensor_tensor(szx[:, 0:NPG, :], bank[7].rearrange("p (g c) -> p g c", g=NPG),
                                                bcol.rearrange("p (o c) -> p o c", o=1).broadcast_to([P, NPG, 64]),
                                                ALU.add)
                        did(nc.vector.tensor_tensor(szx[new, NPG, :], bank[1][new, 0:64], bcol[new, :], ALU.add))
                        nc.vector.tensor_scalar(szl[:, 0:NPG, :], szx[:, 0:NPG, :], 30.0, None, ALU.min)
                        nc.vector.tensor_scalar(szl[new, NPG, :], szx[new, NPG, :], 30.0, None, ALU.min)\
                            .then_inc(sx_done, 1)
                    if it == SX_STEP + 2:
                        dve.wait_ge(sl_done, seq)
                        nc.vector.tensor_tensor(ssp[:, 0:NPG, :], szx[:, 0:NPG, :], szl[:, 0:NPG, :], ALU.max)
                        did(nc.vector.tensor_tensor(ssp[new, NPG, :], szx[new, NPG, :], szl[new, NPG, :], ALU.max))
                        mb = mnew[new, bass.ds(j * QS, QS)].rearrange("p (o q) -> p o q", o=1)\
                            .broadcast_to([TS, HEADS_B, QS])
                        sn = ssp[new, NPG, :].rearrange("p (h q) -> p h q", q=QS)
                        nc.vector.tensor_tensor(sn, sn, mb, ALU.mult).then_inc(suf_step, 1)
                        sufs.up()
                        for pg in range(NPG - 2, -1, -1):
                            dve.wait_ge(suf_step, sufs.at())
                            nc.vector.tensor_tensor(suf[:, pg, :], suf[:, pg + 1, :], ssp[:, pg + 1, :], ALU.add)\
                                .then_inc(suf_step, 1)
                            sufs.up()
                    if it == STEPS - 1:
                        dve.wait_ge(sav, seq)
                        ov = bank[7][:, 0:64].rearrange("p (j e q) -> p j e q", e=2, q=QS)
                        for hh in range(2):
                            r = slice(hh * HD, (hh + 1) * HD)
                            did(nc.vector.tensor_copy(xh[r, :, bass.ds(j * QS + TP, QS)], ov[r, :, hh, :]))
                        for hh in range(2):
                            r = slice(hh * HD, (hh + 1) * HD)
                            last = nc.vector.tensor_tensor(xl[r, :, bass.ds(j * QS + TP, QS)], ov[r, :, hh, :],
                                                           flat(xh[r, :, bass.ds(j * QS + TP, QS)]), ALU.subtract)
                        last.then_inc(so_done, 1)
            for n in range(KT):
                dve.wait_ge(h_back[n], 16)
                add_to_h(n)
            ffn(G_FFN1)
            ple(G_PLE1)
            norm(None)
            for k in range(KT):
                nc.vector.scalar_tensor_tensor(h[:, k, :], h[:, k, :], gain[:, G_FIN, k:k + 1], rstd[:, :],
                                               ALU.mult, ALU.mult).then_inc(y_done, 1)

        @block.tensor
        def _(pe):
            slabs, units, xs, norms = Count(), Count(), Count(), Count()
            mm = nc.tensor.matmul

            def slab():
                pe.wait_ge(w_ready, slabs.up())
                fresh[0] = True
                return (slabs.n - 1) % 2

            fresh = [False]

            def unit_start():
                wait(pe, unit_free, units.up() - G)

            def exact(out, slot, tile, mh, ml, first, last):
                ws = slice(tile * P, (tile + 1) * P)
                ins = mm(out, wh[:, slot, ws], mh, start=first, stop=False)
                if fresh[0]:
                    ins.then_inc(w_used, 1)
                    fresh[0] = False
                mm(out, wh[:, slot, ws], ml, start=False, stop=False)
                return mm(out, wl[:, slot, ws], mh, start=False, stop=last)

            def product_x():
                slot = slab()
                for g in range(G):
                    unit_start()
                    if renewed[0]:
                        pe.wait_ge(x_ready, xs.up(KT))
                    for k in range(KT):
                        last = exact(bank[g][:, 0:GW], slot, k, xh[:, k, cols(g)], xl[:, k, cols(g)], k == 0, k == KT - 1)
                    last.then_inc(unit_done, 1)
                if renewed[0]:
                    renewed[0] = False
                    square_sums()

            def product_a(slot, tile, buf):
                for g in range(G):
                    unit_start()
                    exact(bank[g][:, 0:GW], slot, tile, ah[:, buf, cols(g)], al[:, buf, cols(g)], True, True)\
                        .then_inc(unit_done, 1)

            renewed = [False]

            def square_sums():
                for g in range(G):
                    pe.wait_ge(ssq_done, norms.up())
                    mm(bank[4 + g][:, 0:GW], ones[:, :], ssq[:, g, :], start=True, stop=True).then_inc(nsum_done, 1)

            def norm():
                renewed[0] = True

            pe.wait_ge(s_const, 5)
            norm()

            groups, levs, kts, us, outs, heads, sds, ons, vts, atts, osqs, vtk = [Count() for _ in range(12)]

            def level_scores(c):
                ts = slice(c % 2 * P, c % 2 * P + P)
                for half, bk in ((0, 3), (1, 4)):
                    wait(pe, lev_free, levs.up() - 2)
                    for l in range(3 * half, 3 * half + 3):
                        lhs, rhs = (X[:, l, ts], X[:, l, ts]) if l < NL else (X[:, XK, ts], X[:, XQ, ts])
                        last = mm(bank[bk][:, (l % 3) * P:(l % 3 + 1) * P], lhs, rhs, start=True, stop=True)
                    last.then_inc(pe_lev, 1)

            def keys_transposed(c, rows):
                at = c % 2 * P
                i = kts.up()
                wait(pe, kd_tok, i - 1)
                nc.tensor.transpose(bank[5][0:rows, 0:P], X[:, XKD, at:at + rows], ident[:, :]).then_inc(pe_kt, 1)

            def tile_output(c):
                at = c % 2 * P
                pe.wait_ge(kd_tok, us.up())
                pe.wait_ge(s_done, sds.up())
                mm(bank[6][:, 0:P], kdt[:, :], vtok[:, c, :], start=True, stop=True).then_inc(pe_u, 1)
                pe.wait_ge(att_done, atts.up())
                wait(pe, o_copied, outs.up() - 1)
                wait(pe, orstd_done, osqs.at())
                o = bank[7][:, at:at + P]
                mm(o, S, X[:, XQD, at:at + P], start=True, stop=False)
                mm(o, vtok[:, c, :], att[:, :], start=False, stop=True).then_inc(pe_o, 1)

            def output_sums(width):
                pe.wait_ge(osq_done, osqs.up())
                wait(pe, orstd_done, osqs.at() - 1)
                mm(bank[7][:, GRP:GRP + width], ones[:, :], prod.rearrange("p l t -> p (l t)")[:, 0:width],
                   start=True, stop=True).then_inc(pe_osum, 1)

            def v_transposed():
                pe.wait_ge(unit_free, units.at())
                for c in range(TILES_A + 1):
                    rows = P if c < TILES_A else TS
                    wait(pe, v_tok_done, vtk.up() - 2)
                    nc.tensor.transpose(bank[5 + c % 2][0:rows, 0:P], tv[:, c * P:c * P + rows], ident[:, :])\
                        .then_inc(pe_vt, 1)

            def mix(ahead):
                if ahead:
                    product_x()
                pe.wait_ge(v_tok_done, vts.up(9))
                for g in range(TP // GRP):
                    pe.wait_ge(xg_ready, groups.up())
                    c = 2 * g
                    level_scores(c)
                    keys_transposed(c, P)
                    level_scores(c + 1)
                    tile_output(c)
                    keys_transposed(c + 1, P)
                    tile_output(c + 1)
                    output_sums(GRP)
                    if g == 0 and ahead:
                        product_x()
                pe.wait_ge(xg_ready, groups.up())
                sds.up(2)
                pe.wait_ge(s_done, sds.at() - 1)
                pe.wait_ge(lev_free, levs.up() - 1)
                mm(bank[4][0:TS, 0:TS], X[:, XK, 0:TS], X[:, XQ, 0:TS], start=True, stop=True).then_inc(pe_lev, 1)
                keys_transposed(0, TS)
                pe.wait_ge(att_done, atts.up())
                wait(pe, o_copied, outs.up() - 1)
                pe.wait_ge(orstd_done, osqs.at())
                pe.wait_ge(s0_in, heads.up() * 16)
                pe.wait_ge(kd_tok, us.up())
                o = bank[7]
                mm(o[:, 0:TS], vtok[0:TS, TILES_A, :], att[0:TS, 0:TS], start=True, stop=False)
                for b in range(NB):
                    last = mm(o[:, QS * b:QS * b + QS], S0[:, b, :], X[:, XQD, QS * b:QS * b + QS], start=False,
                              stop=(b == NB - 1))
                last.then_inc(pe_o, 1)
                mm(bank[3][:, :], kdt[0:TS, :], vb[:, 0:4, :], start=True, stop=True)
                mm(bank[4][:, :], kdt[0:TS, :], vb[:, 4:8, :], start=True, stop=True).then_inc(pe_u, 1)
                output_sums(TS)
                if ahead:
                    product_x()
                    product_x()
                    v_transposed()
                pe.wait_ge(on_done, ons.up(5))
                for half in range(2):
                    slot = slab()
                    for n in range(4):
                        product_a(slot, n, 0)

            for _ in range(4):
                product_x()
            v_transposed()
            rounds = HEADS_A - 1
            for i in turns(
                    pe, rounds, 1, sl=(slabs, 6), un=(units, 36), gr=(groups, 5), le=(levs, 17), kt=(kts, 9), us=(us, 9),
                    ou=(outs, 9), he=(heads, 1), sd=(sds, 10), on=(ons, 5), vt=(vts, 9), at=(atts, 9), os=(osqs, 5),
                    vk=(vtk, 9)):
                mix(True)
            mix(False)

            ars = Count()

            def ffn():
                norm()
                for i in turns(pe, FT // 2, 1, sl=(slabs, 6), un=(units, 60), ar=(ars, 6)):
                    for _ in range(4):
                        product_x()
                    for buf in range(2):
                        slot = slab()
                        pe.wait_ge(a_ready, ars.up(3))
                        for n in range(KT):
                            product_a(slot, n, buf)

            def ple():
                norm()
                parts = ars.up()
                for i in turns(pe, KT, 1, sl=(slabs, 2), un=(units, 6)):
                    product_x()
                    if isinstance(i, int):
                        pe.wait_ge(a_ready, parts)
                    slot = slab()
                    for g in range(G):
                        unit_start()
                        for k in range(PK):
                            last = exact(bank[g][:, 0:GW], slot, k, ah[:, k, cols(g)], al[:, k, cols(g)], k == 0,
                                         k == PK - 1)
                        last.then_inc(unit_done, 1)

            def products(n):
                for i in turns(pe, n // 2, 1, sl=(slabs, 2), un=(units, 6)):
                    product_x()
                    product_x()

            ffn()
            ple()
            norm()
            products(16)
            norm()
            products(KT)
            assert units.n == U_Q and slabs.n == BEFORE

            pairs, zs, ats, avs, vpgs = [Count() for _ in range(5)]
            tr = nc.tensor.transpose
            pe.wait_ge(unit_free, units.at())
            pe.wait_ge(q_in, 48)
            for j in range(PAIRS):
                last = tr(bank[4 + j // 4][0:TS, j % 4 * P:(j % 4 + 1) * P], vnT[:, j, :], ident[:, :])
                if j % 4 == 3:
                    last.then_inc(pe_vn, 1)
            pe.wait_ge(vn_done, 2)
            pe.wait_ge(qblk_done, 1)
            pe.wait_ge(maskd, 1)
            for b in turns(pe, PAIRS, 1, pa=(pairs, 1), zs=(zs, 16), at=(ats, 16), av=(avs, 16), vp=(vpgs, 8)):
                seq = pairs.up()

                def sample_scores(pages):
                    for pg in pages:
                        pe.wait_ge(pg_k[pg % KRING], (pg // KRING + 1) * 16 + b * (NPG // KRING * 16))
                        for jj in range(PAIRS):
                            at = pg * 64 + jj * 8
                            last = mm(bank[7][:, at:at + 8], kpg[:, pg % KRING, jj * P:(jj + 1) * P],
                                      qblk[:, jj, bass.ds(b, 1), :].rearrange("p o c -> p (o c)"), start=True, stop=True)
                        last.then_inc(kpg_free, 1)

                pe.wait_ge(v_in, seq * 16)
                for c in range(KT):
                    last = tr(bank[4 + c // 4][:, c % 4 * P:(c % 4 + 1) * P], vc[:, c * P:(c + 1) * P], ident[:, :])
                last.then_inc(pe_v8, 1)
                for it in range(STEPS):
                    if it < 16:
                        qt, hh = it // 2, it % 2
                        before = P * qt
                        qq = q_hl[hh][:, before:before + P]
                        if it < 2:
                            pe.wait_ge(kq_split, 2 * b + it + 1)
                        wait(pe, la_done, zs.up() - 2)
                        if it == SL_STEP:
                            pe.wait_ge(sla, seq)

                        def score(out, keys, last):
                            mm(out, qq, k_hi[hh][:, keys], start=True, stop=False)
                            mm(out, qq, k_lo[hh][:, keys], start=False, stop=last)

                        for half in range(-(-before // 512)):
                            n = min(512, before - 512 * half)
                            score(bank[2 * hh + half][:, 0:n], slice(512 * half, 512 * half + n), True)
                        out = bank[2 * hh + before // 512][:, before % 512:before % 512 + P]
                        score(out, slice(before, before + P), False)
                        mm(out, ident_b[:, :], negm[:, :], start=False, stop=True).then_inc(pe_z, 1)
                    if 2 <= it < 18:
                        n = it - 2
                        i = ats.up()
                        pe.wait_ge(aexp, i)
                        if n == 0:
                            pe.wait_ge(v8_done, seq)
                        wait(pe, at_act, i - 1)
                        if n >= 9:
                            pe.wait_ge(at_dve, n - 8 + b * 8)
                        for c in range(n // 2 + 1):
                            last = tr(bank[4 + c // 4][:, c % 4 * P:(c % 4 + 1) * P],
                                      wt[:, n % 3, c * P:(c + 1) * P], ident[:, :])
                        last.then_inc(pe_at, 1)
                    if 3 <= it < 19:
                        n = it - 3
                        hh = n % 2
                        i = avs.up()
                        pe.wait_ge(at_act, i)
                        if n >= 8:
                            pe.wait_ge(at_dve, n - 7 + b * 8)
                        wait(pe, o_lo, i - 2)
                        for c in range(n // 2 + 1):
                            last = mm(bank[6][hh * HD:(hh + 1) * HD, 0:P], v8[:, c, hh * HD:(hh + 1) * HD],
                                      aT[:, hh, c * P:(c + 1) * P], start=(c == 0), stop=(c == n // 2))
                        last.then_inc(pe_av, 1)
                    if it in PAGE_STEPS:
                        if it == 0:
                            wait(pe, so_done, seq - 1)
                        sample_scores(PAGE_STEPS[it])
                    if it == SX_STEP - 1:
                        for jj in range(PAIRS):
                            last = mm(bank[1][0:TS, jj * 8:jj * 8 + 8], kn[:, jj, :],
                                      qblk[:, jj, bass.ds(b, 1), :].rearrange("p o c -> p (o c)"), start=True, stop=True)
                        last.then_inc(sz_done, 1)
                    if it == SL_STEP - 1:
                        pe.wait_ge(suf_step, (b + 1) * NPG)
                        tail = bank[7].rearrange("p (g c) -> p g c", g=NPG)
                        mm(tail, triP, ssp[:, 0:NPG, :], start=True, stop=False)
                        mm(tail, ones[:, :], suf, start=False, stop=False)
                        mm(tail, ones[0:TS, :], ssp[0:TS, NPG:NPG + 1, :].broadcast_to([TS, NPG, 64]),
                           start=False, stop=True)
                        mm(bank[3][0:TS, 0:64], triP[0:TS, 0:TS], ssp[0:TS, NPG, :], start=True, stop=True)\
                            .then_inc(stail, 1)
                    if SA_STEP < it <= SA_STEP + NPG:
                        pg = it - SA_STEP - 1
                        if pg == 0:
                            pe.wait_ge(sexp, seq)
                            mm(bank[7][:, 0:64], zer, szl[:, 0, :], start=True, stop=False)
                        pe.wait_ge(pg_v[pg % VRING], (pg // VRING + 1) * 16 + b * (NPG // VRING * 16))
                        for jj in range(PAIRS):
                            last = mm(bank[7][:, jj * 8:jj * 8 + 8], vslot(pg % VRING)[:, jj * P:(jj + 1) * P],
                                      szl[:, pg, jj * 8:jj * 8 + 8], start=False, stop=False)
                        last.then_inc(vpg_free, 1)
                        vpgs.up()
                        if pg == NPG - 1:
                            for jj in range(PAIRS):
                                last = mm(bank[7][:, jj * 8:jj * 8 + 8], vn[0:TS, jj * P:(jj + 1) * P],
                                          szl[0:TS, NPG, jj * 8:jj * 8 + 8], start=False, stop=(jj == PAIRS - 1))
                            last.then_inc(sav, 1)
            pe.wait_ge(o_lo, 16 * PAIRS)
            pe.wait_ge(so_done, NB)
            products(N_O)
            ffn()
            ple()
            square_sums()


def kernel(x_prompt, x_sample, p_prompt, p_sample, state_hgrn, cache_k, cache_v, page_table, a_lb, w_a_in,
           g_a_onorm, w_a_o, g_kv, w_kv, w_b_q, w_b_o, sb_bias, g_mix, g_ffn, w_ffn_in, w_ffn_out, g_ple,
           w_ple_in, w_ple_gate, g_final):
    import numpy as _np
    import concourse.bacc as _bacc
    from concourse import mybir as _mybir
    from concourse.bass_utils import run_bass_kernel_spmd as _run

    f32 = _np.float32
    A = lambda a: _np.asarray(a)

    def tall(wt, col):
        return A(wt)[:, col * P:(col + 1) * P].reshape(-1, P, P).transpose(1, 0, 2)

    def wide(wt, row, c0, c1):
        return A(wt)[row * P:(row + 1) * P, c0:c1].reshape(P, -1, P)

    stream = _np.zeros((NSLAB, P, 8, P), f32)
    at = [0]

    def put(s):
        stream[at[0], :, :s.shape[1], :] = s
        at[0] += 1

    wa, wo = A(w_a_in)[0], A(w_a_o)[0]

    def ffn(l):
        wi, wu = A(w_ffn_in)[l], A(w_ffn_out)[l]
        for c in range(0, FT, 2):
            for t in (c, c + 1):
                put(tall(wi, t))
                put(tall(wi, FT + t))
            for t in (c, c + 1):
                put(wide(wu, t, 0, D))

    def ple(l):
        for n in range(KT):
            put(tall(A(w_ple_gate)[l], n))
            put(tall(A(w_ple_in)[l], n))

    for part in range(4):
        put(tall(wa, part * KT))
    for hd in range(HEADS_A):
        if hd + 1 < HEADS_A:
            for part in range(4):
                put(tall(wa, part * KT + hd + 1))
        put(wide(wo, hd, 0, 512))
        put(wide(wo, hd, 512, 1024))
    ffn(0)
    ple(0)
    for n in range(16):
        put(tall(w_kv, n))
    for n in range(KT):
        put(tall(A(w_b_q)[0], n))
    for n in range(KT):
        put(tall(A(w_b_o)[0], n))
    ffn(1)
    ple(1)
    assert at[0] == NSLAB

    def tokens_T(prompt, sample):
        return _np.concatenate([A(prompt).reshape(TP, -1), A(sample).reshape(TS, -1)]).T

    xT = _np.ascontiguousarray(tokens_T(x_prompt, x_sample))
    pT = _np.stack([tokens_T(A(p_prompt)[l], A(p_sample)[l]).reshape(PK, P, T).transpose(1, 0, 2) for l in range(2)])
    cols_ = lambda v: A(v).reshape(KT, P).T
    gm, gf, gp = A(g_mix), A(g_ffn), A(g_ple)
    gains = _np.stack([cols_(v) for v in (gm[0], gf[0], gp[0], g_kv, gm[1], gf[1], gp[1], g_final)], axis=1)
    ins = {
        "wstream": stream.reshape(NSLAB, P, SLAB),
        "xT": xT,
        "pT": pT,
        "state": A(state_hgrn)[0].transpose(1, 2, 0, 3),
        "kT_cache": A(cache_k).reshape(POOLPG, P, PAIRS, P).transpose(0, 3, 2, 1).reshape(POOLPG, P, D),
        "v_cache": A(cache_v).reshape(POOLPG, P, D),
        "table": A(page_table).reshape(1, NB * NPG),
        "lbT": A(a_lb).reshape(2, KT, P).transpose(2, 0, 1),
        "gains": gains,
        "g_on": A(g_a_onorm).reshape(HEADS_A, P).T,
        "sb_bias": A(sb_bias).reshape(1, HEADS_B),
    }
    outs = {
        "yT": (D, T), "st_prompt": (HEADS_A, P, P), "st_sample": (HEADS_A, P, NB, P), "kT_out": (D, T), "vT_out": (D, T),
    }
    nc = _bacc.Bacc("TRN2", target_bir_lowering=False, num_devices=1)
    arrays, args = {}, {}
    for name, a in ins.items():
        a = _np.ascontiguousarray(a)
        arrays[f"in_{name}"] = a
        args[name] = nc.dram_tensor(f"in_{name}", a.shape, _mybir.dt.from_np(a.dtype), kind="ExternalInput").ap()
    for name, shape in outs.items():
        args[name] = nc.dram_tensor(f"out_{name}", shape, _mybir.dt.float32, kind="ExternalOutput").ap()
    yoco_step(nc, **args)
    r = _run(nc, [arrays], core_ids=[0]).results[0]
    y, kk, vv = (_np.asarray(r[f"out_{n}"]).T for n in ("yT", "kT_out", "vT_out"))
    stp, sts = _np.asarray(r["out_st_prompt"]), _np.asarray(r["out_st_sample"])

    def split(a, *tail):
        return (_np.ascontiguousarray(a[:TP]).reshape(1, TP, *tail), _np.ascontiguousarray(a[TP:]).reshape(NB, QS, *tail))

    yp, ys = split(y, D)
    kp, ks = split(kk, HEADS_B, HD)
    vp, vs = split(vv, HEADS_B, HD)
    return (yp, ys, stp.reshape(1, 1, HEADS_A, P, P), _np.ascontiguousarray(sts.transpose(2, 0, 1, 3))[None],
            kp, vp, ks, vs)
```
